# Optimizing a Trainium2 kernel written in Bass

```python
import jax, jax.numpy as jnp
from jax import lax
import numpy as np

D_MODEL = 1024
BATCH = 1
SEQ = 256
DEPTH = 2

CTX_LEN = 256
GRID_W = 64
ROPE_BASE = 10000.0
EPS = 1e-6
Q_BLOCK = 128

MLA_HEADS = 8
MLA_Q_RANK = 256
MLA_KV_RANK = 128
MLA_NOPE = 64
MLA_ROPE = 32
MLA_V = 64
MLA_QK = MLA_NOPE + MLA_ROPE

CONV_CH = 512
CONV_W = 31

GQA_HEADS = 8
GQA_KV_HEADS = 2
GQA_HD = 64

N_BRANCH = 3
IN_SIZES = (MLA_Q_RANK, MLA_KV_RANK, MLA_ROPE, 2 * CONV_CH, GQA_HEADS * GQA_HD, GQA_KV_HEADS * GQA_HD, GQA_KV_HEADS * GQA_HD, N_BRANCH * D_MODEL)
D_IN = MLA_Q_RANK + MLA_KV_RANK + MLA_ROPE + 2 * CONV_CH + GQA_HEADS * GQA_HD + 2 * GQA_KV_HEADS * GQA_HD + N_BRANCH * D_MODEL

N_EXPERTS = 16
N_GROUPS = 4
EXPERTS_PER_GROUP = N_EXPERTS // N_GROUPS
TOP_K = 2
D_EXPERT = 512

kernel_name = "hybrid_mla_conformer_gqa_moe_dit"

def rms_norm(x, g):
    xf = x.astype(jnp.float32)
    y = xf * lax.rsqrt(jnp.mean(xf * xf, axis=-1, keepdims=True) + EPS)
    return (y * g.astype(jnp.float32)).astype(x.dtype)

def layer_norm(x, g, b):
    xf = x.astype(jnp.float32)
    mu = jnp.mean(xf, axis=-1, keepdims=True)
    var = jnp.mean(jnp.square(xf - mu), axis=-1, keepdims=True)
    y = (xf - mu) * lax.rsqrt(var + EPS)
    return (y * g.astype(jnp.float32) + b.astype(jnp.float32)).astype(x.dtype)

def split_cols(p):
    parts, start = [], 0
    for size in IN_SIZES:
        parts.append(p[..., start:start + size])
        start += size
    return parts

def rope_angles(pos, dim):
    inv = ROPE_BASE ** (-jnp.arange(0, dim, 2, dtype=jnp.float32) / dim)
    return pos.astype(jnp.float32)[:, None] * inv[None, :]

def rotate_half(x, ang):
    cos = jnp.cos(ang)[:, None, :].astype(x.dtype)
    sin = jnp.sin(ang)[:, None, :].astype(x.dtype)
    x1, x2 = jnp.split(x, 2, axis=-1)
    return jnp.concatenate([x1 * cos - x2 * sin, x2 * cos + x1 * sin], axis=-1)

def axial_rope(x, row, col):
    r = x.shape[-1]
    xr, xc = jnp.split(x, 2, axis=-1)
    return jnp.concatenate([rotate_half(xr, rope_angles(row, r // 2)), rotate_half(xc, rope_angles(col, r // 2))], axis=-1)

def block_attention(q, k, v, scale):
    b, nq, hk, g, d = q.shape
    nb = nq // Q_BLOCK
    qb = jnp.moveaxis(q.reshape(b, nb, Q_BLOCK, hk, g, d), 1, 0)

    def one_block(qi):
        s = jnp.einsum('bqhgd,bkhd->bhgqk', qi, k, preferred_element_type=jnp.float32) * scale
        p = jax.nn.softmax(s, axis=-1).astype(v.dtype)
        return jnp.einsum('bhgqk,bkhe->bqhge', p, v)

    out = lax.map(one_block, qb)
    return jnp.moveaxis(out, 0, 1).reshape(b, nq, hk, g, v.shape[-1])

def depthwise_conv(u, w, bias):
    out = lax.conv_general_dilated(u, w[:, None, :], window_strides=(1,), padding=[(CONV_W // 2, CONV_W // 2)],
                                   dimension_numbers=('NWC', 'WIO', 'NWC'), feature_group_count=u.shape[-1])
    return out + bias

def prepare(h, l, P, rope):
    b, n, _ = h.shape
    cq, ckv, kpe, conv_in, gq, gk, gv, gate_logits = split_cols(h @ P['w_in'][l])
    q = (rms_norm(cq, P['mla_q_norm'][l]) @ P['mla_w_uq'][l]).reshape(b, n, MLA_HEADS, MLA_QK)
    kv = (rms_norm(ckv, P['mla_kv_norm'][l]) @ P['mla_w_ukv'][l]).reshape(b, n, MLA_HEADS, MLA_NOPE + MLA_V)
    qg, kg = P['mla_q_gain'][l], P['mla_k_gain'][l]
    q_nope = rms_norm(q[..., :MLA_NOPE], qg[:MLA_NOPE])
    q_pe = rms_norm(q[..., MLA_NOPE:], qg[MLA_NOPE:])
    k_nope = rms_norm(kv[..., :MLA_NOPE], kg[:MLA_NOPE])
    v_mla = kv[..., MLA_NOPE:]
    k_pe = rms_norm(kpe, kg[MLA_NOPE:])[:, :, None, :]
    q_g = rms_norm(gq.reshape(b, n, GQA_HEADS, GQA_HD), P['gqa_q_gain'][l])
    k_g = rms_norm(gk.reshape(b, n, GQA_KV_HEADS, GQA_HD), P['gqa_k_gain'][l])
    v_g = gv.reshape(b, n, GQA_KV_HEADS, GQA_HD)
    if rope is not None:
        row, col = rope
        q_pe = axial_rope(q_pe, row, col)
        k_pe = axial_rope(k_pe, row, col)
        q_g = axial_rope(q_g, row, col)
        k_g = axial_rope(k_g, row, col)
    q_mla = jnp.concatenate([q_nope, q_pe], axis=-1)
    k_mla = jnp.concatenate([k_nope, jnp.broadcast_to(k_pe, (b, n, MLA_HEADS, MLA_ROPE))], axis=-1)
    return q_mla, k_mla, v_mla, q_g, k_g, v_g, conv_in, gate_logits

def conformer_conv(u, l, P):
    a, gt = jnp.split(u, 2, axis=-1)
    y = a * jax.nn.sigmoid(gt)
    y = depthwise_conv(y, P['conv_w'][l], P['conv_b'][l])
    y = jax.nn.silu(layer_norm(y, P['conv_ln_g'][l], P['conv_ln_b'][l]))
    return y @ P['conv_w_o'][l]

def mix(q_mla, q_g, conv_in, gate_logits, k_mla, v_mla, k_g, v_g, l, P):
    b, n = conv_in.shape[:2]
    o_mla = block_attention(q_mla[:, :, :, None, :], k_mla, v_mla, MLA_QK ** -0.5)
    o_mla = o_mla.reshape(b, n, MLA_HEADS * MLA_V) @ P['mla_w_o'][l]
    qg = q_g.reshape(b, n, GQA_KV_HEADS, GQA_HEADS // GQA_KV_HEADS, GQA_HD)
    o_gqa = block_attention(qg, k_g, v_g, GQA_HD ** -0.5).reshape(b, n, GQA_HEADS * GQA_HD) @ P['gqa_w_o'][l]
    o_conv = conformer_conv(conv_in, l, P)
    g = jax.nn.sigmoid(gate_logits).reshape(b, n, N_BRANCH, D_MODEL)
    merged = g[..., 0, :] * o_mla + g[..., 1, :] * o_conv + g[..., 2, :] * o_gqa
    return merged @ P['w_out'][l]

def moe(h, l, P):
    b, n, d = h.shape
    t = h.reshape(-1, d)
    s = jax.nn.sigmoid((t @ P['router_w']).astype(jnp.float32))
    sel = s + P['router_bias'].astype(jnp.float32)
    gscore = lax.top_k(sel.reshape(-1, N_GROUPS, EXPERTS_PER_GROUP), TOP_K)[0].sum(-1)
    gbest = jnp.argmax(gscore, axis=-1)
    in_group = (jnp.arange(N_EXPERTS) // EXPERTS_PER_GROUP)[None, :] == gbest[:, None]
    _, idx = lax.top_k(jnp.where(in_group, sel, -jnp.inf), TOP_K)
    w = jnp.take_along_axis(s, idx, axis=-1)
    w = w / jnp.sum(w, axis=-1, keepdims=True)
    combine = jnp.sum(jax.nn.one_hot(idx, N_EXPERTS, dtype=jnp.float32) * w[..., None], axis=1).astype(t.dtype)
    wg, wu, wd = P['moe_w_gate'][l], P['moe_w_up'][l], P['moe_w_down'][l]
    out = jnp.zeros_like(t)
    for e in range(N_EXPERTS):
        he = jax.nn.silu(t @ wg[e]) * (t @ wu[e])
        out = out + combine[:, e:e + 1] * (he @ wd[e])
    return out.reshape(b, n, d)

def setup_inputs(seed: int = 0) -> dict:
    key = jax.random.key(seed)
    ks = jax.random.split(key, 32)
    cnt = [0]

    def nrm(shape, scale):
        k = ks[cnt[0]]
        cnt[0] += 1
        return scale * jax.random.normal(k, shape, jnp.float32)

    def gain(shape):
        return 1.0 + nrm(shape, 0.02)

    L, D, E, F = DEPTH, D_MODEL, N_EXPERTS, D_EXPERT
    return {
        'x': nrm((BATCH, SEQ, D), 1.0),
        'c': nrm((BATCH, D), 1.0),
        'ctx': nrm((BATCH, CTX_LEN, D), 1.0),
        'c_ctx': nrm((D,), 1.0),
        'w_mod': nrm((L, D, 6 * D), 0.5 * D ** -0.5),
        'b_mod': nrm((L, 6 * D), 0.02),
        'norm1_g': gain((L, D)),
        'norm2_g': gain((L, D)),
        'w_in': nrm((L, D, D_IN), D ** -0.5),
        'mla_q_norm': gain((L, MLA_Q_RANK)),
        'mla_kv_norm': gain((L, MLA_KV_RANK)),
        'mla_w_uq': nrm((L, MLA_Q_RANK, MLA_HEADS * MLA_QK), MLA_Q_RANK ** -0.5),
        'mla_w_ukv': nrm((L, MLA_KV_RANK, MLA_HEADS * (MLA_NOPE + MLA_V)), MLA_KV_RANK ** -0.5),
        'mla_q_gain': gain((L, MLA_QK)),
        'mla_k_gain': gain((L, MLA_QK)),
        'mla_w_o': nrm((L, MLA_HEADS * MLA_V, D), (MLA_HEADS * MLA_V) ** -0.5),
        'conv_w': nrm((L, CONV_W, CONV_CH), CONV_W ** -0.5),
        'conv_b': nrm((L, CONV_CH), 0.02),
        'conv_ln_g': gain((L, CONV_CH)),
        'conv_ln_b': nrm((L, CONV_CH), 0.02),
        'conv_w_o': nrm((L, CONV_CH, D), CONV_CH ** -0.5),
        'gqa_q_gain': gain((L, GQA_HD)),
        'gqa_k_gain': gain((L, GQA_HD)),
        'gqa_w_o': nrm((L, GQA_HEADS * GQA_HD, D), (GQA_HEADS * GQA_HD) ** -0.5),
        'w_out': nrm((L, D, D), D ** -0.5),
        'router_w': nrm((D, E), D ** -0.5),
        'router_bias': nrm((E,), 0.01),
        'moe_w_gate': nrm((L, E, D, F), D ** -0.5),
        'moe_w_up': nrm((L, E, D, F), D ** -0.5),
        'moe_w_down': nrm((L, E, F, D), F ** -0.5),
    }

def reference(x, c, ctx, c_ctx, w_mod, b_mod, norm1_g, norm2_g, w_in, mla_q_norm, mla_kv_norm, mla_w_uq, mla_w_ukv,
              mla_q_gain, mla_k_gain, mla_w_o, conv_w, conv_b, conv_ln_g, conv_ln_b, conv_w_o, gqa_q_gain, gqa_k_gain,
              gqa_w_o, w_out, router_w, router_bias, moe_w_gate, moe_w_up, moe_w_down):
    P = dict(w_in=w_in, mla_q_norm=mla_q_norm, mla_kv_norm=mla_kv_norm, mla_w_uq=mla_w_uq, mla_w_ukv=mla_w_ukv,
             mla_q_gain=mla_q_gain, mla_k_gain=mla_k_gain, mla_w_o=mla_w_o, conv_w=conv_w, conv_b=conv_b,
             conv_ln_g=conv_ln_g, conv_ln_b=conv_ln_b, conv_w_o=conv_w_o, gqa_q_gain=gqa_q_gain,
             gqa_k_gain=gqa_k_gain, gqa_w_o=gqa_w_o, w_out=w_out, router_w=router_w, router_bias=router_bias,
             moe_w_gate=moe_w_gate, moe_w_up=moe_w_up, moe_w_down=moe_w_down)
    n = x.shape[1]
    rows = n // GRID_W
    row = jnp.repeat(jnp.arange(rows, dtype=jnp.int32), GRID_W)
    col = jnp.tile(jnp.arange(GRID_W, dtype=jnp.int32), rows)
    rope = (row, col)
    s_lat = jax.nn.silu(c)
    s_ctx = jax.nn.silu(c_ctx)
    xc = ctx
    for l in range(DEPTH):
        last = l == DEPTH - 1
        sh1, sc1, g1, sh2, sc2, g2 = jnp.split((s_lat @ w_mod[l] + b_mod[l])[:, None, :], 6, axis=-1)
        csh1, csc1, cg1, csh2, csc2, cg2 = jnp.split((s_ctx @ w_mod[l] + b_mod[l])[None, None, :], 6, axis=-1)
        h = rms_norm(x, norm1_g[l]) * (1 + sc1) + sh1
        hc = rms_norm(xc, norm1_g[l]) * (1 + csc1) + csh1
        q_mla, k_mla, v_mla, q_g, k_g, v_g, conv_in, gl = prepare(h, l, P, rope)
        cq_mla, ck_mla, cv_mla, cq_g, ck_g, cv_g, cconv_in, cgl = prepare(hc, l, P, None)
        k_mla_all = jnp.concatenate([k_mla, ck_mla], axis=1)
        v_mla_all = jnp.concatenate([v_mla, cv_mla], axis=1)
        k_g_all = jnp.concatenate([k_g, ck_g], axis=1)
        v_g_all = jnp.concatenate([v_g, cv_g], axis=1)
        x = x + g1 * mix(q_mla, q_g, conv_in, gl, k_mla_all, v_mla_all, k_g_all, v_g_all, l, P)
        if not last:
            xc = xc + cg1 * mix(cq_mla, cq_g, cconv_in, cgl, ck_mla, cv_mla, ck_g, cv_g, l, P)
        h2 = rms_norm(x, norm2_g[l]) * (1 + sc2) + sh2
        x = x + g2 * moe(h2, l, P)
        if not last:
            hc2 = rms_norm(xc, norm2_g[l]) * (1 + csc2) + csh2
            xc = xc + cg2 * moe(hc2, l, P)
    return x


_drawn_inputs = setup_inputs


def setup_inputs(seed=0):
    import zlib

    import numpy as np

    out = dict(_drawn_inputs(seed))
    spreads = {}
    factors = {'norm1_g': 8.0,
     'mla_q_norm': 8.0,
     'mla_kv_norm': 4.573,
     'mla_q_gain': 8.0,
     'mla_k_gain': 8.0,
     'conv_b': 10.697,
     'conv_ln_g': 3.034,
     'conv_ln_b': 4.478,
     'gqa_q_gain': 8.0,
     'gqa_k_gain': 8.0}
    for name, (base, spread) in spreads.items():
        noise = np.random.default_rng([zlib.crc32(name.encode()), seed]).standard_normal(out[name].shape)
        drawn = base * np.exp(spread * noise) if base else spread * noise
        out[name] = __import__('jax').numpy.asarray(drawn.astype(out[name].dtype))
    for name, factor in factors.items():
        out[name] = (out[name] * factor).astype(out[name].dtype)
    return out
```

```python
from contextlib import ExitStack

import concourse.bass as bass
from concourse import mybir

P = 128
D, SEQ, CTX, DEPTH = 1024, 256, 256, 2
LT, CT = SEQ // P, CTX // P
NT = LT + CT
KC = D // P
D_MOD = 6 * D
QR, KVR, ROPE, NOPE, VD, H = 256, 128, 32, 64, 64, 8
QK = NOPE + ROPE
CC, CW = 512, 31
GH, GKV, GD = 8, 2, 64
NE, NG, EG, F = 16, 4, 4, 512
GRID_W = 64
EPS = 1e-6
HALF = 512
COL_CQ, COL_CONV, COL_GQ = 0, QR + KVR + ROPE, QR + KVR + ROPE + 2 * CC
COL_GK = COL_GQ + GH * GD
COL_GATE = COL_GK + 2 * GKV * GD
D_IN = COL_GATE + 3 * D
W_CQKV = QR + KVR + ROPE
ITEMS = 24
LISTW = ITEMS + 2
PADW = SEQ + CW - 1

F32 = mybir.dt.float32
I32 = mybir.dt.int32
U32 = mybir.dt.uint32
ALU = mybir.AluOpType
ACT = mybir.ActivationFunctionType
AX = mybir.AxisListType.X

C_ID, C_ROPE = 0, 128
ROPEW = 2 * (2 * 8) + 2 * (2 * 16)
C_ALL = C_ROPE + LT * ROPEW
R_S, R_MASK = 0, 1
R_TRI, R_ONES, R_TOK, R_EID, R_REV, R_GREV, R_IT, R_LT = 0, 128, 256, 260, 276, 292, 296, 304
R_ALL = R_LT + NE * NE


MSLOT = (1, 2, 3, 0, 4, 5)


class Banks:

    def __init__(self, full, free):
        self.full, self.free = full, free
        self.uses = [0] * len(full)
        self.turn = {}
        self.at = {}

    def plan(self, key, banks):
        n = self.turn.get(banks, 0)
        self.turn[banks] = n + 1
        b = banks[n % len(banks)]
        self.at[key] = (b, self.uses[b])
        self.uses[b] += 1

    def wait_free(self, eng, key):
        b, k = self.at[key]
        if k:
            eng.wait_ge(self.free[b], k)

    def wait_full(self, eng, key):
        b, k = self.at[key]
        eng.wait_ge(self.full[b], k + 1)

    def wait_read(self, eng, key):
        b, k = self.at[key]
        eng.wait_ge(self.free[b], k + 1)

    def filled(self, ins, key):
        ins.then_inc(self.full[self.at[key][0]], 1)

    def read(self, ins, key):
        ins.then_inc(self.free[self.at[key][0]], 1)


def backbone(nc, a, consts, out):
    with ExitStack() as ctx:
        sem = lambda n: ctx.enter_context(nc.semaphore(n))
        ps = [ctx.enter_context(nc.psum_tensor(f"bank{i}", [P, HALF], F32)) for i in range(8)]
        base = (nc.sbuf_base + 63) // 64 * 64

        def sb(name, at, shape, dt=F32):
            return nc.alloc_sbuf_tensor_at(name, [P, *shape], dt, offset=base + 4 * at)

        slab = [sb(f"slab{s}", 4096 * s, [8, HALF]) for s in range(6)]
        o = 16384
        ybuf = sb("ybuf", o, [NT, CC])
        ypad = sb("ypad", o + 2048, [4, 2, PADW])
        cv = sb("cv", o + 2048 + 8 * PADW, [4, 2, SEQ])
        q_tm = sb("q_tm", o, [NT, H, QK])
        kfull = sb("kfull", o + 3072, [NT, H, QK])
        merged = sb("merged", o, [NT, D])
        crows = sb("crows", o, [CC])
        o += 2048 + 8 * PADW + 2048
        v_tm = sb("v_tm", o, [NT, H * VD])
        oT_mla = sb("oT_mla", o, [4, NT * P])
        o += 2048
        x_sb = sb("x_sb", o, [NT, D]); o += 4096
        hT = sb("hT", o, [KC, NT * P]); o += 4096
        rowA = sb("rowA", o, [2, D])
        rowB = sb("rowB", o + 2048, [2, D]); o += 4096
        m0 = o
        cqkv = sb("cqkv", o, [NT, W_CQKV])
        normg = sb("normg", o, [D]); o += 4 * W_CQKV
        gkv = sb("gkv", o, [NT, 2 * GKV * GD]); o += 1024
        gq = sb("gq", o, [NT, GH * GD])
        oT_gqa = sb("oT_gqa", o, [4, NT * P]); o += 2048
        zT = sb("zT", o, [4, NT * P]); o += 2048
        o_tm = sb("o_tm", o, [NT, H * VD]); o += 2048
        headT = sb("headT", o, [2, 2, NT * P])
        htile = sb("htile", o, [2, D]); o += 2048
        prob = sb("prob", o, [2, HALF])
        probT = sb("probT", o + 1024, [2, 4, P])
        cT = sb("cT", o, [3, NT * P])
        junk = sb("junk", o, [D]); o += 2048
        sgt = sb("sgt", o, [2, HALF])
        tmp = sb("tmp", o + 1024, [HALF])
        tmp3 = sb("tmp3", o, [1536]); o += 1536
        rcst = sb("rcst", o - 1536, [R_ALL])

        def small(name, shape):
            nonlocal o
            t = sb(name, o, shape)
            n = 1
            for d in shape:
                n *= d
            o += (n + 7) // 8 * 8
            return t

        cst = small("cst", [C_ALL])
        qkg = small("qkg", [2 * QK + 2 * GD + NE])
        colg = small("colg", [3])
        convc = small("convc", [4, CW + 3])
        sT = small("sT", [2 * KC])
        ssum = small("ssum", [3, NT])
        rowi = small("rowi", [2 * 2 * NT])
        wk = small("wk", [2, NT])
        rw = small("rw", [KC, NE])
        rowY = sb("rowY", o, [2, NT], U32)
        rowL = sb("rowL", o + 8, [2, NT], U32)
        toku = sb("toku", o + 16, [NT], U32)
        ni = sb("ni", o + 24, [32], I32)
        cur = sb("cur", o + 56, [2, 8], U32)
        o += 72
        rinv = small("rinv", [4])
        mxs = small("mxs", [4])
        cstat = small("cstat", [NT, 2])
        nmax = small("nmax", [4])
        rsum = small("rsum", [4])
        zero = sb("zero", o, [LISTW], U32)
        lst = sb("lst", o, [LISTW], U32)
        o += 32
        bnst = small("bnst", [NT, 8])
        mv = small("mv", [NT, 2])
        assert base + 4 * o <= nc.sbuf_usable_end, (base + 4 * o - nc.sbuf_usable_end)
        e = m0 + 4 * W_CQKV
        xg = sb("xg", e, [2, D]); e += 2048
        yg = sb("yg", e, [2, D]); e += 2048
        xgT = sb("xgT", e, [2, KC, P]); e += 2048
        sg = sb("sg", e, [2, F]); e += 1024
        hh = sb("hh", e, [2, F]); e += 1024
        hhT = sb("hhT", e, [2, 4, P]); e += 1024
        r1 = sb("r1", e, [32, NT * NE]); e += 2048
        mrow = sb("mrow", m0, [4, HALF])
        mbias = sb("mbias", m0 + 2048, [4, HALF])
        crow = sb("crow", m0 + 4096, [P])
        csig = sb("csig", m0 + 4096 + P, [2 * KC])
        ropt = sb("ropt", m0 + 4 * W_CQKV + 1024 + 2048 + 2048 + 256, [4, 256])
        kpe = sb("kpe", m0 + 4 * W_CQKV + 1024 + 2048 + 2048 + 1280, [NT, ROPE])
        stat = sb("stat", m0 + 4 * W_CQKV + 1024 + 2048 + 2048, [NT, 35])

        mod_d = nc.dram_tensor("mod_d", [2, DEPTH * D_MOD], F32, kind="Internal").ap()
        list_d = [nc.dram_tensor(f"list_d{l}", [P * LISTW, 1], U32, kind="Internal").ap() for l in range(DEPTH)]
        h2_d = [nc.dram_tensor(f"h2_d{l}", [(NT, LT)[l] * P, D], F32, kind="Internal").ap() for l in range(DEPTH)]
        y_d = [nc.dram_tensor(f"y_d{l}", [ITEMS * P, D], F32, kind="Internal").ap() for l in range(DEPTH)]

        ident = cst[:, C_ID:C_ID + P]

        bank = Banks([sem(f"bank_full{i}") for i in range(8)], [sem(f"bank_read{i}") for i in range(8)])
        s_cst, s_c, s_x, s_zero, s_out = sem("s_cst"), sem("s_c"), sem("s_x"), sem("s_zero"), sem("s_out")
        slab_in = [sem(f"slab_in{i}") for i in range(4)]
        mod_in = [sem(f"mod_in{i}") for i in range(4)]
        mod_full, mod_read = sem("mod_full"), sem("mod_read")
        mod_out = [sem(f"mod_out{i}") for i in range(4)]
        s_silu_c, s_zset = sem("s_silu_c"), sem("s_zset")
        dve_step, act_step = sem("dve_step"), sem("act_step")
        names = ["pad", "sq", "sqm", "sqrt", "rows1", "rows2", "rows3", "rows4", "par", "h", "csq", "cn", "st", "nrm",
                 "nmax", "cvd", "lnv", "lns", "mg", "xm", "h2", "h2o", "rcst", "mask", "ni", "xf", "scat"]
        S = [{n: sem(f"{n}{l}") for n in names} for l in range(DEPTH)]
        mnames = ["gu", "sig", "h", "xt", "xtA", "xtD", "ht", "htA", "y", "yA", "yD", "cur"]
        M = [{n: sem(f"moe_{n}{l}") for n in mnames} for l in range(DEPTH)]
        m_in = [[sem(f"moe_in{l}_{i}") for i in range(6)] for l in range(DEPTH)]
        m_xg = [[sem(f"moe_xg{l}_{i}") for i in range(2)] for l in range(DEPTH)]
        m_yo = [[sem(f"moe_yo{l}_{i}") for i in range(2)] for l in range(DEPTH)]
        m_yk = [sem(f"moe_yk{i}") for i in range(2)]

        QT = [NT, LT]
        keys_of = [(0, NT) if t < LT else (LT, NT) for t in range(NT)]

        def slabs(l):
            T = QT[l] - 1

            def win(c0, w):
                return [(w_cols(a["w_in"][l], c0, w), w)]
            yield "b1", win(COL_CONV, CC), (l, "b1", T)
            yield "b2", win(COL_CONV + CC, CC), (l, "b2", T)
            yield "b0", win(COL_CQ, W_CQKV), (l, "b0", NT - 1)
            yield "b4", win(COL_GK, 2 * GKV * GD), (l, "b4", NT - 1)
            yield "b3", win(COL_GQ, GH * GD), (l, "b3", T)
            yield "up", None, (l, "ukv", NT - 1, 1)
            for b, w in enumerate(("mla_w_o", "conv_w_o", "gqa_w_o")):
                yield f"o{b}", [(a[w][l].rearrange("(k p) n -> p k n", p=P), None)], (l, "o", b, 1, T)
                for hf in range(2):
                    yield f"g{b}{hf}", win(COL_GATE + b * D + hf * HALF, HALF), (l, "g", b, hf, T)
            for hf in range(2):
                yield f"w{hf}", [(w_cols(a["w_out"][l], hf * HALF, HALF), HALF)], (l, "w", hf, T)

        def w_cols(w, c0, n):
            return w[:, c0:c0 + n].rearrange("(k p) n -> p k n", p=P)

        slab_plan, slab_at = [], {}
        for l in range(DEPTH):
            for n, (name, src, last) in enumerate(slabs(l)):
                loads = 2 if name == "up" else 1
                slot = n % 4
                before = sum(q[4] for q in slab_plan if q[3] == slot)
                slab_plan.append((l, name, src, slot, loads, last))
                slab_at[l, name] = (slot, 16 * (before + loads))

        def wait_slab(eng, l, name):
            slot, v = slab_at[l, name]
            eng.wait_ge(slab_in[slot], v)
            return slab[slot]

        lo, hi = (0, 1, 2, 3), (4, 5, 6, 7)

        def attn_units(l):
            return [(h, t) for h in range(H) for t in range(QT[l])]

        def plan_layer(l):
            T = QT[l]
            bank.plan((l, "conv_cols"), hi)
            for t in range(NT):
                for hf in range(2):
                    bank.plan((l, "h", t, hf), hi)
            for name, n, bs in (("b1", T, lo), ("b2", T, hi), ("b0", NT, lo), ("b4", NT, hi)):
                for t in range(n):
                    bank.plan((l, name, t), bs)
            for c in range(4):
                bank.plan((l, "yT", c), hi)
            for t in range(T):
                bank.plan((l, "b3", t), lo)
            for c in range(3):
                bank.plan((l, "cT", c), hi)
            for t in range(T):
                bank.plan((l, "cvb", t), hi)
            for c in range(4):
                bank.plan((l, "zT", c), hi)
            for t in range(T):
                bank.plan((l, "uq", t, 0), lo)
                bank.plan((l, "uq", t, 1), lo)
            for t in range(NT):
                bank.plan((l, "ukv", t, 0), lo)
                bank.plan((l, "ukv", t, 1), lo)
            for kind in ("mla", "gqa"):
                for i, step in attn_order(l, kind):
                    if step == "head":
                        bank.plan((l, kind, "qT", i), (0, 1))
                        if kind == "mla" or i % 4 == 0:
                            bank.plan((l, kind, "kT", i), (0, 1))
                    else:
                        bank.plan((l, kind, step, i), {"s": (2, 3), "pT": (4, 5), "pv": (6, 7)}[step])
                for c in range(4):
                    bank.plan((l, kind, "oT", c), hi)
            for b in range(3):
                for hf in range(2):
                    for t in range(T):
                        bank.plan((l, "o", b, hf, t), lo)
                        bank.plan((l, "g", b, hf, t), hi)
            for hf in range(2):
                for t in range(T):
                    bank.plan((l, "mT", t, hf), hi)
            for hf in range(2):
                for t in range(T):
                    bank.plan((l, "w", hf, t), lo)
            for t in range(T):
                for hf in range(2):
                    bank.plan((l, "h2", t, hf), hi)
            bank.plan((l, "router"), (0,))
            bank.plan((l, "place"), (1,))

        def attn_order(l, kind):
            U = attn_units(l)
            yield 0, "head"
            for i in range(len(U) + 2):
                if i + 1 < len(U) and U[i + 1][1] == 0:
                    yield U[i + 1][0], "head"
                if i < len(U):
                    yield i, "s"
                if 1 <= i <= len(U):
                    yield i - 1, "pT"
                if i >= 2:
                    yield i - 2, "pv"

        for l in range(DEPTH):
            plan_layer(l)

        def load_expert(sp, l, slot, kind, w):
            src = w.rearrange("o (k p) n -> p (o k) n", p=P)
            dst = slab[slot][:] if kind < 2 else slab[slot][:].rearrange("p (k j) n -> p k (j n)", k=4)
            sp.dma_start(dst, src).then_inc(m_in[l][slot], 16)

        def store_item(sp, l, m, u, item):
            sp.wait_ge(m["yA"], item + 2)
            sp.wait_ge(m["yD"], item + 2)
            sp.dma_start(y_d[l][bass.ds(item * P, P), :], yg[:, u, :]).then_inc(m_yo[l][u], 16)

        block = ctx.enter_context(nc.Block())

        @block.sync
        def _(sp):
            sp.dma_start(cst[:], consts[:, 0:C_ALL]).then_inc(s_cst, 16)
            sp.dma_start(crow[0:KC, :], a["c"].rearrange("o (k p) -> (o k) p", p=P)).then_inc(s_c, 16)
            sp.dma_start(crow[KC:2 * KC, :], a["c_ctx"].rearrange("(k p) -> k p", p=P)).then_inc(s_c, 16)
            for l in range(DEPTH):
                w_v = a["w_mod"][l].rearrange("(k p) n -> p k n", p=P)
                b_v = a["b_mod"][l:l + 1, :]
                with sp.Fori(0, D_MOD // HALF // 4) as i:
                    for u in range(4):
                        sp.wait_ge(mod_read, 4 * i + (12 * l + u + 1))
                        cols = bass.ds((4 * i + u) * HALF, HALF)
                        sp.dma_start(slab[u][:], w_v[:, :, cols]).then_inc(mod_in[u], 16)
                        sp.dma_start(mbias[0:2, u, :], b_v[:, cols].to_broadcast([2, HALF])).then_inc(mod_in[u], 16)
            sp.dma_start(x_sb[:, 0:LT, :], a["x"].rearrange("o (t p) d -> p (o t) d", p=P)).then_inc(s_x, 16)
            sp.dma_start(x_sb[:, LT:NT, :], a["ctx"].rearrange("o (t p) d -> p (o t) d", p=P)).then_inc(s_x, 16)
            for l in range(DEPTH):
                mine = [q for q in slab_plan if q[0] == l]
                for n, (_, name, src, slot, loads, last) in enumerate(mine):
                    if n >= 4:
                        bank.wait_full(sp, mine[n - 4][5])
                    elif l == 0:
                        sp.wait_ge(mod_read, 24 + 4)
                    if name == "up":
                        flat = slab[slot][:].rearrange("p k n -> p (k n)")
                        uq = a["mla_w_uq"][l].rearrange("(k p) n -> p k n", p=P)
                        sp.dma_start(flat[:, 0:2 * H * QK].rearrange("p (k n) -> p k n", k=2), uq).then_inc(slab_in[slot], 16)
                        sp.dma_start(flat[:, 2 * H * QK:2 * H * QK + H * (NOPE + VD)], a["mla_w_ukv"][l]).then_inc(slab_in[slot], 16)
                        continue
                    ap, w = src[0]
                    if w is None:
                        dst = slab[slot][:].rearrange("p (k j) n -> p k (j n)", k=4)
                    else:
                        dst = slab[slot][:, :, 0:w]
                    sp.dma_start(dst, ap).then_inc(slab_in[slot], 16)

                m = M[l]

                def load_item(u, e):
                    for kind, w in enumerate(("moe_w_gate", "moe_w_up", "moe_w_down")):
                        yield kind, MSLOT[3 * u + kind], a[w][l][e]

                for u in range(2):
                    for kind, slot, w in load_item(u, slice(u, u + 1)):
                        bank.wait_full(sp, mine[{1: 13, 2: 14, 3: 15, 0: 16, 4: 16, 5: 16}[slot]][5])
                        load_expert(sp, l, slot, kind, w)
                sp.wait_ge(S[l]["ni"], 1)
                pairs = sp.value_load(ni[0:1, ITEMS:ITEMS + 1], min_val=NE // 2, max_val=ITEMS // 2)
                with sp.Fori(1, pairs) as q:
                    for u in range(2):
                        e = sp.value_load(ni[0:1, bass.ds(2 * q + u, 1)], min_val=0, max_val=NE - 1)
                        for kind, slot, w in load_item(u, bass.ds(e, 1)):
                            if kind < 2:
                                sp.wait_ge(m["gu"], 4 * q + (2 * u - 4 + kind + 1))
                            else:
                                sp.wait_ge(m["y"], 4 * q + (2 * u - 4 + 2))
                            load_expert(sp, l, slot, kind, w)
                        store_item(sp, l, m, u, 2 * q + (u - 2))
                for u in range(2):
                    store_item(sp, l, m, u, 2 * pairs + (u - 2))

        @block.tensor
        def _(pe):
            def fill(key, mms):
                bank.wait_free(pe, key)
                ins = None
                for ins in mms:
                    pass
                bank.filled(ins, key)

            def pb(key):
                return ps[bank.at[key][0]]

            pe.wait_ge(s_cst, 16)
            pe.wait_ge(s_c, 32)
            pe.transpose(ps[7][:, 0:2 * KC], crow[0:2 * KC, :], ident[0:2 * KC, 0:2 * KC]).then_inc(mod_full, 1)
            pe.wait_ge(s_silu_c, 2)
            for l in range(DEPTH):
                with pe.Fori(0, D_MOD // HALF // 4) as i:
                    for u in range(4):
                        pe.wait_ge(mod_in[u], 32 * i + 32 * (3 * l + 1))
                        pe.wait_ge(mod_read, 4 * i + (12 * l + u + 1))
                        for k in range(KC):
                            mm = pe.matmul(ps[u][0:2, :], sT[:, k:2 * KC:KC], slab[u][:, k, :], start=k == 0, stop=k == KC - 1)
                        mm.then_inc(mod_full, 1)

            def transposes(key, parts, rows=P):
                bank.wait_free(pe, key)
                for src, c in parts:
                    k, n = src.shape[0], src.shape[-1]
                    mm = pe.transpose(pb(key)[0:n, c:c + k], src, ident[0:k, 0:k])
                bank.filled(mm, key)

            def product(key, lhs, rhs, n, c=0, rows=P):
                bank.wait_free(pe, key)
                for k in range(len(lhs)):
                    mm = pe.matmul(pb(key)[0:rows, c:c + n], lhs[k], rhs[k], start=k == 0, stop=k == len(lhs) - 1)
                bank.filled(mm, key)

            for l in range(DEPTH):
                T, s = QT[l], S[l]
                pe.wait_ge(s["par"], 16 * 11)
                transposes((l, "conv_cols"), [(crows[0:CW + 3, c * P:(c + 1) * P], c * (CW + 3)) for c in range(4)])

                for t in range(NT):
                    pe.wait_ge(s["h"], t + 1)
                    for hf in range(2):
                        transposes((l, "h", t, hf), [(htile[:, t % 2, (4 * hf + c) * P:(4 * hf + c + 1) * P], c * P) for c in range(4)])

                def project(name, t, w, key=None):
                    sl = wait_slab(pe, l, name)
                    product(key or (l, name, t), [hT[:, k, t * P:(t + 1) * P] for k in range(KC)], [sl[:, k, 0:w] for k in range(KC)], w)

                for t in range(T):
                    bank.wait_read(pe, (l, "h", t, 0))
                    bank.wait_read(pe, (l, "h", t, 1))
                    project("b1", t, CC)
                for t in range(T):
                    project("b2", t, CC)
                for t in range(NT):
                    bank.wait_read(pe, (l, "h", t, 0))
                    bank.wait_read(pe, (l, "h", t, 1))
                    project("b0", t, W_CQKV)
                for t in range(NT):
                    project("b4", t, 2 * GKV * GD)
                for c in range(4):
                    for t in range(T):
                        bank.wait_read(pe, (l, "b1", t))
                    transposes((l, "yT", c), [(ybuf[:, t, c * P:(c + 1) * P], t * P) for t in range(T)])
                for t in range(T):
                    project("b3", t, GH * GD)
                pe.wait_ge(s["cn"], 1)
                for c in range(3):
                    tiles = range(T) if c < 2 else range(NT)
                    transposes((l, "cT", c), [(cqkv[:, t, c * P:(c + 1) * P], t * P) for t in tiles])
                pe.wait_ge(s["cvd"], 4)
                for t in range(T):
                    r = (t % LT) * P
                    transposes((l, "cvb", t), [(cv[:, c, t // LT, r:r + P], c * P) for c in range(4)])
                for t in range(T):
                    bank.wait_read(pe, (l, "cvb", t))
                for c in range(4):
                    transposes((l, "zT", c), [(ybuf[:, t, c * P:(c + 1) * P], t * P) for t in range(T)])

                sl = wait_slab(pe, l, "up")[:].rearrange("p k n -> p (k n)")
                uq = sl[:, 0:2 * H * QK].rearrange("p (k n) -> p k n", k=2)
                ukv = sl[:, 2 * H * QK:2 * H * QK + H * (NOPE + VD)]
                for c in range(3):
                    bank.wait_read(pe, (l, "cT", c))
                for t in range(T):
                    cols = slice(t * P, (t + 1) * P)
                    product((l, "uq", t, 0), [cT[:, k, cols] for k in range(2)], [uq[:, k, 0:HALF] for k in range(2)], HALF)
                    product((l, "uq", t, 1), [cT[:, k, cols] for k in range(2)], [uq[:, k, HALF:H * QK] for k in range(2)], H * QK - HALF)
                for t in range(NT):
                    for hf in range(2):
                        product((l, "ukv", t, hf), [cT[:, 2, t * P:(t + 1) * P]], [ukv[:, hf * HALF:(hf + 1) * HALF]], HALF)

                pe.wait_ge(s["nrm"], 1)
                U = attn_units(l)
                for kind in ("mla", "gqa"):
                    d = QK if kind == "mla" else GD
                    kslot = (lambda h: h % 2) if kind == "mla" else (lambda h: h // 4)
                    for i, step in attn_order(l, kind):
                        if step == "head":
                            if kind == "mla":
                                q_of, k_of = (lambda t, h: q_tm[:, t, h, :]), (lambda t, h: kfull[:, t, h, :])
                            else:
                                q_of, k_of = (lambda t, h: gq[:, t, h * GD:(h + 1) * GD]), (lambda t, h: gkv[:, t, (h // 4) * GD:(h // 4 + 1) * GD])
                            transposes((l, kind, "qT", i), [(q_of(t, i), t * P) for t in range(T)])
                            if kind == "mla" or i % 4 == 0:
                                transposes((l, kind, "kT", i), [(k_of(t, i), t * P) for t in range(NT)])
                            continue
                        h, t = U[i]
                        k0, k1 = keys_of[t]
                        n = k1 - k0
                        if step == "s":
                            bank.wait_read(pe, (l, kind, "qT", h))
                            bank.wait_read(pe, (l, kind, "kT", h if kind == "mla" else h // 4 * 4))
                            product((l, kind, "s", i), [headT[0:d, h % 2, 0, t * P:(t + 1) * P]],
                                    [headT[0:d, kslot(h), 1, k0 * P:k1 * P]], n * P)
                        elif step == "pT":
                            bank.wait_read(pe, (l, kind, "s", i))
                            transposes((l, kind, "pT", i), [(prob[:, i % 2, j * P:(j + 1) * P], j * P) for j in range(n)])
                        else:
                            bank.wait_read(pe, (l, kind, "pT", i))
                            v = (lambda j: v_tm[:, j, h * VD:(h + 1) * VD]) if kind == "mla" else \
                                (lambda j: gkv[:, j, (GKV + h // 4) * GD:(GKV + h // 4 + 1) * GD])
                            product((l, kind, "pv", i), [probT[:, i % 2, j, :] for j in range(n)],
                                    [v(k0 + j) for j in range(n)], VD)
                    for i in range(len(U)):
                        if i >= len(U) - 2:
                            bank.wait_read(pe, (l, kind, "pv", i))
                    for c in range(4):
                        transposes((l, kind, "oT", c), [(o_tm[:, t, c * P:(c + 1) * P], t * P) for t in range(T)])

                for b in range(3):
                    oT = (oT_mla, zT, oT_gqa)[b]
                    for c in range(4):
                        bank.wait_read(pe, ((l, "mla", "oT", c), (l, "zT", c), (l, "gqa", "oT", c))[b])
                    for hf in range(2):
                        for t in range(T):
                            wo = wait_slab(pe, l, f"o{b}")[:].rearrange("p (k j) n -> p k (j n)", k=4)
                            product((l, "o", b, hf, t), [oT[:, c, t * P:(t + 1) * P] for c in range(4)],
                                    [wo[:, c, hf * HALF:(hf + 1) * HALF] for c in range(4)], HALF)
                            project(f"g{b}{hf}", t, HALF, key=(l, "g", b, hf, t))
                for hf in range(2):
                    for t in range(T):
                        pe.wait_ge(s["mg"], hf * T + t + 1)
                        transposes((l, "mT", t, hf), [(merged[:, t, (4 * hf + c) * P:(4 * hf + c + 1) * P], c * P) for c in range(4)])
                for hf in range(2):
                    for t in range(T):
                        bank.wait_read(pe, (l, "mT", t, 0))
                        bank.wait_read(pe, (l, "mT", t, 1))
                        project(f"w{hf}", t, HALF, key=(l, "w", hf, t))

                for t in range(T):
                    pe.wait_ge(s["h2"], t + 1)
                    for hf in range(2):
                        transposes((l, "h2", t, hf), [(htile[:, t % 2, (4 * hf + c) * P:(4 * hf + c + 1) * P], c * P) for c in range(4)])
                key = (l, "router")
                bank.wait_free(pe, key)
                pe.wait_ge(s_zero, 16 * 7)
                for t in range(T):
                    bank.wait_read(pe, (l, "h2", t, 0))
                    bank.wait_read(pe, (l, "h2", t, 1))
                    for k in range(KC):
                        mm = pe.matmul(pb(key)[:, t * NE:(t + 1) * NE], hT[:, k, t * P:(t + 1) * P], rw[:, k, :], start=k == 0, stop=k == KC - 1)
                bank.filled(mm, key)
                key = (l, "place")
                bank.wait_free(pe, key)
                pe.wait_ge(s["rcst"], 16)
                pe.wait_ge(s["mask"], 1)
                mask = r1[:, R_MASK, 0:T * NE].rearrange("p (t e) -> p t e", e=NE)
                for t in range(T):
                    for b in range(t + 1):
                        lhs = rcst[:, R_TRI:R_TRI + P] if b == t else rcst[:, R_ONES:R_ONES + P]
                        pe.matmul(pb(key)[:, t * NE:(t + 1) * NE], lhs, mask[:, b, :], start=b == 0, stop=b == t)
                for t in range(T):
                    mm = pe.matmul(pb(key)[:, NT * NE:(NT + 1) * NE], rcst[:, R_ONES:R_ONES + P], mask[:, t, :], start=t == 0, stop=t == T - 1)
                bank.filled(mm, key)

                m = M[l]
                G, UP, X0, X1, HT_, Y0, Y1 = (ps[i] for i in (2, 3, 4, 5, 6, 7, 0))

                def gather_T(item, u):
                    pe.wait_ge(m_xg[l][u], item)
                    for hf, X in enumerate((X0, X1)):
                        for c in range(4):
                            mm = pe.transpose(X[:, c * P:(c + 1) * P], xg[:, u, (4 * hf + c) * P:(4 * hf + c + 1) * P], ident)
                        mm.then_inc(m["xt"], 1)

                for key in ((l, "router"), (l, "place"), (l, "h2", T - 1, 0), (l, "h2", T - 1, 1), (l, "h2", T - 2, 0), (l, "h2", T - 2, 1)):
                    bank.wait_read(pe, key)
                for t in range(T):
                    bank.wait_read(pe, (l, "w", 0, t))
                    bank.wait_read(pe, (l, "w", 1, t))
                pe.wait_ge(s["ni"], 1)
                pairs = pe.value_load(ni[0:1, ITEMS:ITEMS + 1], min_val=NE // 2, max_val=ITEMS // 2)
                gather_T(16, 0)
                with pe.Fori(0, pairs) as q:
                    for u in range(2):
                        sg_, su_, sd_ = (MSLOT[3 * u + k] for k in range(3))
                        done = 2 * q + (u + 1)
                        pe.wait_ge(m["xtA"], done)
                        pe.wait_ge(m["xtD"], done)
                        for slot, B, free in ((sg_, G, "sig"), (su_, UP, "h")):
                            pe.wait_ge(m_in[l][slot], 16 * q + 16)
                            pe.wait_ge(m[free], done)
                            for k in range(KC):
                                mm = pe.matmul(B[:], xgT[:, u, k, :], slab[slot][:, k, :], start=k == 0, stop=k == KC - 1)
                            mm.then_inc(m["gu"], 1)
                        gather_T(16 * q + (16 if u == 0 else 32), 1 - u)
                        pe.wait_ge(m["h"], done + 1)
                        pe.wait_ge(m["htA"], done)
                        for c in range(4):
                            mm = pe.transpose(HT_[:, c * P:(c + 1) * P], hh[:, u, c * P:(c + 1) * P], ident)
                        mm.then_inc(m["ht"], 1)
                        pe.wait_ge(m["htA"], done + 1)
                        pe.wait_ge(m_in[l][sd_], 16 * q + 16)
                        wd = slab[sd_][:].rearrange("p (k j) n -> p k (j n)", k=4)
                        for hf, (Y, free) in enumerate(((Y0, "yA"), (Y1, "yD"))):
                            pe.wait_ge(m[free], done)
                            for c in range(4):
                                mm = pe.matmul(Y[:], hhT[:, u, c, :], wd[:, c, hf * HALF:(hf + 1) * HALF], start=c == 0, stop=c == 3)
                            mm.then_inc(m["y"], 1)

        @block.scalar
        def _(act):
            steps = [0]

            def step(ins):
                ins.then_inc(act_step, 1)
                steps[0] += 1
                act.wait_ge(act_step, steps[0])

            def copy_of(key, dst, src):
                bank.wait_full(act, key)
                bank.read(act.activation(dst, src, ACT.Copy), key)

            def pb(key):
                return ps[bank.at[key][0]]

            act.wait_ge(mod_full, 1)
            act.activation(csig[:], ps[7][:, 0:2 * KC], ACT.Sigmoid).then_inc(s_silu_c, 1)
            for l in range(DEPTH):
                with act.Fori(0, D_MOD // HALF // 4) as i:
                    for u in range(4):
                        act.wait_ge(mod_read, 4 * i + (12 * l + u + 5))
                        cols = bass.ds((4 * i + u) * HALF + l * D_MOD, HALF)
                        act.dma_start(mod_d[:, cols], mrow[0:2, u, :]).then_inc(mod_out[u], 16)

            for l in range(DEPTH):
                T, s, m = QT[l], S[l], M[l]

                def rms_rows(which, tiles):
                    for t in tiles:
                        ins = act.activation(junk[:], x_sb[:, t, :], ACT.Square, accum_out=ssum[:, 0, t:t + 1])
                        if t != tiles[-1]:
                            step(ins)
                    ins.then_inc(s["sq"], 1)
                    act.wait_ge(s["sqm"], which)
                    act.activation(ssum[:, 2, 0:len(tiles)], ssum[:, 1, 0:len(tiles)], ACT.Sqrt).then_inc(s["sqrt"], 1)

                if l == 0:
                    act.wait_ge(s_x, 32)
                else:
                    act.wait_ge(S[0]["xf"], NT)
                rms_rows(1, range(NT))
                for t in range(NT):
                    for hf in range(2):
                        key = (l, "h", t, hf)
                        copy_of(key, hT[:, 4 * hf:4 * hf + 4, t * P:(t + 1) * P], pb(key)[:].rearrange("p (c n) -> p c n", c=4))
                for t in range(T):
                    key = (l, "b2", t)
                    bank.wait_full(act, key)
                    if t >= 2:
                        bank.wait_read(act, (l, "b1", t - 2))
                    bank.read(act.activation(sgt[:, t % 2, :], pb(key)[:], ACT.Sigmoid), key)
                for t in range(NT):
                    copy_of((l, "b0", t), cqkv[:, t, :], pb((l, "b0", t))[:, 0:W_CQKV])
                act.wait_ge(s["csq"], 1)
                for t in range(NT):
                    bank.wait_read(act, (l, "b0", t))
                    if t < T:
                        act.activation(junk[:, 0:QR], cqkv[:, t, 0:QR], ACT.Square, accum_out=cstat[:, t, 0:1])
                    ins = act.activation(junk[:, QR:QR + KVR], cqkv[:, t, QR:QR + KVR], ACT.Square, accum_out=cstat[:, t, 1:2])
                    if t < NT - 1:
                        step(ins)
                ins.then_inc(s["csq"], 1)
                for t in range(NT):
                    copy_of((l, "b4", t), gkv[:, t, :], pb((l, "b4", t))[:, 0:2 * GKV * GD])
                act.wait_ge(s["pad"], 1)
                for c in range(4):
                    key = (l, "yT", c)
                    copy_of(key, ypad[:, c, 0:T // LT, CW // 2:CW // 2 + SEQ], pb(key)[:, 0:T * P].rearrange("p (s n) -> p s n", n=SEQ))
                for t in range(T):
                    copy_of((l, "b3", t), gq[:, t, :], pb((l, "b3", t))[:])
                act.wait_ge(s["csq"], 3)
                act.activation(cstat[:], cstat[:], ACT.Sqrt).then_inc(s["csq"], 1)
                for c in range(3):
                    n = (T if c < 2 else NT) * P
                    key = (l, "cT", c)
                    bank.wait_full(act, key)
                    bank.read(act.activation(cT[:, c, 0:n], pb(key)[:, 0:n], ACT.Identity, scale=colg[:, c:c + 1]), key)
                act.wait_ge(s["lnv"], 1)
                act.activation(mv[:, 0:T, 1:2], mv[:, 0:T, 1:2], ACT.Sqrt).then_inc(s["lns"], 1)
                for c in range(4):
                    key = (l, "zT", c)
                    bank.wait_full(act, key)
                    bank.read(act.activation(zT[:, c, 0:T * P], pb(key)[:, 0:T * P], ACT.Silu, scale=convc[:, c, CW + 1:CW + 2],
                                             bias=convc[:, c, CW + 2:CW + 3]), key)
                for t in range(T):
                    q2 = q_tm[:, t].rearrange("p h d -> p (h d)")
                    copy_of((l, "uq", t, 0), q2[:, 0:HALF], pb((l, "uq", t, 0))[:])
                    copy_of((l, "uq", t, 1), q2[:, HALF:H * QK], pb((l, "uq", t, 1))[:, 0:H * QK - HALF])
                for t in range(NT):
                    for hf in range(2):
                        key = (l, "ukv", t, hf)
                        kv = pb(key)[:].rearrange("p (h d) -> p h d", h=4)
                        bank.wait_full(act, key)
                        act.activation(kfull[:, t, 4 * hf:4 * hf + 4, 0:NOPE], kv[:, :, 0:NOPE], ACT.Copy)
                        bank.read(act.activation(v_tm[:, t, 4 * hf * VD:4 * (hf + 1) * VD].rearrange("p (h d) -> p h d", h=4), kv[:, :, NOPE:NOPE + VD], ACT.Copy), key)
                act.wait_ge(s["st"], 1)
                act.activation(stat[:], stat[:], ACT.Sqrt).then_inc(s["st"], 1)

                U = attn_units(l)
                for kind in ("mla", "gqa"):
                    d = QK if kind == "mla" else GD
                    kslot = (lambda h: h % 2) if kind == "mla" else (lambda h: h // 4)
                    scale = float(d) ** -0.5
                    for i, stage in attn_order(l, kind):
                        key = (l, kind, stage, i)
                        if stage == "head":
                            if kind == "mla" or i % 4 == 0:
                                key = (l, kind, "kT", i)
                                copy_of(key, headT[0:d, kslot(i), 1, :], pb(key)[0:d, :])
                            continue
                        h, t = U[i]
                        n = keys_of[t][1] - keys_of[t][0]
                        if stage == "s":
                            act.wait_ge(s["nmax"], (len(U) if kind == "gqa" else 0) + i + 1)
                            bank.wait_full(act, key)
                            if i >= 2:
                                bank.wait_full(act, (l, kind, "pT", i - 2))
                            bank.read(act.activation(prob[:, i % 2, 0:n * P], pb(key)[:, 0:n * P], ACT.Exp,
                                                     bias=nmax[:, i % 4:i % 4 + 1], scale=scale, accum_out=rsum[:, i % 4:i % 4 + 1]), key)
                        elif stage == "pT":
                            if i >= 2:
                                bank.wait_full(act, (l, kind, "pv", i - 2))
                            copy_of(key, probT[:, i % 2, 0:n, :], pb(key)[:, 0:n * P].rearrange("p (j q) -> p j q", q=P))
                    for c in range(4):
                        key = (l, kind, "oT", c)
                        dst = oT_mla if kind == "mla" else oT_gqa
                        copy_of(key, dst[:, c, 0:T * P], pb(key)[:, 0:T * P])

                i, used = 0, []
                for b in range(3):
                    for hf in range(2):
                        for t in range(T):
                            key = (l, "g", b, hf, t)
                            bank.wait_full(act, key)
                            if i >= 2:
                                bank.wait_read(act, used[i - 2])
                            used.append((l, "o", b, hf, t))
                            bank.read(act.activation(sgt[:, i % 2, :], pb(key)[:], ACT.Sigmoid), key)
                            i += 1
                for hf in range(2):
                    for t in range(T):
                        key = (l, "mT", t, hf)
                        copy_of(key, hT[:, 4 * hf:4 * hf + 4, t * P:(t + 1) * P], pb(key)[:].rearrange("p (c n) -> p c n", c=4))

                act.wait_ge(s["xm"], 2 * T)
                rms_rows(2, range(T))
                for t in range(T):
                    act.wait_ge(s["h2"], t + 1)
                    act.dma_start(h2_d[l][t * P:(t + 1) * P, :], htile[:, t % 2, :]).then_inc(s["h2o"], 16)
                    for hf in range(2):
                        key = (l, "h2", t, hf)
                        copy_of(key, hT[:, 4 * hf:4 * hf + 4, t * P:(t + 1) * P], pb(key)[:].rearrange("p (c n) -> p c n", c=4))
                key = (l, "router")
                bank.wait_full(act, key)
                bank.read(act.activation(r1[:, R_S, 0:T * NE], pb(key)[:, 0:T * NE], ACT.Sigmoid), key)

                X0, HT_, Y0 = ps[4], ps[6], ps[7]
                for name in ("sig", "htA", "yA"):
                    act.sem_inc(m[name], 1)
                for u in range(2):
                    act.sem_inc(m_yo[l][u], 16)
                act.wait_ge(s["ni"], 1)
                pairs = act.value_load(ni[0:1, ITEMS:ITEMS + 1], min_val=NE // 2, max_val=ITEMS // 2)
                act.wait_ge(m["xt"], 1)
                act.activation(xgT[:, 0, 0:4, :], X0[:].rearrange("p (c n) -> p c n", c=4), ACT.Copy).then_inc(m["xtA"], 1)
                with act.Fori(0, pairs) as q:
                    for u in range(2):
                        done = 2 * q + (u + 1)
                        act.wait_ge(m["gu"], 4 * q + (2 * u + 1))
                        act.wait_ge(m["h"], done)
                        act.activation(sg[:, u, :], ps[2][:], ACT.Silu).then_inc(m["sig"], 1)
                        act.wait_ge(m["xt"], 4 * q + (2 * u + 3))
                        act.activation(xgT[:, 1 - u, 0:4, :], X0[:].rearrange("p (c n) -> p c n", c=4), ACT.Copy).then_inc(m["xtA"], 1)
                        act.wait_ge(m["ht"], done)
                        act.activation(hhT[:, u], HT_[:].rearrange("p (c n) -> p c n", c=4), ACT.Copy).then_inc(m["htA"], 1)
                        act.wait_ge(m["y"], 4 * q + (2 * u + 1))
                        act.wait_ge(m_yo[l][u], 16 * q + 16)
                        act.activation(yg[:, u, 0:HALF], Y0[:], ACT.Copy).then_inc(m["yA"], 1)
            for t in range(LT):
                act.wait_ge(S[DEPTH - 1]["xf"], t + 1)
                act.dma_start(out[0, t * P:(t + 1) * P, :], x_sb[:, t, :]).then_inc(s_out, 16)
            act.wait_ge(s_out, 16 * LT)

        @block.vector
        def _(dve):
            steps = [0]

            def step(ins):
                ins.then_inc(dve_step, 1)
                steps[0] += 1
                dve.wait_ge(dve_step, steps[0])

            def pb(key):
                return ps[bank.at[key][0]]

            TT, TS, STT, RED = dve.tensor_tensor, dve.tensor_scalar, dve.scalar_tensor_tensor, dve.tensor_reduce

            dve.sem_inc(mod_read, 4)
            for u in range(4):
                dve.sem_inc(mod_out[u], 16)
            dve.memset(slab[4][:], 0.0)
            dve.memset(zero[:], 0).then_inc(s_zset, 1)
            dve.wait_ge(s_silu_c, 1)
            TT(sT[:], ps[7][:, 0:2 * KC], csig[:], ALU.mult).then_inc(s_silu_c, 1)
            for l in range(DEPTH):
                with dve.Fori(0, D_MOD // HALF // 4) as i:
                    for u in range(4):
                        dve.wait_ge(mod_full, 4 * i + (12 * l + u + 2))
                        dve.wait_ge(mod_in[u], 32 * i + 32 * (3 * l + 1))
                        dve.wait_ge(mod_out[u], 16 * i + 16 * (3 * l + 1))
                        TT(mrow[0:2, u, :], ps[u][0:2, :], mbias[0:2, u, :], ALU.add).then_inc(mod_read, 1)

            for l in range(DEPTH):
                T, s, m = QT[l], S[l], M[l]
                key = (l, "conv_cols")
                bank.wait_full(dve, key)
                bank.read(dve.tensor_copy(convc[:].rearrange("p c w -> p (c w)"), pb(key)[:, 0:4 * (CW + 3)]), key)

                def modulated(which, tiles, rows, n_rows, free):
                    dve.wait_ge(s["sq"], which)
                    TS(ssum[:, 1, 0:len(tiles)], ssum[:, 0, 0:len(tiles)], 1.0 / D, EPS, ALU.mult, ALU.add).then_inc(s["sqm"], 1)
                    dve.wait_ge(s[rows], n_rows)
                    for r in range(2 if len(tiles) > LT else 1):
                        ins = STT(out=rowA[:, r, :], in0=rowA[:, r, :], scalar=1.0, in1=normg[:], op0=ALU.add, op1=ALU.mult)
                    step(ins)
                    dve.wait_ge(s["sqrt"], which)
                    step(dve.reciprocal(ssum[:, 2, 0:len(tiles)], ssum[:, 2, 0:len(tiles)]))
                    for t in tiles:
                        free(t)
                        step(STT(out=htile[:, t % 2, :], in0=x_sb[:, t, :], scalar=ssum[:, 2, t:t + 1], in1=rowA[:, t // LT, :],
                                 op0=ALU.mult, op1=ALU.mult))
                        TT(htile[:, t % 2, :], htile[:, t % 2, :], rowB[:, t // LT, :], ALU.add).then_inc(s["h" if which == 1 else "h2"], 1)

                def free1(t):
                    if t >= 2:
                        bank.wait_full(dve, (l, "h", t - 2, 1))
                modulated(1, range(NT), "rows1", 16 * 5, free1)

                for t in range(T):
                    key = (l, "b1", t)
                    bank.wait_read(dve, (l, "b2", t))
                    bank.wait_full(dve, key)
                    bank.read(TT(ybuf[:, t, :], pb(key)[:], sgt[:, t % 2, :], ALU.mult), key)
                dve.memset(cstat[:], 1.0).then_inc(s["csq"], 1)
                dve.wait_ge(s["csq"], 2)
                TS(cstat[:, :, 0:1], cstat[:, :, 0:1], 1.0 / QR, EPS, ALU.mult, ALU.add)
                TS(cstat[:, :, 1:2], cstat[:, :, 1:2], 1.0 / KVR, EPS, ALU.mult, ALU.add).then_inc(s["csq"], 1)
                dve.wait_ge(s["csq"], 4)
                step(dve.reciprocal(cstat[:], cstat[:]))
                for t in range(NT):
                    if t < T:
                        TS(cqkv[:, t, 0:QR], cqkv[:, t, 0:QR], cstat[:, t, 0:1], None, ALU.mult)
                    ins = TS(cqkv[:, t, QR:QR + KVR], cqkv[:, t, QR:QR + KVR], cstat[:, t, 1:2], None, ALU.mult)
                ins.then_inc(s["cn"], 1)

                ns = T // LT
                for c in range(4):
                    bank.wait_read(dve, (l, "yT", c))
                    for w in range(CW):
                        src = ypad[:, c, 0:ns, w:w + SEQ]
                        acc = cv[:, c, 0:ns, :]
                        if w == 0:
                            step(TS(acc, src, convc[:, c, 0:1], convc[:, c, CW:CW + 1], ALU.mult, ALU.add))
                        else:
                            ins = STT(out=acc, in0=src, scalar=convc[:, c, w:w + 1], in1=acc, op0=ALU.mult, op1=ALU.add)
                            if w < CW - 1:
                                step(ins)
                            else:
                                ins.then_inc(s["cvd"], 1)
                for t in range(T):
                    bank.wait_full(dve, (l, "cvb", t))
                    ins = dve.bn_stats(bnst[:, t, 0:6], pb((l, "cvb", t))[:])
                step(ins)
                for t in range(T):
                    ins = dve.bn_aggr(mv[:, t, :], bnst[:, t, 0:6])
                step(ins)
                TS(mv[:, 0:T, 1:2], mv[:, 0:T, 1:2], EPS, None, ALU.add).then_inc(s["lnv"], 1)
                dve.wait_ge(s["lns"], 1)
                step(dve.reciprocal(mv[:, 0:T, 1:2], mv[:, 0:T, 1:2]))
                for t in range(T):
                    key = (l, "cvb", t)
                    bank.read(TS(ybuf[:, t, :], pb(key)[:], mv[:, t, 0:1], mv[:, t, 1:2], ALU.subtract, ALU.mult), key)

                def kv_parts(t):
                    parts = [(kfull[:, t, :, 0:NOPE], 8, 16, QK, NOPE), (gkv[:, t, 0:GKV * GD].rearrange("p (h d) -> p h d", d=GD), 24, 26, 2 * QK + GD, GD),
                             (cqkv[:, t, QR + KVR:W_CQKV].rearrange("p (h d) -> p h d", d=ROPE), 34, 35, QK + NOPE, ROPE)]
                    if t < T:
                        parts += [(q_tm[:, t, :, 0:NOPE], 0, 8, 0, NOPE), (q_tm[:, t, :, NOPE:QK], 26, 34, NOPE, ROPE),
                                  (gq[:, t, :].rearrange("p (h d) -> p h d", d=GD), 16, 24, 2 * QK, GD)]
                    return parts
                step(dve.memset(stat[:], 1.0))
                n = 0
                for t in range(NT):
                    bank.wait_read(dve, (l, "ukv", t, 0))
                    bank.wait_read(dve, (l, "ukv", t, 1))
                    if t < T:
                        bank.wait_read(dve, (l, "uq", t, 0))
                        bank.wait_read(dve, (l, "uq", t, 1))
                        bank.wait_read(dve, (l, "b3", t))
                    bank.wait_read(dve, (l, "b4", t))
                    for x, c0, c1, g, d in kv_parts(t):
                        hs = c1 - c0
                        sq = tmp3[:, (n % 2) * HALF:(n % 2) * HALF + hs * d].rearrange("p (h d) -> p h d", d=d)
                        n += 1
                        step(TT(sq, x, x, ALU.mult))
                        ins = RED(stat[:, t, c0:c1], sq, AX, ALU.add)
                step(ins)
                TS(stat[:, :, 0:26], stat[:, :, 0:26], 1.0 / NOPE, EPS, ALU.mult, ALU.add)
                TS(stat[:, :, 26:35], stat[:, :, 26:35], 1.0 / ROPE, EPS, ALU.mult, ALU.add).then_inc(s["st"], 1)
                dve.wait_ge(s["st"], 2)
                step(dve.reciprocal(stat[:], stat[:]))
                dve.wait_ge(s["par"], 16 * 11)
                for t in range(NT):
                    for x, c0, c1, g, d in kv_parts(t):
                        hs = c1 - c0
                        out_ = kpe[:, t, :].rearrange("p (h d) -> p h d", d=ROPE) if d == ROPE and hs == 1 else x
                        ins = TT(out_, x, stat[:, t, c0:c1].unsqueeze(2).to_broadcast([P, hs, d]), ALU.mult)
                    step(ins)
                    for x, c0, c1, g, d in kv_parts(t):
                        hs = c1 - c0
                        out_ = kpe[:, t, :].rearrange("p (h d) -> p h d", d=ROPE) if d == ROPE and hs == 1 else x
                        ins = TT(out_, out_, qkg[:, g:g + d].unsqueeze(1).to_broadcast([P, hs, d]), ALU.mult)
                    step(ins)
                    if t < LT:
                        r0 = C_ROPE + t * ROPEW
                        for x, hs, f, c0 in ((q_tm[:, t, :, NOPE:QK], H, 8, 0), (kpe[:, t, :].rearrange("p (h d) -> p h d", d=ROPE), 1, 8, 0),
                                             (gq[:, t, :].rearrange("p (h d) -> p h d", d=GD), GH, 16, 32),
                                             (gkv[:, t, 0:GKV * GD].rearrange("p (h d) -> p h d", d=GD), GKV, 16, 32)):
                            v = x.rearrange("p h (a b f) -> p h a b f", a=2, b=2)
                            x1, x2 = v[:, :, :, 0, :], v[:, :, :, 1, :]
                            cs, sn = (cst[:, r0 + c0 + k * 2 * f:r0 + c0 + (k + 1) * 2 * f].rearrange("p (a f) -> p a f", f=f).unsqueeze(1)
                                      .to_broadcast([P, hs, 2, f]) for k in range(2))
                            tt = [ropt[:, k, 0:hs * 2 * f].rearrange("p (h a f) -> p h a f", a=2, f=f) for k in range(4)]
                            TT(tt[0], x1, cs, ALU.mult)
                            TT(tt[1], x2, sn, ALU.mult)
                            TT(tt[2], x2, cs, ALU.mult)
                            step(TT(tt[3], x1, sn, ALU.mult))
                            TT(x1, tt[0], tt[1], ALU.subtract)
                            step(TT(x2, tt[2], tt[3], ALU.add))
                    ins = dve.tensor_copy(kfull[:, t, :, NOPE:QK], kpe[:, t, :].unsqueeze(1).to_broadcast([P, H, ROPE]))
                ins.then_inc(s["nrm"], 1)

                U = attn_units(l)
                for kind in ("mla", "gqa"):
                    d = QK if kind == "mla" else GD
                    for i, stage in attn_order(l, kind):
                        key = (l, kind, stage, i)
                        if stage == "head":
                            key = (l, kind, "qT", i)
                            bank.wait_full(dve, key)
                            bank.read(dve.tensor_copy(headT[0:d, i % 2, 0, 0:T * P], pb(key)[0:d, 0:T * P]), key)
                            continue
                        h, t = U[i]
                        n = keys_of[t][1] - keys_of[t][0]
                        if stage == "s":
                            bank.wait_full(dve, key)
                            step(dve.reduce_max(mxs[:, i % 4:i % 4 + 1], pb(key)[:, 0:n * P], AX))
                            TS(nmax[:, i % 4:i % 4 + 1], mxs[:, i % 4:i % 4 + 1], -float(d) ** -0.5, None, ALU.mult).then_inc(s["nmax"], 1)
                        elif stage == "pv":
                            bank.wait_read(dve, (l, kind, "s", i))
                            step(dve.reciprocal(rinv[:, i % 4:i % 4 + 1], rsum[:, i % 4:i % 4 + 1]))
                            bank.wait_full(dve, key)
                            if kind == "gqa" and i == 0:
                                bank.wait_full(dve, (l, "mla", "oT", 3))
                            bank.read(TS(o_tm[:, t, h * VD:(h + 1) * VD], pb(key)[:, 0:VD], rinv[:, i % 4:i % 4 + 1], None, ALU.mult), key)

                i = 0
                for b in range(3):
                    for hf in range(2):
                        for t in range(T):
                            key = (l, "o", b, hf, t)
                            bank.wait_full(dve, key)
                            bank.wait_read(dve, (l, "g", b, hf, t))
                            dst = merged[:, t, hf * HALF:(hf + 1) * HALF]
                            if b == 0:
                                bank.read(TT(dst, pb(key)[:], sgt[:, i % 2, :], ALU.mult), key)
                            else:
                                bank.read(TT(tmp[:], pb(key)[:], sgt[:, i % 2, :], ALU.mult), key)
                                bank.wait_read(dve, key)
                                ins = TT(dst, dst, tmp[:], ALU.add)
                                if b == 2:
                                    ins.then_inc(s["mg"], 1)
                                    dve.wait_ge(s["mg"], hf * T + t + 1)
                                else:
                                    step(ins)
                            i += 1
                dve.wait_ge(s["rows2"], 32)
                for hf in range(2):
                    for t in range(T):
                        key = (l, "w", hf, t)
                        bank.wait_full(dve, key)
                        cols = slice(hf * HALF, (hf + 1) * HALF)
                        bank.read(TT(tmp[:], pb(key)[:], rowA[:, t // LT, cols], ALU.mult), key)
                        bank.wait_read(dve, key)
                        ins = TT(x_sb[:, t, cols], x_sb[:, t, cols], tmp[:], ALU.add)
                        ins.then_inc(s["xm"], 1)
                        dve.wait_ge(s["xm"], hf * T + t + 1)

                def free2(t):
                    if t >= 2:
                        bank.wait_full(dve, (l, "h2", t - 2, 1))
                        dve.wait_ge(s["h2o"], 32)
                modulated(2, range(T), "rows3", 16 * (3 if T <= LT else 5), free2)

                dve.wait_ge(s["rcst"], 16)
                key = (l, "router")
                bank.wait_read(dve, key)
                slots = [2]
                W = T * NE

                def r(n_=1):
                    k = slots[0]
                    slots[0] += n_
                    return r1[:, k:k + n_, :].rearrange("p k n -> p (k n)")

                def te(x, k=T):
                    return x[:, 0:k * NE].rearrange("p (t e) -> p t e", e=NE)

                def bc(x, n_, w_):
                    return x[:, 0:n_].unsqueeze(2).to_broadcast([P, n_, w_])

                sc = r1[:, R_S, :]
                sel = r()
                dve.tensor_copy(toku[:, 0:NT], rcst[:, R_TOK:R_TOK + NT])
                step(TT(te(sel), te(sc), qkg[:, 2 * QK + 2 * GD:2 * QK + 2 * GD + NE].unsqueeze(1).to_broadcast([P, T, NE]), ALU.add))
                G4 = T * NG
                sp_ = sel[:, 0:W].rearrange("p (g q) -> p g q", q=2)
                mx, mn, a1, a2, a3, a4, gs, gm, k1, k2 = (r() for _ in range(10))
                pr = lambda x: x[:, 0:2 * G4].rearrange("p (g q) -> p g q", q=2)
                TT(mx[:, 0:2 * G4].unsqueeze(2), sp_[:, :, 0:1], sp_[:, :, 1:2], ALU.max)
                step(TT(mn[:, 0:2 * G4].unsqueeze(2), sp_[:, :, 0:1], sp_[:, :, 1:2], ALU.min))
                TT(a1[:, 0:G4].unsqueeze(2), pr(mx)[:, :, 0:1], pr(mx)[:, :, 1:2], ALU.max)
                TT(a2[:, 0:G4].unsqueeze(2), pr(mx)[:, :, 0:1], pr(mx)[:, :, 1:2], ALU.min)
                step(TT(a3[:, 0:G4].unsqueeze(2), pr(mn)[:, :, 0:1], pr(mn)[:, :, 1:2], ALU.max))
                step(TT(a4[:, 0:G4], a2[:, 0:G4], a3[:, 0:G4], ALU.max))
                step(TT(gs[:, 0:G4], a1[:, 0:G4], a4[:, 0:G4], ALU.add))

                def first_largest(out_, x, n_, w_, rev):
                    v = lambda y: y[:, 0:n_ * w_].rearrange("p (n w) -> p n w", w=w_)
                    step(RED(k1[:, 0:n_], v(x), AX, ALU.max))
                    step(TT(v(k2), v(x), bc(k1, n_, w_), ALU.is_equal))
                    step(TT(v(k2), v(k2), rcst[:, rev:rev + w_].unsqueeze(1).to_broadcast([P, n_, w_]), ALU.mult))
                    step(RED(k1[:, 0:n_], v(k2), AX, ALU.max))
                    step(TT(v(out_), v(k2), bc(k1, n_, w_), ALU.is_equal))

                first_largest(gm, gs, T, NG, R_GREV)
                pen = a1
                BIG = 1e30
                grp = lambda x: x[:, 0:W].rearrange("p (g q) -> p g q", q=EG)
                TS(pen[:, 0:G4], gm[:, 0:G4], BIG, -BIG, ALU.mult, ALU.add)
                inside = r()
                step(TT(grp(inside), grp(sel), bc(gm, G4, EG), ALU.mult))
                step(TT(grp(inside), grp(inside), bc(pen, G4, EG), ALU.add))
                oh = r1[:, slots[0]:slots[0] + 2, 0:W]
                o1, o2 = r(), r()
                first_largest(o1, inside, T, NE, R_REV)
                second = r()
                step(STT(out=second[:, 0:W], in0=o1[:, 0:W], scalar=-2 * BIG, in1=inside[:, 0:W], op0=ALU.mult, op1=ALU.add))
                first_largest(o2, second, T, NE, R_REV)
                mask = r1[:, R_MASK, :]
                TT(mask[:, 0:W], o1[:, 0:W], o2[:, 0:W], ALU.add).then_inc(s["mask"], 1)
                oh4 = oh.rearrange("p k (t e) -> p k t e", e=NE)
                prod = r(2)
                p4 = prod[:, 0:2 * NT * NE].rearrange("p (k n) -> p k n", k=2)[:, :, 0:W].rearrange("p k (t e) -> p k t e", e=NE)
                res = r()

                def picked(row, table):
                    for k in range(2):
                        ins = TT(p4[:, k], oh4[:, k], table, ALU.mult)
                    step(ins)
                    for k in range(2):
                        ins = RED(res[:, row * 8 + k * T:row * 8 + (k + 1) * T], p4[:, k], AX, ALU.add)
                    step(ins)
                    return res[:, row * 8:row * 8 + 2 * T]

                w_ = picked(0, te(sc))
                den = res[:, 8:8 + T]
                step(TT(den, w_[:, 0:T], w_[:, T:2 * T], ALU.add))
                step(dve.reciprocal(den, den))
                for k in range(2):
                    TT(wk[:, k, 0:T], w_[:, k * T:(k + 1) * T], den, ALU.mult)
                key = (l, "place")
                pos, cnt = r(), r()
                bank.wait_full(dve, key)
                dve.tensor_copy(pos[:, 0:W], pb(key)[:, 0:W])
                bank.read(dve.tensor_copy(cnt[:, 0:NE], pb(key)[:, NT * NE:(NT + 1) * NE]), key)
                bank.wait_read(dve, key)
                over = cnt[:, NE:2 * NE]
                step(TS(over, cnt[:, 0:NE], float(P), None, ALU.is_gt))
                step(STT(out=over, in0=cnt[:, 0:NE], scalar=float(2 * P), in1=over, op0=ALU.is_gt, op1=ALU.add))
                step(STT(out=over, in0=cnt[:, 0:NE], scalar=float(3 * P), in1=over, op0=ALU.is_gt, op1=ALU.add))
                big = r(4)
                b3 = big[:, 0:NE * NE].rearrange("p (e f) -> p e f", f=NE)
                ob, incl = cnt[:, 2 * NE:3 * NE], cnt[:, 3 * NE:4 * NE]
                step(TT(b3, rcst[:, R_LT:R_LT + NE * NE].rearrange("p (e f) -> p e f", f=NE), over.unsqueeze(1).to_broadcast([P, NE, NE]), ALU.mult))
                step(RED(ob, b3, AX, ALU.add))
                step(TT(incl, ob, over, ALU.add))
                V = incl[:, NE - 1:NE]
                fl = r()
                npair = fl[:, 0:1]
                step(TS(npair, V, 1.0, float(NE // 2), ALU.is_ge, ALU.add))
                for x in (3.0, 5.0, 7.0):
                    step(STT(out=npair, in0=V, scalar=x, in1=npair, op0=ALU.is_ge, op1=ALU.add))
                i3 = big[:, 0:8 * NE].rearrange("p (e f) -> p e f", f=NE)
                step(TT(i3, incl.unsqueeze(1).to_broadcast([P, 8, NE]), rcst[:, R_IT:R_IT + 8].unsqueeze(2).to_broadcast([P, 8, NE]), ALU.is_le))
                step(RED(fl[:, 8:16], i3, AX, ALU.add))
                TS(ni[:, NE:ITEMS], fl[:, 8:16], float(NE - 1), None, ALU.min)
                dve.tensor_copy(ni[:, 0:NE], rcst[:, R_EID:R_EID + NE])
                TS(ni[:, ITEMS + 2:ITEMS + 3], npair, 4.0, -2.0, ALU.mult, ALU.add)
                TS(ni[:, ITEMS + 3:ITEMS + 4], npair, 4.0, 2.0, ALU.mult, ALU.add)
                TS(ni[:, ITEMS + 1:ITEMS + 2], npair, 16.0, 16.0, ALU.mult, ALU.add)
                dve.tensor_copy(ni[:, ITEMS:ITEMS + 1], npair).then_inc(s["ni"], 1)
                p_ = picked(1, te(pos))
                e_ = picked(2, rcst[:, R_EID:R_EID + NE].unsqueeze(1).to_broadcast([P, T, NE]))
                b_ = picked(3, ob.unsqueeze(1).to_broadcast([P, T, NE]))
                gt, j_, it, sl = (res[:, 8 * k:8 * k + 2 * T] for k in (4, 5, 6, 7))
                step(TS(gt, p_, float(P), None, ALU.is_ge))
                step(STT(out=j_, in0=p_, scalar=float(2 * P), in1=gt, op0=ALU.is_ge, op1=ALU.add))
                step(STT(out=j_, in0=p_, scalar=float(3 * P), in1=j_, op0=ALU.is_ge, op1=ALU.add))
                step(STT(out=it, in0=j_, scalar=float(NE - 1), in1=b_, op0=ALU.add, op1=ALU.add))
                step(TT(it, it, e_, ALU.subtract))
                step(TT(it, it, gt, ALU.mult))
                step(TT(it, it, e_, ALU.add))
                step(STT(out=sl, in0=j_, scalar=-float(P), in1=p_, op0=ALU.mult, op1=ALU.add))
                for k in range(2):
                    cols = slice(k * T, (k + 1) * T)
                    STT(out=rowY[:, k, 0:T], in0=it[:, cols], scalar=float(P), in1=sl[:, cols], op0=ALU.mult, op1=ALU.add)
                    ins = STT(out=rowL[:, k, 0:T], in0=sl[:, cols], scalar=float(LISTW), in1=it[:, cols], op0=ALU.mult, op1=ALU.add)
                ins.then_inc(s["mask"], 1)

                UP, X1, Y1 = ps[3], ps[5], ps[0]
                for name in ("h", "yD"):
                    dve.sem_inc(m[name], 1)
                pairs = dve.value_load(ni[0:1, ITEMS:ITEMS + 1], min_val=NE // 2, max_val=ITEMS // 2)
                dve.wait_ge(m["xt"], 2)
                dve.tensor_copy(xgT[:, 0, 4:8, :], X1[:].rearrange("p (c n) -> p c n", c=4)).then_inc(m["xtD"], 1)
                with dve.Fori(0, pairs) as q:
                    for u in range(2):
                        done = 2 * q + (u + 1)
                        dve.wait_ge(m["gu"], 4 * q + (2 * u + 2))
                        dve.wait_ge(m["sig"], done + 1)
                        TT(hh[:, u, :], UP[:], sg[:, u, :], ALU.mult).then_inc(m["h"], 1)
                        dve.wait_ge(m["xt"], 4 * q + (2 * u + 4))
                        dve.tensor_copy(xgT[:, 1 - u, 4:8, :], X1[:].rearrange("p (c n) -> p c n", c=4)).then_inc(m["xtD"], 1)
                        dve.wait_ge(m["y"], 4 * q + (2 * u + 2))
                        dve.wait_ge(m_yo[l][u], 16 * q + 16)
                        dve.tensor_copy(yg[:, u, HALF:D], Y1[:]).then_inc(m["yD"], 1)

                dve.wait_ge(s["rows4"], 16 * (T // LT))
                for t in range(T):
                    u = t % 2
                    dve.wait_ge(m_yk[u], 32 * (l * NT // 2 + t // 2 + 1))
                    TS(xg[:, u, :], xg[:, u, :], wk[:, 0, t:t + 1], None, ALU.mult)
                    step(TS(yg[:, u, :], yg[:, u, :], wk[:, 1, t:t + 1], None, ALU.mult))
                    step(TT(yg[:, u, :], yg[:, u, :], xg[:, u, :], ALU.add))
                    step(TT(yg[:, u, :], yg[:, u, :], rowA[:, t // LT, :], ALU.mult))
                    TT(x_sb[:, t, :], x_sb[:, t, :], yg[:, u, :], ALU.add).then_inc(s["xf"], 1)

        @block.gpsimd
        def _(pool):
            pool.wait_ge(s_zset, 1)
            for l in range(DEPTH):
                pool.dma_start(list_d[l].rearrange("(p w) o -> p (w o)", p=P), zero[:]).then_inc(s_zero, 16)
                for h in range(2):
                    rows = y_d[l][(NE + 4 * h) * P:(NE + 4 * h + 4) * P, :]
                    pool.dma_start(rows.rearrange("(i p) d -> p i d", p=P), slab[4][:].rearrange("p (i j) n -> p i (j n)", i=4)).then_inc(s_zero, 16)
            pool.wait_ge(s_zero, 16 * 6)

            def spread(dst, row, done):
                pool.dma_start(dst, row.to_broadcast([P, row.shape[-1]])).then_inc(done, 16)

            for l in range(DEPTH):
                T, s, m = QT[l], S[l], M[l]

                def mod_row(which, r):
                    return mod_d[r:r + 1, l * D_MOD + which * D:l * D_MOD + (which + 1) * D]
                if l:
                    pool.wait_ge(S[l - 1]["xf"], NT)
                par = s["par"]
                pool.dma_start(crows[0:CW, :], a["conv_w"][l]).then_inc(par, 16)
                for k, name in enumerate(("conv_b", "conv_ln_g", "conv_ln_b")):
                    pool.dma_start(crows[CW + k:CW + k + 1, :], a[name][l:l + 1, :]).then_inc(par, 16)
                spread(qkg[:, 0:QK], a["mla_q_gain"][l:l + 1, :], par)
                spread(qkg[:, QK:2 * QK], a["mla_k_gain"][l:l + 1, :], par)
                spread(qkg[:, 2 * QK:2 * QK + GD], a["gqa_q_gain"][l:l + 1, :], par)
                spread(qkg[:, 2 * QK + GD:2 * QK + 2 * GD], a["gqa_k_gain"][l:l + 1, :], par)
                spread(qkg[:, 2 * QK + 2 * GD:], a["router_bias"].rearrange("(o e) -> o e", o=1), par)
                pool.dma_start(colg[:, 0:2].rearrange("p (k o) -> p k o", o=1), a["mla_q_norm"][l].rearrange("(k p o) -> p k o", p=P, o=1),
                               allow_slow_non_contiguous=True).then_inc(par, 16)
                pool.dma_start(colg[:, 2:3], a["mla_kv_norm"][l].rearrange("(p o) -> p o", o=1)).then_inc(par, 16)
                if l == 0:
                    pool.dma_start(rw[:], a["router_w"].rearrange("(k p) e -> p k e", p=P)).then_inc(s_zero, 16)
                    for u in range(4):
                        pool.wait_ge(mod_out[u], 16 * (DEPTH * 3 + 1))
                spread(normg[:], a["norm1_g"][l:l + 1, :], s["rows1"])
                for r in range(2):
                    spread(rowB[:, r, :], mod_row(0, r), s["rows1"])
                    spread(rowA[:, r, :], mod_row(1, r), s["rows1"])
                bank.wait_full(pool, (l, "conv_cols"))
                pool.memset(ypad[:], 0.0).then_inc(s["pad"], 1)
                pool.wait_ge(s["h"], NT)
                for r in range(2):
                    spread(rowA[:, r, :], mod_row(2, r), s["rows2"])
                n = T // LT
                bank.wait_full(pool, (l, "mla", "oT", 0))
                for r in range(n):
                    spread(rowB[:, r, :], mod_row(3, r), s["rows3"])
                spread(normg[:], a["norm2_g"][l:l + 1, :], s["rows3"])
                pool.wait_ge(s["xm"], 2 * T)
                pool.dma_start(rcst[:], consts[:, C_ALL:C_ALL + R_ALL]).then_inc(s["rcst"], 16)
                for r in range(n):
                    spread(rowA[:, r, :], mod_row(4, r), s["rows3"])
                pool.wait_ge(s["h2"], T)
                for r in range(n):
                    spread(rowA[:, r, :], mod_row(5, r), s["rows4"])
                pool.wait_ge(s["mask"], 2)
                pool.wait_ge(s_zero, 16 * 7)
                for t in range(T):
                    for k in range(2):
                        pool.indirect_dma_start(list_d[l], bass.IndirectOffsetOnAxis(ap=rowL[:, k, t:t + 1], axis=0), toku[:, t:t + 1], None).then_inc(s["scat"], 16)
                pool.wait_ge(s["scat"], 32 * T)
                pool.wait_ge(s["h2o"], 16 * T)
                pool.dma_start(lst[:], list_d[l].rearrange("(p w) o -> p (w o)", p=P)).then_inc(s["scat"], 16)
                pool.wait_ge(s["scat"], 32 * T + 16)
                pool.wait_ge(s["ni"], 1)
                pairs = pool.value_load(ni[0:1, ITEMS:ITEMS + 1], min_val=NE // 2, max_val=ITEMS // 2)
                stored = pool.value_load(ni[0:1, ITEMS + 1:ITEMS + 2], min_val=16, max_val=16 * ITEMS)

                def gather(u):
                    pool.indirect_dma_start(xg[:, u, :], None, h2_d[l], bass.IndirectOffsetOnAxis(ap=cur[:, u, 0:1], axis=0)).then_inc(m_xg[l][u], 16)

                def take(u, col):
                    return pool.tensor_copy(cur[:, u, 0:1], lst[:, col])
                for u in range(2):
                    take(u, slice(u, u + 1)).then_inc(m["cur"], 1)
                pool.wait_ge(m["cur"], 2)
                for u in range(2):
                    gather(u)
                with pool.Fori(4, 2 * pairs + 2, 2) as i:
                    pool.wait_ge(m["xt"], 2 * i - 4)
                    for u in range(2):
                        take(u, bass.ds(i - 2 + u, 1)).then_inc(m["cur"], 1)
                    for u in range(2):
                        pool.wait_ge(s["ni"], 1)
                        pool.wait_ge(m["cur"], i)
                        gather(u)
                before_last = pool.value_load(ni[0:1, ITEMS + 2:ITEMS + 3], min_val=1, max_val=4 * ITEMS)
                pool.wait_ge(s["ni"], 1)
                pool.wait_ge(m["xt"], before_last)
                gather(0)
                all_xt = pool.value_load(ni[0:1, ITEMS + 3:ITEMS + 4], min_val=1, max_val=4 * ITEMS)
                for t in range(T):
                    u = t % 2
                    pool.wait_ge(s["ni"], 1)
                    if t == 0:
                        for v in range(2):
                            pool.wait_ge(m_yo[l][v], stored)
                        pool.wait_ge(m["xt"], all_xt)
                    if t >= 2:
                        pool.wait_ge(s["xf"], t - 1)
                    for k, dst in ((0, xg), (1, yg)):
                        pool.indirect_dma_start(dst[:, u, :], None, y_d[l], bass.IndirectOffsetOnAxis(ap=rowY[:, k, t:t + 1], axis=0)).then_inc(m_yk[u], 16)


_INS = ["x", "c", "ctx", "c_ctx", "w_mod", "b_mod", "norm1_g", "norm2_g", "w_in", "mla_q_norm", "mla_kv_norm", "mla_w_uq",
        "mla_w_ukv", "mla_q_gain", "mla_k_gain", "mla_w_o", "conv_w", "conv_b", "conv_ln_g", "conv_ln_b", "conv_w_o",
        "gqa_q_gain", "gqa_k_gain", "gqa_w_o", "w_out", "router_w", "router_bias", "moe_w_gate", "moe_w_up", "moe_w_down"]


def constants():
    import numpy as np

    f = np.float32
    t = np.zeros((P, C_ALL + R_ALL), f)
    t[:, C_ID:C_ID + P] = np.eye(P, dtype=f)
    n = np.arange(SEQ)
    for tile in range(LT):
        rows = slice(tile * P, (tile + 1) * P)
        at = C_ROPE + tile * ROPEW
        for dim in (ROPE // 2, GD // 2):
            inv = (f(10000.0) ** (-np.arange(0, dim, 2, dtype=f) / f(dim))).astype(f)
            ang = np.concatenate([pos[:, None].astype(f) * inv[None, :] for pos in (n // GRID_W, n % GRID_W)], axis=1)
            for fn in (np.cos, np.sin):
                t[:, at:at + dim] = fn(ang[rows]).astype(f)
                at += dim
    r = t[:, C_ALL:]
    r[:, R_TRI:R_TRI + P] = np.triu(np.ones((P, P), f), 1)
    r[:, R_ONES:R_ONES + P] = 1
    r[:, R_TOK:R_TOK + NT] = np.arange(P)[:, None] + P * np.arange(NT)[None, :]
    r[:, R_EID:R_EID + NE] = np.arange(NE)
    r[:, R_REV:R_REV + NE] = NE - np.arange(NE)
    r[:, R_GREV:R_GREV + NG] = NG - np.arange(NG)
    r[:, R_IT:R_IT + 8] = np.arange(8)
    r[:, R_LT:R_LT + NE * NE] = np.tril(np.ones((NE, NE), f), -1).reshape(-1)
    return t


def kernel(**inputs):
    import numpy as _np
    import concourse.bacc as _bacc
    from concourse.bass_utils import run_bass_kernel_spmd as _run

    nc = _bacc.Bacc("TRN2", target_bir_lowering=False, num_devices=1)
    arrays, aps = {}, {}
    for name in _INS:
        v = _np.ascontiguousarray(inputs[name])
        arrays[f"in_{name}"] = v
        aps[name] = nc.dram_tensor(f"in_{name}", v.shape, mybir.dt.from_np(v.dtype), kind="ExternalInput").ap()
    v = constants()
    arrays["constants"] = v
    consts = nc.dram_tensor("constants", v.shape, F32, kind="ExternalInput").ap()
    out = nc.dram_tensor("out", (1, SEQ, D), F32, kind="ExternalOutput").ap()
    backbone(nc, aps, consts, out)
    return _run(nc, [arrays], core_ids=[0]).results[0]["out"]
```

```python
from contextlib import ExitStack

import concourse.bass as bass
from concourse import mybir

P = 128
D, SEQ, CTX, DEPTH = 1024, 256, 256, 2
LT, CT = SEQ // P, CTX // P
NT = LT + CT
KC = D // P
D_MOD = 6 * D
QR, KVR, ROPE, NOPE, VD, H = 256, 128, 32, 64, 64, 8
QK = NOPE + ROPE
CC, CW = 512, 31
GH, GKV, GD = 8, 2, 64
NE, NG, EG, F = 16, 4, 4, 512
GRID_W = 64
EPS = 1e-6
HALF = 512
COL_CQ, COL_CONV, COL_GQ = 0, QR + KVR + ROPE, QR + KVR + ROPE + 2 * CC
COL_GK = COL_GQ + GH * GD
COL_GATE = COL_GK + 2 * GKV * GD
D_IN = COL_GATE + 3 * D
W_CQKV = QR + KVR + ROPE
ITEMS = 24
LISTW = ITEMS + 2
PADW = SEQ + CW - 1

ZEROED = 16 * 11
HEAD_A = GH + GKV + 1

F32 = mybir.dt.float32
I32 = mybir.dt.int32
U32 = mybir.dt.uint32
ALU = mybir.AluOpType
ACT = mybir.ActivationFunctionType
AX = mybir.AxisListType.X

C_ID, C_ROPE = 0, 128
ROPEW = 2 * (2 * 8) + 2 * (2 * 16)
C_ALL = C_ROPE + LT * ROPEW
R_S, R_MASK = 0, 1
R_TRI, R_ONES, R_TOK, R_EID, R_REV, R_GREV, R_IT, R_LT = 0, 128, 256, 260, 276, 292, 296, 304
R_ALL = R_LT + NE * NE


MODB, MODG = D_MOD // HALF, D_MOD // HALF // 4
MODSLOT = (1, 2, 3, 0)
MERGE = (2, 0)
MSLOT = (4, 5, 1, 2, 3, 0)


class Banks:

    def __init__(self, full, free):
        self.full, self.free = full, free
        self.uses = [0] * len(full)
        self.turn = {}
        self.at = {}

    def plan(self, key, banks):
        n = self.turn.get(banks, 0)
        self.turn[banks] = n + 1
        b = banks[n % len(banks)]
        self.at[key] = (b, self.uses[b])
        self.uses[b] += 1

    def wait_free(self, eng, key):
        b, k = self.at[key]
        if k:
            eng.wait_ge(self.free[b], k)

    def wait_full(self, eng, key):
        b, k = self.at[key]
        eng.wait_ge(self.full[b], k + 1)

    def wait_read(self, eng, key):
        b, k = self.at[key]
        eng.wait_ge(self.free[b], k + 1)

    def filled(self, ins, key):
        ins.then_inc(self.full[self.at[key][0]], 1)

    def read(self, ins, key):
        ins.then_inc(self.free[self.at[key][0]], 1)


def backbone(nc, a, consts, out):
    with ExitStack() as ctx:
        sem = lambda n: ctx.enter_context(nc.semaphore(n))
        ps = [ctx.enter_context(nc.psum_tensor(f"bank{i}", [P, HALF], F32)) for i in range(8)]
        base = (nc.sbuf_base + 63) // 64 * 64

        def sb(name, at, shape, dt=F32):
            return nc.alloc_sbuf_tensor_at(name, [P, *shape], dt, offset=base + 4 * at)

        slab = [sb(f"slab{s}", 4096 * s, [8, HALF]) for s in range(6)]
        o = 16384
        ybuf = sb("ybuf", o, [NT, CC])
        ypad = sb("ypad", o + 2048, [4, 2, PADW])
        cv = sb("cv", o + 2048 + 8 * PADW, [4, 2, SEQ])
        q_tm = sb("q_tm", o, [NT, H, QK])
        kfull = sb("kfull", o + 3072, [NT, H, QK])
        o += 2048 + 8 * PADW + 2048
        v_tm = sb("v_tm", o, [NT, H * VD])
        oT_mla = sb("oT_mla", o, [4, NT * P])
        o += 2048
        x_sb = sb("x_sb", o, [NT, D]); o += 4096
        hT = sb("hT", o, [KC, NT * P]); o += 4096
        rowA = sb("rowA", o, [2, D])
        rowB = sb("rowB", o + 2048, [2, D])
        merged = sb("merged", o, [NT, D]); o += 4096
        m0 = o
        cqkv = sb("cqkv", o, [NT, W_CQKV])
        normg = sb("normg", o, [D]); o += 4 * W_CQKV
        gkv = sb("gkv", o, [NT, 2 * GKV * GD]); o += 1024
        gq = sb("gq", o, [NT, GH * GD])
        oT_gqa = sb("oT_gqa", o, [4, NT * P]); o += 2048
        zT = sb("zT", o, [4, NT * P]); o += 2048
        o_tm = sb("o_tm", o, [NT, H * VD])
        rowG = sb("rowG", o, [2, D]); o += 2048
        headT = sb("headT", o, [2, 2, NT * P])
        htile = sb("htile", o, [2, D]); o += 2048
        prob = sb("prob", o, [2, HALF])
        probT = sb("probT", o + 1024, [2, 4, P])
        cT = sb("cT", o, [3, NT * P])
        junk = sb("junk", o, [D]); o += 2048
        sgt = sb("sgt", o, [2, HALF])
        tmp = sb("tmp", o + 1024, [HALF])
        tmp3 = sb("tmp3", o, [1536]); o += 1536
        rcst = sb("rcst", o - 1536, [R_ALL])

        def small(name, shape):
            nonlocal o
            t = sb(name, o, shape)
            n = 1
            for d in shape:
                n *= d
            o += (n + 7) // 8 * 8
            return t

        cst = small("cst", [C_ALL])
        qkg = small("qkg", [2 * QK + 2 * GD + NE])
        colg = small("colg", [3])
        crows = small("crows", [CC])
        convc = small("convc", [4, CW + 3])
        sT = small("sT", [2 * KC])
        ssum = small("ssum", [3, NT])
        wk = small("wk", [2, NT])
        rw = small("rw", [KC, NE])
        rowY = sb("rowY", o, [2, NT], U32)
        rowL = sb("rowL", o + 8, [2, NT], U32)
        toku = sb("toku", o + 16, [NT], U32)
        ni = sb("ni", o + 24, [32], I32)
        cur = sb("cur", o + 56, [2, 8], U32)
        o += 72
        rinv = small("rinv", [4])
        mxs = small("mxs", [4])
        cstat = small("cstat", [NT, 2])
        nmax = small("nmax", [4])
        rsum = small("rsum", [4])
        zero = sb("zero", o, [LISTW], U32)
        lst = sb("lst", o, [LISTW], U32)
        o += 32
        assert base + 4 * o <= nc.sbuf_usable_end, (base + 4 * o - nc.sbuf_usable_end)
        e = m0 + 4 * W_CQKV
        xg = sb("xg", e, [2, D]); e += 2048
        yg = sb("yg", e, [2, D]); e += 2048
        xgT = sb("xgT", e, [2, KC, P]); e += 2048
        sg = sb("sg", e, [2, F]); e += 1024
        hh = sb("hh", e, [2, F]); e += 1024
        hhT = sb("hhT", e, [2, 4, P]); e += 1024
        r1 = sb("r1", e, [32, NT * NE]); e += 2048
        mods = sb("mods", m0 + 4 * W_CQKV + 1024, [D_MOD])
        crow = sb("crow", m0 + 4 * W_CQKV + 1024 + 3 * 2048, [P])
        csig = sb("csig", m0 + 4 * W_CQKV + 1024 + 3 * 2048 + P, [2 * KC])
        rowC = sb("rowC", 16384, [2, D])
        ropt = sb("ropt", m0 + 4 * W_CQKV + 1024 + 2048 + 2048 + 256, [4, 256])
        kpe = sb("kpe", m0 + 4 * W_CQKV + 1024 + 2048 + 2048 + 1280, [NT, ROPE])
        stat = sb("stat", m0 + 4 * W_CQKV + 1024 + 2048 + 2048, [NT, 35])
        bnst = sb("bnst", m0 + 4 * W_CQKV + 1024 + 2048 + 2048 + 144, [NT, 8])
        mv = sb("mv", m0 + 4 * W_CQKV + 1024 + 2048 + 2048 + 176, [NT, 2])

        mod_d = nc.dram_tensor("mod_d", [2, DEPTH * D_MOD], F32, kind="Internal").ap()
        list_d = [nc.dram_tensor(f"list_d{l}", [P * LISTW, 1], U32, kind="Internal").ap() for l in range(DEPTH)]
        h2_d = [nc.dram_tensor(f"h2_d{l}", [(NT, LT)[l] * P, D], F32, kind="Internal").ap() for l in range(DEPTH)]
        y_d = [nc.dram_tensor(f"y_d{l}", [ITEMS * P, D], F32, kind="Internal").ap() for l in range(DEPTH)]

        ident = cst[:, C_ID:C_ID + P]

        bank = Banks([sem(f"bank_full{i}") for i in range(8)], [sem(f"bank_read{i}") for i in range(8)])
        s_cst, s_c, s_x, s_zero, s_out = sem("s_cst"), sem("s_c"), sem("s_x"), sem("s_zero"), sem("s_out")
        slab_in = [sem(f"slab_in{i}") for i in range(4)]
        mod_in = [sem(f"mod_in{i}") for i in range(4)]
        mod_full, mod_read = sem("mod_full"), sem("mod_read")
        mod_out = [sem(f"mod_out{i}") for i in range(MODG)]
        s_bias = sem("s_bias")
        s_silu_c, s_zset = sem("s_silu_c"), sem("s_zset")
        dve_step, act_step = sem("dve_step"), sem("act_step")
        names = ["pad", "sq", "sqm", "sqrt", "rows1", "rows2", "rows3", "rows4", "par", "h", "csq", "cn", "st", "nrm",
                 "nmax", "cvd", "lnv", "lns", "mg", "xm", "h2", "h2o", "rcst", "mask", "ni", "xf", "scat"]
        S = [{n: sem(f"{n}{l}") for n in names} for l in range(DEPTH)]
        mnames = ["gu", "sig", "h", "xt", "xtA", "xtD", "ht", "htA", "y", "yA", "yD", "cur"]
        M = [{n: sem(f"moe_{n}{l}") for n in mnames} for l in range(DEPTH)]
        m_in = [[sem(f"moe_in{l}_{i}") for i in range(6)] for l in range(DEPTH)]
        m_xg = [[sem(f"moe_xg{l}_{i}") for i in range(2)] for l in range(DEPTH)]
        m_yo = [[sem(f"moe_yo{l}_{i}") for i in range(2)] for l in range(DEPTH)]
        m_yk = [sem(f"moe_yk{i}") for i in range(2)]

        QT = [NT, LT]
        keys_of = [(0, NT) if t < LT else (LT, NT) for t in range(NT)]

        def slabs(l):
            T = QT[l] - 1

            def win(c0, w):
                return [(w_cols(a["w_in"][l], c0, w), w)]
            def gates(b):
                for hf in range(2):
                    yield f"g{b}{hf}", win(COL_GATE + b * D + hf * HALF, HALF), (l, "g", b, hf, T)

            def branch(b):
                w = a[("mla_w_o", "conv_w_o", "gqa_w_o")[b]]
                yield f"o{b}", [(w[l].rearrange("(k p) n -> p k n", p=P), None)], (l, "o", b, 1, T)
            yield "b1", win(COL_CONV, CC), (l, "b1", T)
            yield "b2", win(COL_CONV + CC, CC), (l, "b2", T)
            yield "b0", win(COL_CQ, W_CQKV), (l, "b0", NT - 1)
            yield "b4", win(COL_GK, 2 * GKV * GD), (l, "b4", NT - 1)
            yield "b3", win(COL_GQ, GH * GD), (l, "b3", T)
            yield from gates(1)
            yield "up", None, (l, "ukv", NT - 1, 1)
            yield from branch(1)
            for b in MERGE:
                yield from branch(b)
                yield from gates(b)
            for hf in range(2):
                yield f"w{hf}", [(w_cols(a["w_out"][l], hf * HALF, HALF), HALF)], (l, "w", hf, T)

        def w_cols(w, c0, n):
            return w[:, c0:c0 + n].rearrange("(k p) n -> p k n", p=P)

        slab_plan, slab_at = [], {}
        for l in range(DEPTH):
            for n, (name, src, last) in enumerate(slabs(l)):
                loads = 2 if name == "up" else 1
                slot = n % 4
                before = sum(q[4] for q in slab_plan if q[3] == slot)
                slab_plan.append((l, name, src, slot, loads, last))
                slab_at[l, name] = (slot, 16 * (before + loads))

        def wait_slab(eng, l, name):
            slot, v = slab_at[l, name]
            eng.wait_ge(slab_in[slot], v)
            return slab[slot]

        lo, hi = (0, 1, 2, 3), (4, 5, 6, 7)

        def attn_units(l):
            return [(h, t) for h in range(H) for t in range(QT[l])]

        def plan_layer(l):
            T = QT[l]
            for t in range(T):
                for hf in range(2):
                    bank.plan((l, "h", t, hf), hi)
            for t in range(T):
                bank.plan((l, "b1", t), lo)
                bank.plan((l, "b2", t), hi)
            for t in range(T, NT):
                for hf in range(2):
                    bank.plan((l, "h", t, hf), hi)
            bank.plan((l, "conv_cols"), hi)
            for t in range(NT):
                bank.plan((l, "b0", t), lo)
            for c in range(4):
                bank.plan((l, "yT", c), hi)
            for t in range(NT):
                bank.plan((l, "b4", t), hi)
            for t in range(T):
                bank.plan((l, "b3", t), lo)
            for t in range(T):
                bank.plan((l, "g", 1, 0, t), lo)
            for c in range(3):
                bank.plan((l, "cT", c), hi)
            for t in range(T):
                bank.plan((l, "cvb", t), hi)
            for t in range(T):
                bank.plan((l, "g", 1, 1, t), lo)
            for c in range(4):
                bank.plan((l, "zT", c), hi)
            for t in range(T):
                bank.plan((l, "uq", t, 0), lo)
                bank.plan((l, "uq", t, 1), lo)
            for t in range(NT):
                bank.plan((l, "ukv", t, 0), lo)
                bank.plan((l, "ukv", t, 1), lo)
            for hf in range(2):
                for t in range(T):
                    bank.plan((l, "o", 1, hf, t), hi)
            for kind in ("gqa", "mla"):
                for i, step in attn_order(l, kind):
                    if step == "head":
                        bank.plan((l, kind, "qT", i), (0, 1))
                        if kind == "mla" or i % 4 == 0:
                            bank.plan((l, kind, "kT", i), (0, 1))
                    else:
                        bank.plan((l, kind, step, i), {"s": (2, 3), "pT": (4, 5), "pv": (6, 7)}[step])
                for c in range(4):
                    bank.plan((l, kind, "oT", c), hi)
            for b in MERGE:
                for hf in range(2):
                    for t in range(T):
                        bank.plan((l, "o", b, hf, t), lo)
                        bank.plan((l, "g", b, hf, t), hi)
            for hf in range(2):
                for t in range(T):
                    bank.plan((l, "mT", t, hf), hi)
            for hf in range(2):
                for t in range(T):
                    bank.plan((l, "w", hf, t), lo)
            for t in range(T):
                for hf in range(2):
                    bank.plan((l, "h2", t, hf), (4, 5))
            bank.plan((l, "router"), (0,))
            bank.plan((l, "place"), (1,))
            if l + 1 < DEPTH:
                for j in range(MODB):
                    bank.plan((l, "mod", j), (2, 3, 6, 7))

        def par_count(l):
            return 16 * (11 if l == 0 else 10)

        def attn_order(l, kind):
            U = attn_units(l)
            yield 0, "head"
            for i in range(len(U) + 2):
                if i + 1 < len(U) and U[i + 1][1] == 0:
                    yield U[i + 1][0], "head"
                if i < len(U):
                    yield i, "s"
                if 1 <= i <= len(U):
                    yield i - 1, "pT"
                if i >= 2:
                    yield i - 2, "pv"

        for l in range(DEPTH):
            plan_layer(l)

        def load_expert(sp, l, slot, kind, w):
            src = w.rearrange("o (k p) n -> p (o k) n", p=P)
            dst = slab[slot][:] if kind < 2 else slab[slot][:].rearrange("p (k j) n -> p k (j n)", k=4)
            sp.dma_start(dst, src).then_inc(m_in[l][slot], 16)

        def store_item(sp, l, m, u, item):
            sp.wait_ge(m["yA"], item + 2)
            sp.wait_ge(m["yD"], item + 2)
            sp.dma_start(y_d[l][bass.ds(item * P, P), :], yg[:, u, :]).then_inc(m_yo[l][u], 16)

        block = ctx.enter_context(nc.Block())

        @block.sync
        def _(sp):
            sp.dma_start(cst[:], consts[:, 0:C_ALL]).then_inc(s_cst, 16)
            sp.dma_start(crow[0:KC, :], a["c"].rearrange("o (k p) -> (o k) p", p=P)).then_inc(s_c, 16)
            sp.dma_start(crow[KC:2 * KC, :], a["c_ctx"].rearrange("(k p) -> k p", p=P)).then_inc(s_c, 16)
            w_v = a["w_mod"][0].rearrange("(k p) n -> p k n", p=P)
            with sp.Fori(0, MODG) as i:
                for u in range(4):
                    sp.wait_ge(mod_read, 4 * i + (u + 1))
                    sp.dma_start(slab[u][:], w_v[:, :, bass.ds((4 * i + u) * HALF, HALF)]).then_inc(mod_in[u], 16)
            for l in range(DEPTH):
                mine = [q for q in slab_plan if q[0] == l]
                for n, (_, name, src, slot, loads, last) in enumerate(mine):
                    if n >= 4:
                        bank.wait_full(sp, mine[n - 4][5])
                    elif l == 0:
                        sp.wait_ge(mod_read, MODB + 1 + slot)
                    if name == "up":
                        flat = slab[slot][:].rearrange("p k n -> p (k n)")
                        uq = a["mla_w_uq"][l].rearrange("(k p) n -> p k n", p=P)
                        sp.dma_start(flat[:, 0:2 * H * QK].rearrange("p (k n) -> p k n", k=2), uq).then_inc(slab_in[slot], 16)
                        sp.dma_start(flat[:, 2 * H * QK:2 * H * QK + H * (NOPE + VD)], a["mla_w_ukv"][l]).then_inc(slab_in[slot], 16)
                        continue
                    ap, w = src[0]
                    if w is None:
                        dst = slab[slot][:].rearrange("p (k j) n -> p k (j n)", k=4)
                    else:
                        dst = slab[slot][:, :, 0:w]
                    sp.dma_start(dst, ap).then_inc(slab_in[slot], 16)

                m = M[l]

                def load_item(u, e):
                    for kind, w in enumerate(("moe_w_gate", "moe_w_up", "moe_w_down")):
                        yield kind, MSLOT[3 * u + kind], a[w][l][e]

                slot_last = {1: mine[13][5], 2: mine[14][5], 3: mine[15][5], 0: mine[16][5], 4: mine[12][5], 5: mine[12][5]}
                for u in range(2):
                    for kind, slot, w in load_item(u, slice(u, u + 1)):
                        bank.wait_full(sp, slot_last[slot])
                        load_expert(sp, l, slot, kind, w)
                        if (u, kind) == (0, 1) and l + 1 < DEPTH:
                            w_v = a["w_mod"][l + 1].rearrange("(k p) n -> p k n", p=P)
                            for j in range(MODB):
                                at = MODSLOT[j % 4]
                                bank.wait_full(sp, slot_last[at])
                                sp.dma_start(slab[at][:], w_v[:, :, j * HALF:(j + 1) * HALF]).then_inc(mod_in[at], 16)
                                slot_last[at] = (l, "mod", j)
                sp.wait_ge(S[l]["ni"], 1)
                pairs = sp.value_load(ni[0:1, ITEMS:ITEMS + 1], min_val=NE // 2, max_val=ITEMS // 2)
                with sp.Fori(1, pairs) as q:
                    for u in range(2):
                        e = sp.value_load(ni[0:1, bass.ds(2 * q + u, 1)], min_val=0, max_val=NE - 1)
                        for kind, slot, w in load_item(u, bass.ds(e, 1)):
                            if kind < 2:
                                sp.wait_ge(m["gu"], 4 * q + (2 * u - 4 + kind + 1))
                            else:
                                sp.wait_ge(m["y"], 4 * q + (2 * u - 4 + 2))
                            load_expert(sp, l, slot, kind, w)
                        store_item(sp, l, m, u, 2 * q + (u - 2))
                for u in range(2):
                    store_item(sp, l, m, u, 2 * pairs + (u - 2))

        @block.tensor
        def _(pe):
            def fill(key, mms):
                bank.wait_free(pe, key)
                ins = None
                for ins in mms:
                    pass
                bank.filled(ins, key)

            def pb(key):
                return ps[bank.at[key][0]]

            pe.wait_ge(s_cst, 16)
            pe.wait_ge(s_c, 32)
            pe.transpose(ps[7][:, 0:2 * KC], crow[0:2 * KC, :], ident[0:2 * KC, 0:2 * KC]).then_inc(mod_full, 1)
            pe.wait_ge(s_silu_c, 2)
            with pe.Fori(0, MODG) as i:
                for u in range(4):
                    pe.wait_ge(mod_in[u], 16 * i + 16)
                    pe.wait_ge(mod_read, 4 * i + (u + 1))
                    for k in range(KC):
                        mm = pe.matmul(ps[u][0:2, :], sT[:, k:2 * KC:KC], slab[u][:, k, :], start=k == 0, stop=k == KC - 1)
                    mm.then_inc(mod_full, 1)

            def transposes(key, parts, rows=P):
                bank.wait_free(pe, key)
                for src, c in parts:
                    k, n = src.shape[0], src.shape[-1]
                    mm = pe.transpose(pb(key)[0:n, c:c + k], src, ident[0:k, 0:k])
                bank.filled(mm, key)

            def product(key, lhs, rhs, n, c=0, rows=P):
                bank.wait_free(pe, key)
                for k in range(len(lhs)):
                    mm = pe.matmul(pb(key)[0:rows, c:c + n], lhs[k], rhs[k], start=k == 0, stop=k == len(lhs) - 1)
                bank.filled(mm, key)

            for l in range(DEPTH):
                T, s = QT[l], S[l]

                def h_transposes(t):
                    pe.wait_ge(s["h"], t + 1)
                    for hf in range(2):
                        transposes((l, "h", t, hf), [(htile[:, t % 2, (4 * hf + c) * P:(4 * hf + c + 1) * P], c * P) for c in range(4)])

                def project(name, t, w, key=None):
                    sl = wait_slab(pe, l, name)
                    product(key or (l, name, t), [hT[:, k, t * P:(t + 1) * P] for k in range(KC)], [sl[:, k, 0:w] for k in range(KC)], w)

                for t in range(T):
                    h_transposes(t)
                    bank.wait_read(pe, (l, "h", t, 0))
                    bank.wait_read(pe, (l, "h", t, 1))
                    project("b1", t, CC)
                for t in range(T):
                    project("b2", t, CC)
                for t in range(T, NT):
                    h_transposes(t)
                pe.wait_ge(s["par"], par_count(l))
                transposes((l, "conv_cols"), [(crows[0:CW + 3, c * P:(c + 1) * P], c * (CW + 3)) for c in range(4)])
                for t in range(NT):
                    bank.wait_read(pe, (l, "h", t, 0))
                    bank.wait_read(pe, (l, "h", t, 1))
                    project("b0", t, W_CQKV)
                    if t:
                        continue
                    for c in range(4):
                        for v in range(T):
                            bank.wait_read(pe, (l, "b1", v))
                        transposes((l, "yT", c), [(ybuf[:, v, c * P:(c + 1) * P], v * P) for v in range(T)])
                for t in range(NT):
                    project("b4", t, 2 * GKV * GD)
                for t in range(T):
                    project("b3", t, GH * GD)
                for t in range(T):
                    project("g10", t, HALF, key=(l, "g", 1, 0, t))
                pe.wait_ge(s["cn"], 1)
                for c in range(3):
                    tiles = range(T) if c < 2 else range(NT)
                    transposes((l, "cT", c), [(cqkv[:, t, c * P:(c + 1) * P], t * P) for t in tiles])
                pe.wait_ge(s["cvd"], 4)
                for t in range(T):
                    r = (t % LT) * P
                    transposes((l, "cvb", t), [(cv[:, c, t // LT, r:r + P], c * P) for c in range(4)])
                for t in range(T):
                    project("g11", t, HALF, key=(l, "g", 1, 1, t))
                for t in range(T):
                    bank.wait_read(pe, (l, "cvb", t))
                for c in range(4):
                    transposes((l, "zT", c), [(ybuf[:, t, c * P:(c + 1) * P], t * P) for t in range(T)])

                sl = wait_slab(pe, l, "up")[:].rearrange("p k n -> p (k n)")
                uq = sl[:, 0:2 * H * QK].rearrange("p (k n) -> p k n", k=2)
                ukv = sl[:, 2 * H * QK:2 * H * QK + H * (NOPE + VD)]
                for c in range(3):
                    bank.wait_read(pe, (l, "cT", c))
                for t in range(T):
                    cols = slice(t * P, (t + 1) * P)
                    product((l, "uq", t, 0), [cT[:, k, cols] for k in range(2)], [uq[:, k, 0:HALF] for k in range(2)], HALF)
                    product((l, "uq", t, 1), [cT[:, k, cols] for k in range(2)], [uq[:, k, HALF:H * QK] for k in range(2)], H * QK - HALF)
                for t in range(NT):
                    for hf in range(2):
                        product((l, "ukv", t, hf), [cT[:, 2, t * P:(t + 1) * P]], [ukv[:, hf * HALF:(hf + 1) * HALF]], HALF)

                def branch(b, hf, t):
                    oT = (oT_mla, zT, oT_gqa)[b]
                    wo = wait_slab(pe, l, f"o{b}")[:].rearrange("p (k j) n -> p k (j n)", k=4)
                    product((l, "o", b, hf, t), [oT[:, c, t * P:(t + 1) * P] for c in range(4)],
                            [wo[:, c, hf * HALF:(hf + 1) * HALF] for c in range(4)], HALF)
                for c in range(4):
                    bank.wait_read(pe, (l, "zT", c))
                for hf in range(2):
                    for t in range(T):
                        branch(1, hf, t)

                U = attn_units(l)
                for kind in ("gqa", "mla"):
                    pe.wait_ge(s["nrm"], 1 if kind == "gqa" else 2)
                    d = QK if kind == "mla" else GD
                    kslot = (lambda h: h % 2) if kind == "mla" else (lambda h: h // 4)
                    for i, step in attn_order(l, kind):
                        if step == "head":
                            if kind == "mla":
                                q_of, k_of = (lambda t, h: q_tm[:, t, h, :]), (lambda t, h: kfull[:, t, h, :])
                            else:
                                q_of, k_of = (lambda t, h: gq[:, t, h * GD:(h + 1) * GD]), (lambda t, h: gkv[:, t, (h // 4) * GD:(h // 4 + 1) * GD])
                            transposes((l, kind, "qT", i), [(q_of(t, i), t * P) for t in range(T)])
                            if kind == "mla" or i % 4 == 0:
                                transposes((l, kind, "kT", i), [(k_of(t, i), t * P) for t in range(NT)])
                            continue
                        h, t = U[i]
                        k0, k1 = keys_of[t]
                        n = k1 - k0
                        if step == "s":
                            bank.wait_read(pe, (l, kind, "qT", h))
                            bank.wait_read(pe, (l, kind, "kT", h if kind == "mla" else h // 4 * 4))
                            product((l, kind, "s", i), [headT[0:d, h % 2, 0, t * P:(t + 1) * P]],
                                    [headT[0:d, kslot(h), 1, k0 * P:k1 * P]], n * P)
                        elif step == "pT":
                            bank.wait_read(pe, (l, kind, "s", i))
                            transposes((l, kind, "pT", i), [(prob[:, i % 2, j * P:(j + 1) * P], j * P) for j in range(n)])
                        else:
                            bank.wait_read(pe, (l, kind, "pT", i))
                            v = (lambda j: v_tm[:, j, h * VD:(h + 1) * VD]) if kind == "mla" else \
                                (lambda j: gkv[:, j, (GKV + h // 4) * GD:(GKV + h // 4 + 1) * GD])
                            product((l, kind, "pv", i), [probT[:, i % 2, j, :] for j in range(n)],
                                    [v(k0 + j) for j in range(n)], VD)
                    for i in range(len(U)):
                        if i >= len(U) - 2:
                            bank.wait_read(pe, (l, kind, "pv", i))
                    for c in range(4):
                        transposes((l, kind, "oT", c), [(o_tm[:, t, c * P:(c + 1) * P], t * P) for t in range(T)])

                for b in MERGE:
                    for c in range(4):
                        bank.wait_read(pe, (l, "mla" if b == 0 else "gqa", "oT", c))
                    for hf in range(2):
                        for t in range(T):
                            branch(b, hf, t)
                            project(f"g{b}{hf}", t, HALF, key=(l, "g", b, hf, t))
                for hf in range(2):
                    for t in range(T):
                        pe.wait_ge(s["mg"], hf * T + t + 1)
                        transposes((l, "mT", t, hf), [(merged[:, t, (4 * hf + c) * P:(4 * hf + c + 1) * P], c * P) for c in range(4)])
                def h2_transposes(t):
                    pe.wait_ge(s["h2"], t + 1)
                    for hf in range(2):
                        transposes((l, "h2", t, hf), [(htile[:, t % 2, (4 * hf + c) * P:(4 * hf + c + 1) * P], c * P) for c in range(4)])

                for hf in range(2):
                    for t in range(T):
                        bank.wait_read(pe, (l, "mT", t, 0))
                        bank.wait_read(pe, (l, "mT", t, 1))
                        project(f"w{hf}", t, HALF, key=(l, "w", hf, t))
                        if hf and t >= 2:
                            h2_transposes(t - 2)

                def modulation(js):
                    for j in js if l + 1 < DEPTH else ():
                        at = MODSLOT[j % 4]
                        pe.wait_ge(mod_in[at], 16 * (MODG + j // 4 + 1))
                        product((l, "mod", j), [sT[:, k:2 * KC:KC] for k in range(KC)], [slab[at][:, k, :] for k in range(KC)], HALF, rows=2)

                modulation([0])
                for t in range(T - 2, T):
                    h2_transposes(t)
                modulation([1])
                key = (l, "router")
                bank.wait_free(pe, key)
                pe.wait_ge(s_zero, ZEROED)
                for t in range(T):
                    bank.wait_read(pe, (l, "h2", t, 0))
                    bank.wait_read(pe, (l, "h2", t, 1))
                    for k in range(KC):
                        mm = pe.matmul(pb(key)[:, t * NE:(t + 1) * NE], hT[:, k, t * P:(t + 1) * P], rw[:, k, :], start=k == 0, stop=k == KC - 1)
                bank.filled(mm, key)
                modulation([2, 3])
                key = (l, "place")
                bank.wait_free(pe, key)
                pe.wait_ge(s["rcst"], 16)
                pe.wait_ge(s["mask"], 1)
                mask = r1[:, R_MASK, 0:T * NE].rearrange("p (t e) -> p t e", e=NE)
                for t in range(T):
                    for b in range(t + 1):
                        lhs = rcst[:, R_TRI:R_TRI + P] if b == t else rcst[:, R_ONES:R_ONES + P]
                        pe.matmul(pb(key)[:, t * NE:(t + 1) * NE], lhs, mask[:, b, :], start=b == 0, stop=b == t)
                for t in range(T):
                    mm = pe.matmul(pb(key)[:, NT * NE:(NT + 1) * NE], rcst[:, R_ONES:R_ONES + P], mask[:, t, :], start=t == 0, stop=t == T - 1)
                bank.filled(mm, key)
                modulation(range(4, MODB))

                m = M[l]
                G, UP, X0, X1, HT_, Y0, Y1 = (ps[i] for i in (2, 3, 4, 5, 6, 7, 0))

                def gather_T(item, u):
                    pe.wait_ge(m_xg[l][u], item)
                    for hf, X in enumerate((X0, X1)):
                        for c in range(4):
                            mm = pe.transpose(X[:, c * P:(c + 1) * P], xg[:, u, (4 * hf + c) * P:(4 * hf + c + 1) * P], ident)
                        mm.then_inc(m["xt"], 1)

                for key in ((l, "router"), (l, "place"), (l, "h2", T - 1, 0), (l, "h2", T - 1, 1), (l, "h2", T - 2, 0), (l, "h2", T - 2, 1)):
                    bank.wait_read(pe, key)
                for t in range(T):
                    bank.wait_read(pe, (l, "w", 0, t))
                    bank.wait_read(pe, (l, "w", 1, t))
                for j in range(MODB - 4, MODB) if l + 1 < DEPTH else ():
                    bank.wait_read(pe, (l, "mod", j))
                pe.wait_ge(s["ni"], 1)
                pairs = pe.value_load(ni[0:1, ITEMS:ITEMS + 1], min_val=NE // 2, max_val=ITEMS // 2)
                gather_T(16, 0)
                with pe.Fori(0, pairs) as q:
                    for u in range(2):
                        sg_, su_, sd_ = (MSLOT[3 * u + k] for k in range(3))
                        done = 2 * q + (u + 1)
                        pe.wait_ge(m["xtA"], done)
                        pe.wait_ge(m["xtD"], done)
                        for slot, B, free in ((sg_, G, "sig"), (su_, UP, "h")):
                            pe.wait_ge(m_in[l][slot], 16 * q + 16)
                            pe.wait_ge(m[free], done)
                            for k in range(KC):
                                mm = pe.matmul(B[:], xgT[:, u, k, :], slab[slot][:, k, :], start=k == 0, stop=k == KC - 1)
                            mm.then_inc(m["gu"], 1)
                        gather_T(16 * q + (16 if u == 0 else 32), 1 - u)
                        pe.wait_ge(m["h"], done + 1)
                        pe.wait_ge(m["htA"], done)
                        for c in range(4):
                            mm = pe.transpose(HT_[:, c * P:(c + 1) * P], hh[:, u, c * P:(c + 1) * P], ident)
                        mm.then_inc(m["ht"], 1)
                        pe.wait_ge(m["htA"], done + 1)
                        pe.wait_ge(m_in[l][sd_], 16 * q + 16)
                        wd = slab[sd_][:].rearrange("p (k j) n -> p k (j n)", k=4)
                        for hf, (Y, free) in enumerate(((Y0, "yA"), (Y1, "yD"))):
                            pe.wait_ge(m[free], done)
                            for c in range(4):
                                mm = pe.matmul(Y[:], hhT[:, u, c, :], wd[:, c, hf * HALF:(hf + 1) * HALF], start=c == 0, stop=c == 3)
                            mm.then_inc(m["y"], 1)

        @block.scalar
        def _(act):
            steps = [0]

            def step(ins):
                ins.then_inc(act_step, 1)
                steps[0] += 1
                act.wait_ge(act_step, steps[0])

            def copy_of(key, dst, src):
                bank.wait_full(act, key)
                bank.read(act.activation(dst, src, ACT.Copy), key)

            def pb(key):
                return ps[bank.at[key][0]]

            act.dma_start(x_sb[:, 0:LT, :], a["x"].rearrange("o (t p) d -> p (o t) d", p=P)).then_inc(s_x, 16)
            act.dma_start(x_sb[:, LT:NT, :], a["ctx"].rearrange("o (t p) d -> p (o t) d", p=P)).then_inc(s_x, 16)
            act.wait_ge(mod_full, 1)
            act.activation(csig[:], ps[7][:, 0:2 * KC], ACT.Sigmoid).then_inc(s_silu_c, 1)

            def modulation_out(l, g):
                w = D_MOD // MODG
                act.dma_start(mod_d[:, l * D_MOD + g * w:l * D_MOD + (g + 1) * w], mods[0:2, g * w:(g + 1) * w]).then_inc(mod_out[g], 16)

            for l in range(DEPTH):
                T, s, m = QT[l], S[l], M[l]

                def square(n, t):
                    if n:
                        act.wait_ge(s["sq"], n)
                    act.activation(junk[:], x_sb[:, t, :], ACT.Square, accum_out=ssum[:, 0, t:t + 1]).then_inc(s["sq"], 1)

                def root(n, t):
                    act.wait_ge(s["sqm"], n + 1)
                    act.activation(ssum[:, 2, t:t + 1], ssum[:, 1, t:t + 1], ACT.Sqrt).then_inc(s["sqrt"], 1)

                def h_copies(name, t):
                    for hf in range(2):
                        key = (l, name, t, hf)
                        copy_of(key, hT[:, 4 * hf:4 * hf + 4, t * P:(t + 1) * P], pb(key)[:].rearrange("p (c n) -> p c n", c=4))

                def conv_input_gates():
                    for t in range(T):
                        key = (l, "b2", t)
                        bank.wait_full(act, key)
                        if t >= 2:
                            bank.wait_read(act, (l, "b1", t - 2))
                        bank.read(act.activation(sgt[:, t % 2, :], pb(key)[:], ACT.Sigmoid), key)

                if l == 0:
                    act.wait_ge(s_x, 32)
                    for t in range(NT):
                        square(t, t)
                    for t in range(NT):
                        root(t, t)
                    for g in range(MODG):
                        act.wait_ge(mod_read, 4 * (g + 1) + 4)
                        modulation_out(l, g)
                    for t in range(T):
                        h_copies("h", t)
                    conv_input_gates()
                    for g in range(MODG):
                        act.wait_ge(mod_out[g], 16)
                else:
                    for t in range(NT):
                        act.wait_ge(S[l - 1]["xf"], t + 1)
                        square(t, t)
                        root(t, t)
                        if t and t - 1 < T:
                            h_copies("h", t - 1)
                    conv_input_gates()
                    for t in range(T, NT):
                        h_copies("h", t)
                copy_of((l, "b0", 0), cqkv[:, 0, :], pb((l, "b0", 0))[:, 0:W_CQKV])
                act.wait_ge(s["pad"], 1)
                for c in range(4):
                    key = (l, "yT", c)
                    copy_of(key, ypad[:, c, 0:T // LT, CW // 2:CW // 2 + SEQ], pb(key)[:, 0:T * P].rearrange("p (s n) -> p s n", n=SEQ))
                for t in range(1, NT):
                    copy_of((l, "b0", t), cqkv[:, t, :], pb((l, "b0", t))[:, 0:W_CQKV])
                act.wait_ge(s["csq"], 1)
                for t in range(NT):
                    bank.wait_read(act, (l, "b0", t))
                    if t < T:
                        act.activation(junk[:, 0:QR], cqkv[:, t, 0:QR], ACT.Square, accum_out=cstat[:, t, 0:1])
                    ins = act.activation(junk[:, QR:QR + KVR], cqkv[:, t, QR:QR + KVR], ACT.Square, accum_out=cstat[:, t, 1:2])
                    if t < NT - 1:
                        step(ins)
                ins.then_inc(s["csq"], 1)
                for t in range(NT):
                    copy_of((l, "b4", t), gkv[:, t, :], pb((l, "b4", t))[:, 0:2 * GKV * GD])
                for t in range(T):
                    copy_of((l, "b3", t), gq[:, t, :], pb((l, "b3", t))[:])
                act.wait_ge(s["csq"], 3)
                act.activation(cstat[:], cstat[:], ACT.Sqrt).then_inc(s["csq"], 1)

                def conv_gate(hf):
                    for t in range(T):
                        key = (l, "g", 1, hf, t)
                        bank.wait_full(act, key)
                        bank.read(act.activation(merged[:, t, hf * HALF:(hf + 1) * HALF], pb(key)[:], ACT.Sigmoid), key)
                conv_gate(0)
                for c in range(3):
                    n = (T if c < 2 else NT) * P
                    key = (l, "cT", c)
                    bank.wait_full(act, key)
                    bank.read(act.activation(cT[:, c, 0:n], pb(key)[:, 0:n], ACT.Identity, scale=colg[:, c:c + 1]), key)
                act.wait_ge(s["lnv"], 1)
                act.activation(mv[:, 0:T, 1:2], mv[:, 0:T, 1:2], ACT.Sqrt).then_inc(s["lns"], 1)
                conv_gate(1)
                for c in range(4):
                    key = (l, "zT", c)
                    bank.wait_full(act, key)
                    bank.read(act.activation(zT[:, c, 0:T * P], pb(key)[:, 0:T * P], ACT.Silu, scale=convc[:, c, CW + 1:CW + 2],
                                             bias=convc[:, c, CW + 2:CW + 3]), key)
                for t in range(T):
                    q2 = q_tm[:, t].rearrange("p h d -> p (h d)")
                    copy_of((l, "uq", t, 0), q2[:, 0:HALF], pb((l, "uq", t, 0))[:])
                    copy_of((l, "uq", t, 1), q2[:, HALF:H * QK], pb((l, "uq", t, 1))[:, 0:H * QK - HALF])
                act.wait_ge(s["st"], 1)
                act.activation(stat[:, :, 0:HEAD_A], stat[:, :, 0:HEAD_A], ACT.Sqrt).then_inc(s["st"], 1)
                for t in range(NT):
                    for hf in range(2):
                        key = (l, "ukv", t, hf)
                        kv = pb(key)[:].rearrange("p (h d) -> p h d", h=4)
                        bank.wait_full(act, key)
                        act.activation(kfull[:, t, 4 * hf:4 * hf + 4, 0:NOPE], kv[:, :, 0:NOPE], ACT.Copy)
                        bank.read(act.activation(v_tm[:, t, 4 * hf * VD:4 * (hf + 1) * VD].rearrange("p (h d) -> p h d", h=4), kv[:, :, NOPE:NOPE + VD], ACT.Copy), key)
                act.wait_ge(s["st"], 3)
                act.activation(stat[:, :, HEAD_A:35], stat[:, :, HEAD_A:35], ACT.Sqrt).then_inc(s["st"], 1)

                U = attn_units(l)
                for kind in ("gqa", "mla"):
                    d = QK if kind == "mla" else GD
                    kslot = (lambda h: h % 2) if kind == "mla" else (lambda h: h // 4)
                    scale = float(d) ** -0.5
                    for i, stage in attn_order(l, kind):
                        key = (l, kind, stage, i)
                        if stage == "head":
                            if kind == "mla" or i % 4 == 0:
                                key = (l, kind, "kT", i)
                                copy_of(key, headT[0:d, kslot(i), 1, :], pb(key)[0:d, :])
                            continue
                        h, t = U[i]
                        n = keys_of[t][1] - keys_of[t][0]
                        if stage == "s":
                            act.wait_ge(s["nmax"], (len(U) if kind == "mla" else 0) + i + 1)
                            bank.wait_full(act, key)
                            if i >= 2:
                                bank.wait_full(act, (l, kind, "pT", i - 2))
                            bank.read(act.activation(prob[:, i % 2, 0:n * P], pb(key)[:, 0:n * P], ACT.Exp,
                                                     bias=nmax[:, i % 4:i % 4 + 1], scale=scale, accum_out=rsum[:, i % 4:i % 4 + 1]), key)
                        elif stage == "pT":
                            if i >= 2:
                                bank.wait_full(act, (l, kind, "pv", i - 2))
                            copy_of(key, probT[:, i % 2, 0:n, :], pb(key)[:, 0:n * P].rearrange("p (j q) -> p j q", q=P))
                    for c in range(4):
                        key = (l, kind, "oT", c)
                        dst = oT_mla if kind == "mla" else oT_gqa
                        copy_of(key, dst[:, c, 0:T * P], pb(key)[:, 0:T * P])

                i, used = 0, []
                for b in MERGE:
                    for hf in range(2):
                        for t in range(T):
                            key = (l, "g", b, hf, t)
                            bank.wait_full(act, key)
                            if i >= 2:
                                bank.wait_read(act, used[i - 2])
                            used.append((l, "o", b, hf, t))
                            bank.read(act.activation(sgt[:, i % 2, :], pb(key)[:], ACT.Sigmoid), key)
                            i += 1
                for hf in range(2):
                    for t in range(T):
                        key = (l, "mT", t, hf)
                        copy_of(key, hT[:, 4 * hf:4 * hf + 4, t * P:(t + 1) * P], pb(key)[:].rearrange("p (c n) -> p c n", c=4))

                stored = []

                def h2_store(t):
                    if t not in stored:
                        stored.append(t)
                        act.wait_ge(s["h2"], t + 1)
                        act.dma_start(h2_d[l][t * P:(t + 1) * P, :], htile[:, t % 2, :]).then_inc(s["h2o"], 16)
                for t in range(T):
                    act.wait_ge(s["xm"], T + t + 1)
                    square(NT + t, t)
                    if t >= 2:
                        h2_store(t - 2)
                        h2_store(1)
                        h_copies("h2", t - 2)
                    root(NT + t, t)
                for t in range(T - 2, T):
                    h2_store(t)
                    h_copies("h2", t)
                key = (l, "router")
                bank.wait_full(act, key)
                bank.read(act.activation(r1[:, R_S, 0:T * NE], pb(key)[:, 0:T * NE], ACT.Sigmoid), key)
                if l + 1 < DEPTH:
                    for g in range(MODG):
                        for j in range(4 * g, 4 * g + 4):
                            bank.wait_read(act, (l, "mod", j))
                        modulation_out(l + 1, g)
                    for g in range(MODG):
                        act.wait_ge(mod_out[g], 32)

                X0, HT_, Y0 = ps[4], ps[6], ps[7]
                for name in ("sig", "htA", "yA"):
                    act.sem_inc(m[name], 1)
                for u in range(2):
                    act.sem_inc(m_yo[l][u], 16)
                act.wait_ge(s["ni"], 1)
                pairs = act.value_load(ni[0:1, ITEMS:ITEMS + 1], min_val=NE // 2, max_val=ITEMS // 2)
                act.wait_ge(m["xt"], 1)
                act.activation(xgT[:, 0, 0:4, :], X0[:].rearrange("p (c n) -> p c n", c=4), ACT.Copy).then_inc(m["xtA"], 1)
                with act.Fori(0, pairs) as q:
                    for u in range(2):
                        done = 2 * q + (u + 1)
                        act.wait_ge(m["gu"], 4 * q + (2 * u + 1))
                        act.wait_ge(m["h"], done)
                        act.activation(sg[:, u, :], ps[2][:], ACT.Silu).then_inc(m["sig"], 1)
                        act.wait_ge(m["xt"], 4 * q + (2 * u + 3))
                        act.activation(xgT[:, 1 - u, 0:4, :], X0[:].rearrange("p (c n) -> p c n", c=4), ACT.Copy).then_inc(m["xtA"], 1)
                        act.wait_ge(m["ht"], done)
                        act.activation(hhT[:, u], HT_[:].rearrange("p (c n) -> p c n", c=4), ACT.Copy).then_inc(m["htA"], 1)
                        act.wait_ge(m["y"], 4 * q + (2 * u + 1))
                        act.wait_ge(m_yo[l][u], 16 * q + 16)
                        act.activation(yg[:, u, 0:HALF], Y0[:], ACT.Copy).then_inc(m["yA"], 1)
            for t in range(LT):
                act.wait_ge(S[DEPTH - 1]["xf"], t + 1)
                act.dma_start(out[0, t * P:(t + 1) * P, :], x_sb[:, t, :]).then_inc(s_out, 16)
            act.wait_ge(s_out, 16 * LT)

        @block.vector
        def _(dve):
            steps = [0]

            def step(ins):
                ins.then_inc(dve_step, 1)
                steps[0] += 1
                dve.wait_ge(dve_step, steps[0])

            def pb(key):
                return ps[bank.at[key][0]]

            TT, TS, STT, RED = dve.tensor_tensor, dve.tensor_scalar, dve.scalar_tensor_tensor, dve.tensor_reduce

            dve.sem_inc(mod_read, 4)
            dve.memset(rowC[:], 0.0)
            dve.memset(zero[:], 0).then_inc(s_zset, 1)
            dve.wait_ge(s_silu_c, 1)
            TT(sT[:], ps[7][:, 0:2 * KC], csig[:], ALU.mult).then_inc(s_silu_c, 1)

            def mean(l, n, t):
                dve.wait_ge(S[l]["sq"], n + 1)
                TS(ssum[:, 1, t:t + 1], ssum[:, 0, t:t + 1], 1.0 / D, EPS, ALU.mult, ALU.add).then_inc(S[l]["sqm"], 1)
            for t in range(NT):
                mean(0, t, t)
            dve.wait_ge(s_bias, 16)
            with dve.Fori(0, MODG) as i:
                for u in range(4):
                    dve.wait_ge(mod_full, 4 * i + (u + 2))
                    cols = mods[0:2, bass.ds((4 * i + u) * HALF, HALF)]
                    TT(cols, ps[u][0:2, :], cols, ALU.add).then_inc(mod_read, 1)

            for l in range(DEPTH):
                T, s, m = QT[l], S[l], M[l]

                def scales(k, rows, n_rows, n):
                    dve.wait_ge(S[k][rows], n_rows)
                    for r in range(n):
                        ins = STT(out=rowA[:, r, :], in0=rowA[:, r, :], scalar=1.0, in1=normg[:], op0=ALU.add, op1=ALU.mult)
                    step(ins)

                def normalise(k, n, t, free, done):
                    dve.wait_ge(S[k]["sqrt"], n + 1)
                    step(dve.reciprocal(ssum[:, 2, t:t + 1], ssum[:, 2, t:t + 1]))
                    free(k, t)
                    step(STT(out=htile[:, t % 2, :], in0=x_sb[:, t, :], scalar=ssum[:, 2, t:t + 1], in1=rowA[:, t // LT, :],
                             op0=ALU.mult, op1=ALU.mult))
                    TT(htile[:, t % 2, :], htile[:, t % 2, :], rowB[:, t // LT, :], ALU.add).then_inc(S[k][done], 1)

                def free1(k, t):
                    if t >= 2:
                        bank.wait_full(dve, (k, "h", t - 2, 1))
                if l == 0:
                    scales(0, "rows1", 16 * 5, 2)
                    for t in range(NT):
                        normalise(0, t, t, free1, "h")
                    dve.wait_ge(s_zero, ZEROED)
                    for g in range(MODG):
                        dve.wait_ge(mod_out[g], 16)

                for t in range(T):
                    key = (l, "b1", t)
                    bank.wait_read(dve, (l, "b2", t))
                    bank.wait_full(dve, key)
                    bank.read(TT(ybuf[:, t, :], pb(key)[:], sgt[:, t % 2, :], ALU.mult), key)
                dve.memset(cstat[:], 1.0).then_inc(s["csq"], 1)
                key = (l, "conv_cols")
                bank.wait_full(dve, key)
                bank.read(dve.tensor_copy(convc[:].rearrange("p c w -> p (c w)"), pb(key)[:, 0:4 * (CW + 3)]), key)
                bank.wait_read(dve, key)

                def cn():
                    dve.wait_ge(s["csq"], 2)
                    TS(cstat[:, :, 0:1], cstat[:, :, 0:1], 1.0 / QR, EPS, ALU.mult, ALU.add)
                    TS(cstat[:, :, 1:2], cstat[:, :, 1:2], 1.0 / KVR, EPS, ALU.mult, ALU.add).then_inc(s["csq"], 1)
                    dve.wait_ge(s["csq"], 4)
                    step(dve.reciprocal(cstat[:], cstat[:]))
                    for t in range(NT):
                        if t < T:
                            TS(cqkv[:, t, 0:QR], cqkv[:, t, 0:QR], cstat[:, t, 0:1], None, ALU.mult)
                        ins = TS(cqkv[:, t, QR:QR + KVR], cqkv[:, t, QR:QR + KVR], cstat[:, t, 1:2], None, ALU.mult)
                    ins.then_inc(s["cn"], 1)

                ns = T // LT
                for pair in ((0, 1), (2, 3)):
                    tap = {}
                    for w in range(CW):
                        for c in pair:
                            src = ypad[:, c, 0:ns, w:w + SEQ]
                            acc = cv[:, c, 0:ns, :]
                            if w == 0:
                                bank.wait_read(dve, (l, "yT", c))
                                ins = TS(acc, src, convc[:, c, 0:1], convc[:, c, CW:CW + 1], ALU.mult, ALU.add)
                            else:
                                dve.wait_ge(dve_step, tap[c])
                                ins = STT(out=acc, in0=src, scalar=convc[:, c, w:w + 1], in1=acc, op0=ALU.mult, op1=ALU.add)
                            if w < CW - 1:
                                ins.then_inc(dve_step, 1)
                                steps[0] += 1
                                tap[c] = steps[0]
                            else:
                                ins.then_inc(s["cvd"], 1)
                    if pair[0] == 0:
                        cn()
                for t in range(T):
                    bank.wait_full(dve, (l, "cvb", t))
                    ins = dve.bn_stats(bnst[:, t, 0:6], pb((l, "cvb", t))[:])
                step(ins)
                for t in range(T):
                    ins = dve.bn_aggr(mv[:, t, :], bnst[:, t, 0:6])
                step(ins)
                TS(mv[:, 0:T, 1:2], mv[:, 0:T, 1:2], EPS, None, ALU.add).then_inc(s["lnv"], 1)
                dve.wait_ge(s["lns"], 1)
                step(dve.reciprocal(mv[:, 0:T, 1:2], mv[:, 0:T, 1:2]))
                for t in range(T):
                    key = (l, "cvb", t)
                    bank.read(TS(ybuf[:, t, :], pb(key)[:], mv[:, t, 0:1], mv[:, t, 1:2], ALU.subtract, ALU.mult), key)

                def heads(x, d):
                    return x.rearrange("p (h d) -> p h d", d=d)

                def parts_a(t):
                    parts = [(heads(gkv[:, t, 0:GKV * GD], GD), 8, 10, 2 * QK + GD, GD, heads(gkv[:, t, 0:GKV * GD], GD), 16, 32),
                             (heads(cqkv[:, t, QR + KVR:W_CQKV], ROPE), 10, 11, QK + NOPE, ROPE, heads(kpe[:, t, :], ROPE), 8, 0)]
                    if t < T:
                        parts += [(heads(gq[:, t, :], GD), 0, 8, 2 * QK, GD, heads(gq[:, t, :], GD), 16, 32)]
                    return parts

                def parts_b(t):
                    parts = [(kfull[:, t, :, 0:NOPE], 19, 27, QK, NOPE, kfull[:, t, :, 0:NOPE], 0, 0)]
                    if t < T:
                        parts += [(q_tm[:, t, :, 0:NOPE], 11, 19, 0, NOPE, q_tm[:, t, :, 0:NOPE], 0, 0),
                                  (q_tm[:, t, :, NOPE:QK], 27, 35, NOPE, ROPE, q_tm[:, t, :, NOPE:QK], 8, 0)]
                    return parts
                squares = [0]

                def statistics(parts):
                    for t in range(NT):
                        if parts is parts_b:
                            for hf in range(2):
                                bank.wait_read(dve, (l, "ukv", t, hf))
                                if t < T:
                                    bank.wait_read(dve, (l, "uq", t, hf))
                        else:
                            bank.wait_read(dve, (l, "b4", t))
                            if t < T:
                                bank.wait_read(dve, (l, "b3", t))
                        for x, c0, c1, g, d, dst, f, r in parts(t):
                            at = squares[0] % 2 * HALF
                            squares[0] += 1
                            sq = heads(tmp3[:, at:at + (c1 - c0) * d], d)
                            step(TT(sq, x, x, ALU.mult))
                            ins = RED(stat[:, t, c0:c1], sq, AX, ALU.add)
                    step(ins)

                def gains(parts, t):
                    for k in range(2):
                        for x, c0, c1, g, d, dst, f, r in parts(t):
                            hs = c1 - c0
                            if k == 0:
                                ins = TT(dst, x, stat[:, t, c0:c1].unsqueeze(2).to_broadcast([P, hs, d]), ALU.mult)
                            else:
                                ins = TT(dst, dst, qkg[:, g:g + d].unsqueeze(1).to_broadcast([P, hs, d]), ALU.mult)
                        step(ins)
                    if t >= LT:
                        return ins
                    for x, c0, c1, g, d, dst, f, r in parts(t):
                        if not f:
                            continue
                        hs = c1 - c0
                        v = dst.rearrange("p h (a b f) -> p h a b f", a=2, b=2)
                        x1, x2 = v[:, :, :, 0, :], v[:, :, :, 1, :]
                        r0 = C_ROPE + t * ROPEW + r
                        cs, sn = (cst[:, r0 + k * 2 * f:r0 + (k + 1) * 2 * f].rearrange("p (a f) -> p a f", f=f).unsqueeze(1)
                                  .to_broadcast([P, hs, 2, f]) for k in range(2))
                        tt = [ropt[:, k, 0:hs * 2 * f].rearrange("p (h a f) -> p h a f", a=2, f=f) for k in range(4)]
                        TT(tt[0], x1, cs, ALU.mult)
                        TT(tt[1], x2, sn, ALU.mult)
                        TT(tt[2], x2, cs, ALU.mult)
                        step(TT(tt[3], x1, sn, ALU.mult))
                        TT(x1, tt[0], tt[1], ALU.subtract)
                        ins = TT(x2, tt[2], tt[3], ALU.add)
                        step(ins)

                def conv_branch(hf):
                    for t in range(T):
                        key = (l, "o", 1, hf, t)
                        bank.wait_read(dve, (l, "g", 1, hf, t))
                        bank.wait_full(dve, key)
                        dst = merged[:, t, hf * HALF:(hf + 1) * HALF]
                        bank.read(TT(dst, pb(key)[:], dst, ALU.mult), key)

                step(dve.memset(stat[:], 1.0))
                statistics(parts_a)
                TS(stat[:, :, 0:10], stat[:, :, 0:10], 1.0 / GD, EPS, ALU.mult, ALU.add)
                TS(stat[:, :, 10:HEAD_A], stat[:, :, 10:HEAD_A], 1.0 / ROPE, EPS, ALU.mult, ALU.add).then_inc(s["st"], 1)
                dve.wait_ge(s["st"], 2)
                step(dve.reciprocal(stat[:, :, 0:HEAD_A], stat[:, :, 0:HEAD_A]))
                for t in range(NT):
                    gains(parts_a, t)
                dve.sem_inc(s["nrm"], 1)
                statistics(parts_b)
                TS(stat[:, :, HEAD_A:27], stat[:, :, HEAD_A:27], 1.0 / NOPE, EPS, ALU.mult, ALU.add)
                TS(stat[:, :, 27:35], stat[:, :, 27:35], 1.0 / ROPE, EPS, ALU.mult, ALU.add).then_inc(s["st"], 1)
                conv_branch(0)
                dve.wait_ge(s["st"], 4)
                step(dve.reciprocal(stat[:, :, HEAD_A:35], stat[:, :, HEAD_A:35]))
                for t in range(NT):
                    ins = dve.tensor_copy(kfull[:, t, :, NOPE:QK], kpe[:, t, :].unsqueeze(1).to_broadcast([P, H, ROPE]))
                for t in range(NT):
                    gains(parts_b, t)
                dve.sem_inc(s["nrm"], 1)
                conv_branch(1)

                U = attn_units(l)
                for kind in ("gqa", "mla"):
                    d = QK if kind == "mla" else GD
                    for i, stage in attn_order(l, kind):
                        key = (l, kind, stage, i)
                        if stage == "head":
                            key = (l, kind, "qT", i)
                            bank.wait_full(dve, key)
                            bank.read(dve.tensor_copy(headT[0:d, i % 2, 0, 0:T * P], pb(key)[0:d, 0:T * P]), key)
                            continue
                        h, t = U[i]
                        n = keys_of[t][1] - keys_of[t][0]
                        if stage == "s":
                            bank.wait_full(dve, key)
                            step(dve.reduce_max(mxs[:, i % 4:i % 4 + 1], pb(key)[:, 0:n * P], AX))
                            TS(nmax[:, i % 4:i % 4 + 1], mxs[:, i % 4:i % 4 + 1], -float(d) ** -0.5, None, ALU.mult).then_inc(s["nmax"], 1)
                        elif stage == "pv":
                            bank.wait_read(dve, (l, kind, "s", i))
                            step(dve.reciprocal(rinv[:, i % 4:i % 4 + 1], rsum[:, i % 4:i % 4 + 1]))
                            bank.wait_full(dve, key)
                            if kind == "mla" and i == 0:
                                bank.wait_full(dve, (l, "gqa", "oT", 3))
                            bank.read(TS(o_tm[:, t, h * VD:(h + 1) * VD], pb(key)[:, 0:VD], rinv[:, i % 4:i % 4 + 1], None, ALU.mult), key)

                i = 0
                for b in MERGE:
                    for hf in range(2):
                        for t in range(T):
                            key = (l, "o", b, hf, t)
                            bank.wait_full(dve, key)
                            bank.wait_read(dve, (l, "g", b, hf, t))
                            dst = merged[:, t, hf * HALF:(hf + 1) * HALF]
                            bank.read(TT(tmp[:], pb(key)[:], sgt[:, i % 2, :], ALU.mult), key)
                            bank.wait_read(dve, key)
                            ins = TT(dst, dst, tmp[:], ALU.add)
                            if b == MERGE[-1]:
                                ins.then_inc(s["mg"], 1)
                                dve.wait_ge(s["mg"], hf * T + t + 1)
                            else:
                                step(ins)
                            i += 1
                def free2(k, t):
                    if t >= 2:
                        bank.wait_full(dve, (k, "h2", t - 2, 1))
                        dve.wait_ge(s["h2o"], 32)
                dve.wait_ge(s["rows2"], 16 * (T // LT))
                for hf in range(2):
                    if hf:
                        scales(l, "rows3", 16 * (3 if T <= LT else 5), T // LT)
                    for t in range(T):
                        key = (l, "w", hf, t)
                        bank.wait_full(dve, key)
                        cols = slice(hf * HALF, (hf + 1) * HALF)
                        bank.read(TT(tmp[:], pb(key)[:], rowG[:, t // LT, cols], ALU.mult), key)
                        bank.wait_read(dve, key)
                        ins = TT(x_sb[:, t, cols], x_sb[:, t, cols], tmp[:], ALU.add)
                        ins.then_inc(s["xm"], 1)
                        dve.wait_ge(s["xm"], hf * T + t + 1)
                        if hf and t:
                            mean(l, NT + t - 1, t - 1)
                            normalise(l, NT + t - 1, t - 1, free2, "h2")
                mean(l, NT + T - 1, T - 1)
                normalise(l, NT + T - 1, T - 1, free2, "h2")

                def modulation(js):
                    if l + 1 < DEPTH:
                        for j in js:
                            key = (l, "mod", j)
                            bank.wait_full(dve, key)
                            cols = mods[0:2, j * HALF:(j + 1) * HALF]
                            bank.read(TT(cols, pb(key)[0:2, :], cols, ALU.add), key)
                dve.wait_ge(s_bias, 32 if l + 1 < DEPTH else 16)
                modulation([0, 1])

                dve.wait_ge(s["rcst"], 16)
                key = (l, "router")
                bank.wait_read(dve, key)
                slots = [2]
                W = T * NE

                def r(n_=1):
                    k = slots[0]
                    slots[0] += n_
                    return r1[:, k:k + n_, :].rearrange("p k n -> p (k n)")

                def te(x, k=T):
                    return x[:, 0:k * NE].rearrange("p (t e) -> p t e", e=NE)

                def bc(x, n_, w_):
                    return x[:, 0:n_].unsqueeze(2).to_broadcast([P, n_, w_])

                sc = r1[:, R_S, :]
                sel = r()
                dve.tensor_copy(toku[:, 0:NT], rcst[:, R_TOK:R_TOK + NT])
                step(TT(te(sel), te(sc), qkg[:, 2 * QK + 2 * GD:2 * QK + 2 * GD + NE].unsqueeze(1).to_broadcast([P, T, NE]), ALU.add))
                G4 = T * NG
                sp_ = sel[:, 0:W].rearrange("p (g q) -> p g q", q=2)
                mx, mn, a1, a2, a3, a4, gs, gm, k1, k2 = (r() for _ in range(10))
                pr = lambda x: x[:, 0:2 * G4].rearrange("p (g q) -> p g q", q=2)
                TT(mx[:, 0:2 * G4].unsqueeze(2), sp_[:, :, 0:1], sp_[:, :, 1:2], ALU.max)
                step(TT(mn[:, 0:2 * G4].unsqueeze(2), sp_[:, :, 0:1], sp_[:, :, 1:2], ALU.min))
                TT(a1[:, 0:G4].unsqueeze(2), pr(mx)[:, :, 0:1], pr(mx)[:, :, 1:2], ALU.max)
                TT(a2[:, 0:G4].unsqueeze(2), pr(mx)[:, :, 0:1], pr(mx)[:, :, 1:2], ALU.min)
                step(TT(a3[:, 0:G4].unsqueeze(2), pr(mn)[:, :, 0:1], pr(mn)[:, :, 1:2], ALU.max))
                step(TT(a4[:, 0:G4], a2[:, 0:G4], a3[:, 0:G4], ALU.max))
                step(TT(gs[:, 0:G4], a1[:, 0:G4], a4[:, 0:G4], ALU.add))

                def first_largest(out_, x, n_, w_, rev):
                    v = lambda y: y[:, 0:n_ * w_].rearrange("p (n w) -> p n w", w=w_)
                    step(RED(k1[:, 0:n_], v(x), AX, ALU.max))
                    step(TT(v(k2), v(x), bc(k1, n_, w_), ALU.is_equal))
                    step(TT(v(k2), v(k2), rcst[:, rev:rev + w_].unsqueeze(1).to_broadcast([P, n_, w_]), ALU.mult))
                    step(RED(k1[:, 0:n_], v(k2), AX, ALU.max))
                    step(TT(v(out_), v(k2), bc(k1, n_, w_), ALU.is_equal))

                first_largest(gm, gs, T, NG, R_GREV)
                pen = a1
                BIG = 1e30
                grp = lambda x: x[:, 0:W].rearrange("p (g q) -> p g q", q=EG)
                TS(pen[:, 0:G4], gm[:, 0:G4], BIG, -BIG, ALU.mult, ALU.add)
                inside = r()
                step(TT(grp(inside), grp(sel), bc(gm, G4, EG), ALU.mult))
                step(TT(grp(inside), grp(inside), bc(pen, G4, EG), ALU.add))
                oh = r1[:, slots[0]:slots[0] + 2, 0:W]
                o1, o2 = r(), r()
                first_largest(o1, inside, T, NE, R_REV)
                second = r()
                step(STT(out=second[:, 0:W], in0=o1[:, 0:W], scalar=-2 * BIG, in1=inside[:, 0:W], op0=ALU.mult, op1=ALU.add))
                first_largest(o2, second, T, NE, R_REV)
                mask = r1[:, R_MASK, :]
                TT(mask[:, 0:W], o1[:, 0:W], o2[:, 0:W], ALU.add).then_inc(s["mask"], 1)
                modulation([2, 3])
                oh4 = oh.rearrange("p k (t e) -> p k t e", e=NE)
                prod = r(2)
                p4 = prod[:, 0:2 * NT * NE].rearrange("p (k n) -> p k n", k=2)[:, :, 0:W].rearrange("p k (t e) -> p k t e", e=NE)
                res = r()

                def picked(row, table):
                    for k in range(2):
                        ins = TT(p4[:, k], oh4[:, k], table, ALU.mult)
                    step(ins)
                    for k in range(2):
                        ins = RED(res[:, row * 8 + k * T:row * 8 + (k + 1) * T], p4[:, k], AX, ALU.add)
                    step(ins)
                    return res[:, row * 8:row * 8 + 2 * T]

                w_ = picked(0, te(sc))
                den = res[:, 8:8 + T]
                step(TT(den, w_[:, 0:T], w_[:, T:2 * T], ALU.add))
                step(dve.reciprocal(den, den))
                for k in range(2):
                    TT(wk[:, k, 0:T], w_[:, k * T:(k + 1) * T], den, ALU.mult)
                key = (l, "place")
                pos, cnt = r(), r()
                bank.wait_full(dve, key)
                dve.tensor_copy(pos[:, 0:W], pb(key)[:, 0:W])
                bank.read(dve.tensor_copy(cnt[:, 0:NE], pb(key)[:, NT * NE:(NT + 1) * NE]), key)
                bank.wait_read(dve, key)
                over = cnt[:, NE:2 * NE]
                step(TS(over, cnt[:, 0:NE], float(P), None, ALU.is_gt))
                step(STT(out=over, in0=cnt[:, 0:NE], scalar=float(2 * P), in1=over, op0=ALU.is_gt, op1=ALU.add))
                step(STT(out=over, in0=cnt[:, 0:NE], scalar=float(3 * P), in1=over, op0=ALU.is_gt, op1=ALU.add))
                big = r(4)
                b3 = big[:, 0:NE * NE].rearrange("p (e f) -> p e f", f=NE)
                ob, incl = cnt[:, 2 * NE:3 * NE], cnt[:, 3 * NE:4 * NE]
                step(TT(b3, rcst[:, R_LT:R_LT + NE * NE].rearrange("p (e f) -> p e f", f=NE), over.unsqueeze(1).to_broadcast([P, NE, NE]), ALU.mult))
                step(RED(ob, b3, AX, ALU.add))
                step(TT(incl, ob, over, ALU.add))
                V = incl[:, NE - 1:NE]
                fl = r()
                npair = fl[:, 0:1]
                step(TS(npair, V, 1.0, float(NE // 2), ALU.is_ge, ALU.add))
                for x in (3.0, 5.0, 7.0):
                    step(STT(out=npair, in0=V, scalar=x, in1=npair, op0=ALU.is_ge, op1=ALU.add))
                i3 = big[:, 0:8 * NE].rearrange("p (e f) -> p e f", f=NE)
                step(TT(i3, incl.unsqueeze(1).to_broadcast([P, 8, NE]), rcst[:, R_IT:R_IT + 8].unsqueeze(2).to_broadcast([P, 8, NE]), ALU.is_le))
                step(RED(fl[:, 8:16], i3, AX, ALU.add))
                TS(ni[:, NE:ITEMS], fl[:, 8:16], float(NE - 1), None, ALU.min)
                dve.tensor_copy(ni[:, 0:NE], rcst[:, R_EID:R_EID + NE])
                TS(ni[:, ITEMS + 2:ITEMS + 3], npair, 4.0, -2.0, ALU.mult, ALU.add)
                TS(ni[:, ITEMS + 3:ITEMS + 4], npair, 4.0, 2.0, ALU.mult, ALU.add)
                TS(ni[:, ITEMS + 1:ITEMS + 2], npair, 16.0, 16.0, ALU.mult, ALU.add)
                dve.tensor_copy(ni[:, ITEMS:ITEMS + 1], npair).then_inc(s["ni"], 1)
                p_ = picked(1, te(pos))
                e_ = picked(2, rcst[:, R_EID:R_EID + NE].unsqueeze(1).to_broadcast([P, T, NE]))
                b_ = picked(3, ob.unsqueeze(1).to_broadcast([P, T, NE]))
                gt, j_, it, sl = (res[:, 8 * k:8 * k + 2 * T] for k in (4, 5, 6, 7))
                step(TS(gt, p_, float(P), None, ALU.is_ge))
                step(STT(out=j_, in0=p_, scalar=float(2 * P), in1=gt, op0=ALU.is_ge, op1=ALU.add))
                step(STT(out=j_, in0=p_, scalar=float(3 * P), in1=j_, op0=ALU.is_ge, op1=ALU.add))
                step(STT(out=it, in0=j_, scalar=float(NE - 1), in1=b_, op0=ALU.add, op1=ALU.add))
                step(TT(it, it, e_, ALU.subtract))
                step(TT(it, it, gt, ALU.mult))
                step(TT(it, it, e_, ALU.add))
                step(STT(out=sl, in0=j_, scalar=-float(P), in1=p_, op0=ALU.mult, op1=ALU.add))
                for k in range(2):
                    cols = slice(k * T, (k + 1) * T)
                    STT(out=rowY[:, k, 0:T], in0=it[:, cols], scalar=float(P), in1=sl[:, cols], op0=ALU.mult, op1=ALU.add)
                    ins = STT(out=rowL[:, k, 0:T], in0=sl[:, cols], scalar=float(LISTW), in1=it[:, cols], op0=ALU.mult, op1=ALU.add)
                ins.then_inc(s["mask"], 1)
                modulation(range(4, MODB))
                if l + 1 < DEPTH:
                    for g in range(MODG):
                        dve.wait_ge(mod_out[g], 32)

                UP, X1, Y1 = ps[3], ps[5], ps[0]
                for name in ("h", "yD"):
                    dve.sem_inc(m[name], 1)
                pairs = dve.value_load(ni[0:1, ITEMS:ITEMS + 1], min_val=NE // 2, max_val=ITEMS // 2)
                dve.wait_ge(m["xt"], 2)
                dve.tensor_copy(xgT[:, 0, 4:8, :], X1[:].rearrange("p (c n) -> p c n", c=4)).then_inc(m["xtD"], 1)
                with dve.Fori(0, pairs) as q:
                    for u in range(2):
                        done = 2 * q + (u + 1)
                        dve.wait_ge(m["gu"], 4 * q + (2 * u + 2))
                        dve.wait_ge(m["sig"], done + 1)
                        TT(hh[:, u, :], UP[:], sg[:, u, :], ALU.mult).then_inc(m["h"], 1)
                        dve.wait_ge(m["xt"], 4 * q + (2 * u + 4))
                        dve.tensor_copy(xgT[:, 1 - u, 4:8, :], X1[:].rearrange("p (c n) -> p c n", c=4)).then_inc(m["xtD"], 1)
                        dve.wait_ge(m["y"], 4 * q + (2 * u + 2))
                        dve.wait_ge(m_yo[l][u], 16 * q + 16)
                        dve.tensor_copy(yg[:, u, HALF:D], Y1[:]).then_inc(m["yD"], 1)

                if l + 1 < DEPTH:
                    scales(l + 1, "rows1", 16 * 5, 2)
                dve.wait_ge(s["rows4"], 16 * (T // LT))
                for t in range(T):
                    u = t % 2
                    dve.wait_ge(m_yk[u], 32 * (l * NT // 2 + t // 2 + 1))
                    step(TS(yg[:, u, :], yg[:, u, :], wk[:, 1, t:t + 1], None, ALU.mult))
                    step(STT(out=yg[:, u, :], in0=xg[:, u, :], scalar=wk[:, 0, t:t + 1], in1=yg[:, u, :], op0=ALU.mult, op1=ALU.add))
                    step(TT(yg[:, u, :], yg[:, u, :], rowC[:, t // LT, :], ALU.mult))
                    TT(x_sb[:, t, :], x_sb[:, t, :], yg[:, u, :], ALU.add).then_inc(s["xf"], 1)
                    if l + 1 < DEPTH and t:
                        mean(l + 1, t - 1, t - 1)
                        normalise(l + 1, t - 1, t - 1, free1, "h")
                if l + 1 < DEPTH:
                    mean(l + 1, NT - 1, NT - 1)
                    normalise(l + 1, NT - 1, NT - 1, free1, "h")

        @block.gpsimd
        def _(pool):
            def spread(dst, row, done):
                pool.dma_start(dst, row.to_broadcast([dst.shape[0], row.shape[-1]])).then_inc(done, 16)

            def mod_row(l, which, r):
                return mod_d[r:r + 1, l * D_MOD + which * D:l * D_MOD + (which + 1) * D]

            def parameters(l):
                par = S[l]["par"]
                pool.dma_start(crows[0:CW, :], a["conv_w"][l]).then_inc(par, 16)
                for k, name in enumerate(("conv_b", "conv_ln_g", "conv_ln_b")):
                    pool.dma_start(crows[CW + k:CW + k + 1, :], a[name][l:l + 1, :]).then_inc(par, 16)
                spread(qkg[:, 0:QK], a["mla_q_gain"][l:l + 1, :], par)
                spread(qkg[:, QK:2 * QK], a["mla_k_gain"][l:l + 1, :], par)
                spread(qkg[:, 2 * QK:2 * QK + GD], a["gqa_q_gain"][l:l + 1, :], par)
                spread(qkg[:, 2 * QK + GD:2 * QK + 2 * GD], a["gqa_k_gain"][l:l + 1, :], par)
                if l == 0:
                    spread(qkg[:, 2 * QK + 2 * GD:], a["router_bias"].rearrange("(o e) -> o e", o=1), par)
                pool.dma_start(colg[:, 0:2].rearrange("p (k o) -> p k o", o=1), a["mla_q_norm"][l].rearrange("(k p o) -> p k o", p=P, o=1),
                               allow_slow_non_contiguous=True).then_inc(par, 16)
                pool.dma_start(colg[:, 2:3], a["mla_kv_norm"][l].rearrange("(p o) -> p o", o=1)).then_inc(par, 16)

            def rows1(l):
                spread(normg[:], a["norm1_g"][l:l + 1, :], S[l]["rows1"])
                pool.wait_ge(mod_out[0], 16 * (l + 1))
                for r in range(2):
                    spread(rowA[:, r, :], mod_row(l, 1, r), S[l]["rows1"])
                    spread(rowB[:, r, :], mod_row(l, 0, r), S[l]["rows1"])

            spread(mods[0:2, :], a["b_mod"][0:1, :], s_bias)
            parameters(0)
            pool.dma_start(rw[:], a["router_w"].rearrange("(k p) e -> p k e", p=P)).then_inc(s_zero, 16)
            pool.memset(ypad[:], 0.0).then_inc(S[0]["pad"], 1)
            rows1(0)
            pool.wait_ge(s_zset, 1)
            for l in range(DEPTH):
                pool.dma_start(list_d[l].rearrange("(p w) o -> p (w o)", p=P), zero[:]).then_inc(s_zero, 16)
                for h in range(4):
                    rows = y_d[l][(NE + 2 * h) * P:(NE + 2 * h + 2) * P, :]
                    pool.dma_start(rows.rearrange("(i p) d -> p i d", p=P), rowC[:]).then_inc(s_zero, 16)

            for l in range(DEPTH):
                T, s, m = QT[l], S[l], M[l]
                n = T // LT
                bank.wait_full(pool, (l, "mla", "oT", 3))
                for g in range(1, MODG):
                    pool.wait_ge(mod_out[g], 16 * (l + 1))
                for r in range(n):
                    spread(rowG[:, r, :], mod_row(l, 2, r), s["rows2"])
                spread(normg[:], a["norm2_g"][l:l + 1, :], s["rows3"])
                bank.wait_full(pool, (l, "mT", T - 1, 1))
                for r in range(n):
                    spread(rowB[:, r, :], mod_row(l, 3, r), s["rows3"])
                    spread(rowA[:, r, :], mod_row(l, 4, r), s["rows3"])
                pool.wait_ge(s["xm"], 2 * T)
                pool.dma_start(rcst[:], consts[:, C_ALL:C_ALL + R_ALL]).then_inc(s["rcst"], 16)
                if l + 1 < DEPTH:
                    spread(mods[0:2, :], a["b_mod"][l + 1:l + 2, :], s_bias)
                    parameters(l + 1)
                pool.wait_ge(s["mask"], 2)
                pool.wait_ge(s_zero, ZEROED)
                for t in range(T):
                    for k in range(2):
                        pool.indirect_dma_start(list_d[l], bass.IndirectOffsetOnAxis(ap=rowL[:, k, t:t + 1], axis=0), toku[:, t:t + 1], None).then_inc(s["scat"], 16)
                pool.wait_ge(s["scat"], 32 * T)
                pool.wait_ge(s["h2o"], 16 * T)
                pool.dma_start(lst[:], list_d[l].rearrange("(p w) o -> p (w o)", p=P)).then_inc(s["scat"], 16)
                pool.wait_ge(s["scat"], 32 * T + 16)
                pool.wait_ge(s["ni"], 1)
                pairs = pool.value_load(ni[0:1, ITEMS:ITEMS + 1], min_val=NE // 2, max_val=ITEMS // 2)
                stored = pool.value_load(ni[0:1, ITEMS + 1:ITEMS + 2], min_val=16, max_val=16 * ITEMS)

                def gather(u):
                    pool.indirect_dma_start(xg[:, u, :], None, h2_d[l], bass.IndirectOffsetOnAxis(ap=cur[:, u, 0:1], axis=0)).then_inc(m_xg[l][u], 16)

                def take(u, col):
                    return pool.tensor_copy(cur[:, u, 0:1], lst[:, col])
                for u in range(2):
                    take(u, slice(u, u + 1)).then_inc(m["cur"], 1)
                pool.wait_ge(m["cur"], 2)
                gather(0)
                if l + 1 < DEPTH:
                    for g in range(MODG):
                        pool.wait_ge(mod_out[g], 32)
                gather(1)
                if l + 1 < DEPTH:
                    pool.wait_ge(s["h2"], T)
                    rows1(l + 1)
                with pool.Fori(4, 2 * pairs + 2, 2) as i:
                    pool.wait_ge(m["xt"], 2 * i - 4)
                    for u in range(2):
                        take(u, bass.ds(i - 2 + u, 1)).then_inc(m["cur"], 1)
                    for u in range(2):
                        pool.wait_ge(s["ni"], 1)
                        pool.wait_ge(m["cur"], i)
                        gather(u)
                before_last = pool.value_load(ni[0:1, ITEMS + 2:ITEMS + 3], min_val=1, max_val=4 * ITEMS)
                pool.wait_ge(s["ni"], 1)
                pool.wait_ge(m["xt"], before_last)
                gather(0)
                pool.wait_ge(s["ni"], 1)
                pool.wait_ge(m["gu"], before_last)
                for r in range(n):
                    spread(rowC[:, r, :], mod_row(l, 5, r), s["rows4"])
                if l + 1 < DEPTH:
                    pool.memset(ypad[:], 0.0).then_inc(S[l + 1]["pad"], 1)
                all_xt = pool.value_load(ni[0:1, ITEMS + 3:ITEMS + 4], min_val=1, max_val=4 * ITEMS)
                for t in range(T):
                    u = t % 2
                    pool.wait_ge(s["ni"], 1)
                    if t == 0:
                        for v in range(2):
                            pool.wait_ge(m_yo[l][v], stored)
                        pool.wait_ge(m["xt"], all_xt)
                    if t >= 2:
                        pool.wait_ge(s["xf"], t - 1)
                    for k, dst in ((0, xg), (1, yg)):
                        pool.indirect_dma_start(dst[:, u, :], None, y_d[l], bass.IndirectOffsetOnAxis(ap=rowY[:, k, t:t + 1], axis=0)).then_inc(m_yk[u], 16)


_INS = ["x", "c", "ctx", "c_ctx", "w_mod", "b_mod", "norm1_g", "norm2_g", "w_in", "mla_q_norm", "mla_kv_norm", "mla_w_uq",
        "mla_w_ukv", "mla_q_gain", "mla_k_gain", "mla_w_o", "conv_w", "conv_b", "conv_ln_g", "conv_ln_b", "conv_w_o",
        "gqa_q_gain", "gqa_k_gain", "gqa_w_o", "w_out", "router_w", "router_bias", "moe_w_gate", "moe_w_up", "moe_w_down"]


def constants():
    import numpy as np

    f = np.float32
    t = np.zeros((P, C_ALL + R_ALL), f)
    t[:, C_ID:C_ID + P] = np.eye(P, dtype=f)
    n = np.arange(SEQ)
    for tile in range(LT):
        rows = slice(tile * P, (tile + 1) * P)
        at = C_ROPE + tile * ROPEW
        for dim in (ROPE // 2, GD // 2):
            inv = (f(10000.0) ** (-np.arange(0, dim, 2, dtype=f) / f(dim))).astype(f)
            ang = np.concatenate([pos[:, None].astype(f) * inv[None, :] for pos in (n // GRID_W, n % GRID_W)], axis=1)
            for fn in (np.cos, np.sin):
                t[:, at:at + dim] = fn(ang[rows]).astype(f)
                at += dim
    r = t[:, C_ALL:]
    r[:, R_TRI:R_TRI + P] = np.triu(np.ones((P, P), f), 1)
    r[:, R_ONES:R_ONES + P] = 1
    r[:, R_TOK:R_TOK + NT] = np.arange(P)[:, None] + P * np.arange(NT)[None, :]
    r[:, R_EID:R_EID + NE] = np.arange(NE)
    r[:, R_REV:R_REV + NE] = NE - np.arange(NE)
    r[:, R_GREV:R_GREV + NG] = NG - np.arange(NG)
    r[:, R_IT:R_IT + 8] = np.arange(8)
    r[:, R_LT:R_LT + NE * NE] = np.tril(np.ones((NE, NE), f), -1).reshape(-1)
    return t


def kernel(**inputs):
    import numpy as _np
    import concourse.bacc as _bacc
    from concourse.bass_utils import run_bass_kernel_spmd as _run

    nc = _bacc.Bacc("TRN2", target_bir_lowering=False, num_devices=1)
    arrays, aps = {}, {}
    for name in _INS:
        v = _np.ascontiguousarray(inputs[name])
        arrays[f"in_{name}"] = v
        aps[name] = nc.dram_tensor(f"in_{name}", v.shape, mybir.dt.from_np(v.dtype), kind="ExternalInput").ap()
    v = constants()
    arrays["constants"] = v
    consts = nc.dram_tensor("constants", v.shape, F32, kind="ExternalInput").ap()
    out = nc.dram_tensor("out", (1, SEQ, D), F32, kind="ExternalOutput").ap()
    backbone(nc, aps, consts, out)
    return _run(nc, [arrays], core_ids=[0]).results[0]["out"]
```

```python
from contextlib import ExitStack

import concourse.bass as bass
from concourse import mybir

P = 128
D, SEQ, CTX, DEPTH = 1024, 256, 256, 2
LT, CT = SEQ // P, CTX // P
NT = LT + CT
KC = D // P
D_MOD = 6 * D
QR, KVR, ROPE, NOPE, VD, H = 256, 128, 32, 64, 64, 8
QK = NOPE + ROPE
CC, CW = 512, 31
GH, GKV, GD = 8, 2, 64
NE, NG, EG, F = 16, 4, 4, 512
GRID_W = 64
EPS = 1e-6
HALF = 512
COL_CQ, COL_CONV, COL_GQ = 0, QR + KVR + ROPE, QR + KVR + ROPE + 2 * CC
COL_GK = COL_GQ + GH * GD
COL_GATE = COL_GK + 2 * GKV * GD
W_CQKV = QR + KVR + ROPE
ITEMS = 24
LISTW = ITEMS + 2
PADW = SEQ + CW - 1

ZEROED = 16 * 5
HEAD_A = GH + GKV + 1

F32 = mybir.dt.float32
I32 = mybir.dt.int32
U32 = mybir.dt.uint32
ALU = mybir.AluOpType
ACT = mybir.ActivationFunctionType
AX = mybir.AxisListType.X

C_ID, C_ROPE = 0, 128
ROPEW = 2 * (2 * 8) + 2 * (2 * 16)
C_ALL = C_ROPE + LT * ROPEW
R_S, R_MASK = 0, 1
R_TRI, R_ONES, R_TOK, R_EID, R_REV, R_GREV, R_IT, R_LT = 0, 128, 256, 260, 276, 292, 296, 304
R_ALL = R_LT + NE * NE


MODB, MODG = D_MOD // HALF, D_MOD // HALF // 4
MODSLOT = (1, 2, 3, 0)
RING = (0, 2)
MERGE = (2, 0)
MSLOT = (4, 5, 1, 2, 3, 0)


class Banks:

    def __init__(self, full, free):
        self.full, self.free = full, free
        self.uses = [0] * len(full)
        self.turn = {}
        self.at = {}

    def plan(self, key, banks):
        n = self.turn.get(banks, 0)
        self.turn[banks] = n + 1
        b = banks[n % len(banks)]
        self.at[key] = (b, self.uses[b])
        self.uses[b] += 1

    def wait_free(self, eng, key):
        b, k = self.at[key]
        if k:
            eng.wait_ge(self.free[b], k)

    def wait_full(self, eng, key):
        b, k = self.at[key]
        eng.wait_ge(self.full[b], k + 1)

    def wait_read(self, eng, key):
        b, k = self.at[key]
        eng.wait_ge(self.free[b], k + 1)

    def filled(self, ins, key):
        ins.then_inc(self.full[self.at[key][0]], 1)

    def read(self, ins, key):
        ins.then_inc(self.free[self.at[key][0]], 1)


def backbone(nc, a, consts, out):
    with ExitStack() as ctx:
        sem = lambda n: ctx.enter_context(nc.semaphore(n))
        ps = [ctx.enter_context(nc.psum_tensor(f"bank{i}", [P, HALF], F32)) for i in range(8)]
        base = (nc.sbuf_base + 63) // 64 * 64

        def sb(name, at, shape, dt=F32):
            return nc.alloc_sbuf_tensor_at(name, [P, *shape], dt, offset=base + 4 * at)

        slab = [sb(f"slab{s}", 4096 * s, [8, HALF]) for s in range(6)]
        o = 16384
        ybuf = sb("ybuf", o, [NT, CC])
        ypad = sb("ypad", o + 2048, [4, 2, PADW])
        cv = sb("cv", o + 2048 + 8 * PADW, [4, 2, SEQ])
        q_tm = sb("q_tm", o, [NT, H, QK])
        kfull = sb("kfull", o + 3072, [NT, H, QK])
        o += 2048 + 8 * PADW + 2048
        v_tm = sb("v_tm", o, [NT, H * VD])
        terms_a = sb("terms_a", o, [4, 2, SEQ])
        oT_mla = sb("oT_mla", o, [4, NT * P])
        o += 2048
        x_sb = sb("x_sb", o, [NT, D]); o += 4096
        hT = sb("hT", o, [KC, NT * P]); o += 4096
        rowA = sb("rowA", o, [2, D])
        rowB = sb("rowB", o + 2048, [2, D])
        merged = sb("merged", o, [NT, D]); o += 4096
        m0 = o
        cqkv = sb("cqkv", o, [NT, W_CQKV])
        normg = sb("normg", o, [D]); o += 4 * W_CQKV
        gkv = sb("gkv", o, [NT, 2 * GKV * GD]); o += 1024
        gq = sb("gq", o, [NT, GH * GD])
        oT_gqa = sb("oT_gqa", o, [4, NT * P]); o += 2048
        zT = sb("zT", o, [4, NT * P])
        terms_b = sb("terms_b", o, [4, 2, SEQ]); o += 2048
        o_tm = sb("o_tm", o, [NT, H * VD])
        rowG = sb("rowG", o, [2, D]); o += 2048
        headT = sb("headT", o, [2, 2, NT * P])
        htile = sb("htile", o, [2, D]); o += 2048
        prob = sb("prob", o, [2, HALF])
        probT = sb("probT", o + 1024, [2, 4, P])
        cT = sb("cT", o, [3, NT * P])
        junk = sb("junk", o, [D]); o += 2048
        sgt = sb("sgt", o, [2, HALF])
        tmp = sb("tmp", o + 1024, [HALF])
        tmp3 = sb("tmp3", o, [1536]); o += 1536
        rcst = sb("rcst", m0 + D, [R_ALL])

        def small(name, shape):
            nonlocal o
            t = sb(name, o, shape)
            n = 1
            for d in shape:
                n *= d
            o += (n + 7) // 8 * 8
            return t

        cst = small("cst", [C_ALL])
        qkg = small("qkg", [2 * QK + 2 * GD + NE])
        colg = small("colg", [3])
        crows = small("crows", [CC])
        convc = small("convc", [4, CW + 3])
        sT = small("sT", [2 * KC])
        ssum = small("ssum", [3, NT])
        wk = small("wk", [2, NT])
        rw = small("rw", [KC, NE])
        rowY = sb("rowY", o, [2, NT], U32)
        rowL = sb("rowL", o + 8, [2, NT], U32)
        toku = sb("toku", o + 16, [NT], U32)
        ni = sb("ni", o + 24, [32], I32)
        cur = sb("cur", o + 56, [2, 8], U32)
        o += 72
        rinv = small("rinv", [4])
        mxs = small("mxs", [4])
        warm = small("warm", [1])
        cstat = small("cstat", [NT, 2])
        nmax = small("nmax", [4])
        rsum = small("rsum", [8])
        zero = sb("zero", o, [LISTW], U32)
        lst = sb("lst", o, [LISTW], U32)
        o += 32
        assert base + 4 * o <= nc.sbuf_usable_end, (base + 4 * o - nc.sbuf_usable_end)
        e = m0 + 4 * W_CQKV
        xg = sb("xg", e, [2, D]); e += 2048
        yg = sb("yg", e, [2, D]); e += 2048
        xgT = sb("xgT", e, [2, KC, P]); e += 2048
        sg = sb("sg", e, [2, F]); e += 1024
        hh = sb("hh", e, [2, F]); e += 1024
        hhT = sb("hhT", e, [2, 4, P]); e += 1024
        r1 = sb("r1", e, [32, NT * NE]); e += 2048
        mods = sb("mods", m0 + 4 * W_CQKV + 1024, [D_MOD])
        crow = sb("crow", m0 + 4 * W_CQKV + 1024 + 3 * 2048, [P])
        csig = sb("csig", m0 + 4 * W_CQKV + 1024 + 3 * 2048 + P, [2 * KC])
        rowC = sb("rowC", 16384, [2, D])
        xg2 = sb("xg2", 16384 + 2048 + 8 * PADW, [2, D])
        yg2 = sb("yg2", 16384 + 4096 + 8 * PADW, [2, D])
        chosen = [(xg[:, t % 2, :], yg[:, t % 2, :]) if t < 2 else (xg2[:, t % 2, :], yg2[:, t % 2, :]) for t in range(NT)]
        ropt = sb("ropt", m0 + 4 * W_CQKV + 1024 + 2048 + 2048 + 256, [4, 256])
        kpe = sb("kpe", m0 + 4 * W_CQKV + 1024 + 2048 + 2048 + 1280, [NT, ROPE])
        stat = sb("stat", m0 + 4 * W_CQKV + 1024 + 2048 + 2048, [NT, 35])
        bnst = sb("bnst", m0 + 4 * W_CQKV + 1024 + 2048 + 2048 + 144, [NT, 8])
        mv = sb("mv", m0 + 4 * W_CQKV + 1024 + 2048 + 2048 + 176, [NT, 2])

        mod_d = nc.dram_tensor("mod_d", [2, DEPTH * D_MOD], F32, kind="Internal").ap()
        list_d = [nc.dram_tensor(f"list_d{l}", [P * LISTW, 1], U32, kind="Internal").ap() for l in range(DEPTH)]
        h2_d = [nc.dram_tensor(f"h2_d{l}", [(NT, LT)[l] * P, D], F32, kind="Internal").ap() for l in range(DEPTH)]
        y_d = [nc.dram_tensor(f"y_d{l}", [ITEMS * P, D], F32, kind="Internal").ap() for l in range(DEPTH)]

        ident = cst[:, C_ID:C_ID + P]

        bank = Banks([sem(f"bank_full{i}") for i in range(8)], [sem(f"bank_read{i}") for i in range(8)])
        s_cst, s_c, s_x, s_zero, s_out = sem("s_cst"), sem("s_c"), sem("s_x"), sem("s_zero"), sem("s_out")
        slab_in = [sem(f"slab_in{i}") for i in range(4)]
        mod_in = [sem(f"mod_in{i}") for i in range(4)]
        mod_full, mod_read = sem("mod_full"), sem("mod_read")
        mod_out = [sem(f"mod_out{i}") for i in range(MODG)]
        s_bias = sem("s_bias")
        s_silu_c, s_zset = sem("s_silu_c"), sem("s_zset")
        dve_step, act_step, pool_step = sem("dve_step"), sem("act_step"), sem("pool_step")
        names = ["term", "pad", "sq", "sqm", "sqrt", "rows1", "rows2", "rows3", "rows4", "par", "h", "csq", "cn", "st", "nrm",
                 "nmax", "cvd", "lnv", "lns", "mg", "xm", "h2", "h2o", "rcst", "mask", "ni", "xf", "scat"]
        S = [{n: sem(f"{n}{l}") for n in names} for l in range(DEPTH)]
        mnames = ["gu", "sig", "h", "xt", "xtA", "xtD", "ht", "htA", "y", "yA", "yD", "cur"]
        M = [{n: sem(f"moe_{n}{l}") for n in mnames} for l in range(DEPTH)]
        m_in = [[sem(f"moe_in{l}_{i}") for i in range(6)] for l in range(DEPTH)]
        m_xg = [[sem(f"moe_xg{l}_{i}") for i in range(2)] for l in range(DEPTH)]
        m_yo = [[sem(f"moe_yo{l}_{i}") for i in range(2)] for l in range(DEPTH)]
        m_yk = [sem(f"moe_yk{i}") for i in range(NT)]

        def term(w):
            return (terms_a, terms_b)[w // 4 % 2][:, w % 4]

        QT = [NT, LT]
        T_LAST = [T - 1 for T in QT]
        keys_of = [(0, NT) if t < LT else (LT, NT) for t in range(NT)]

        def slabs(l):
            T = QT[l] - 1

            def win(c0, w):
                return [(w_cols(a["w_in"][l], c0, w), w)]
            def gates(b):
                for hf in range(2):
                    yield f"g{b}{hf}", win(COL_GATE + b * D + hf * HALF, HALF), (l, "g", b, hf, T)

            def branch(b):
                w = a[("mla_w_o", "conv_w_o", "gqa_w_o")[b]]
                yield f"o{b}", [(w[l].rearrange("(k p) n -> p k n", p=P), None)], (l, "o", b, 1, T)
            yield "b1", win(COL_CONV, CC), (l, "b1", T)
            yield "b2", win(COL_CONV + CC, CC), (l, "b2", T)
            yield "b0", win(COL_CQ, W_CQKV), (l, "b0", NT - 1)
            yield "b4", win(COL_GK, 2 * GKV * GD), (l, "b4", NT - 1)
            yield "b3", win(COL_GQ, GH * GD), (l, "b3", T)
            yield from gates(1)
            yield "up", None, (l, "ukv", NT - 1, 1)
            yield from branch(1)
            for b in MERGE:
                yield from branch(b)
                yield from gates(b)
            for hf in range(2):
                yield f"w{hf}", [(w_cols(a["w_out"][l], hf * HALF, HALF), HALF)], (l, "w", hf, T)

        def w_cols(w, c0, n):
            return w[:, c0:c0 + n].rearrange("(k p) n -> p k n", p=P)

        slab_plan, slab_at = [], {}
        for l in range(DEPTH):
            for n, (name, src, last) in enumerate(slabs(l)):
                loads = 2 if name == "up" else 1
                slot = (n + RING[l]) % 4
                before = sum(q[4] for q in slab_plan if q[3] == slot)
                slab_plan.append((l, name, src, slot, loads, last))
                slab_at[l, name] = (slot, 16 * (before + loads))

        def wait_slab(eng, l, name):
            slot, v = slab_at[l, name]
            eng.wait_ge(slab_in[slot], v)
            return slab[slot]

        lo, hi = (0, 1, 2, 3), (4, 5, 6, 7)

        def attn_units(l):
            return [(h, t) for h in range(H) for t in range(QT[l])]

        def plan_layer(l):
            T = QT[l]
            for t in range(T):
                for hf in range(2):
                    bank.plan((l, "h", t, hf), hi)
            for t in range(T):
                bank.plan((l, "b1", t), lo)
                bank.plan((l, "b2", t), hi)
            for t in range(T, NT):
                for hf in range(2):
                    bank.plan((l, "h", t, hf), hi)
            bank.plan((l, "conv_cols"), hi)
            for t in range(NT):
                bank.plan((l, "b0", t), lo)
            for c in range(4):
                bank.plan((l, "yT", c), hi)
            for t in range(NT):
                bank.plan((l, "b4", t), hi)
            for t in range(T):
                bank.plan((l, "b3", t), lo)
            for t in range(T):
                bank.plan((l, "g", 1, 0, t), lo)
            for c in range(3):
                bank.plan((l, "cT", c), hi)
            for t in range(T):
                bank.plan((l, "cvb", t), hi)
            for t in range(T):
                bank.plan((l, "g", 1, 1, t), lo)
            for c in range(4):
                bank.plan((l, "zT", c), hi)
            for t in range(NT):
                if t < T:
                    bank.plan((l, "uq", t, 0), lo)
                    bank.plan((l, "uq", t, 1), lo)
                bank.plan((l, "ukv", t, 0), lo)
                bank.plan((l, "ukv", t, 1), lo)
            for hf in range(2):
                for t in range(T):
                    bank.plan((l, "o", 1, hf, t), hi)
            for kind in ("gqa", "mla"):
                for i, step in attn_order(l, kind):
                    if step == "head":
                        bank.plan((l, kind, "qT", i), (0, 1))
                        if kind == "mla" or i % 4 == 0:
                            bank.plan((l, kind, "kT", i), (0, 1))
                    else:
                        bank.plan((l, kind, step, i), {"s": (2, 3), "pT": (4, 5), "pv": (6, 7)}[step])
                for c in range(4):
                    bank.plan((l, kind, "oT", c), hi)
            for b in MERGE:
                for hf in range(2):
                    for t in range(T):
                        bank.plan((l, "o", b, hf, t), lo)
                        bank.plan((l, "g", b, hf, t), hi)
            for hf in range(2):
                for t in range(T):
                    bank.plan((l, "mT", t, hf), hi)
            for hf in range(2):
                for t in range(T):
                    bank.plan((l, "w", hf, t), lo)
            for t in range(T):
                for hf in range(2):
                    bank.plan((l, "h2", t, hf), (4, 5))
            bank.plan((l, "router"), (0,))
            bank.plan((l, "place"), (1,))
            if l + 1 < DEPTH:
                for j in range(MODB):
                    bank.plan((l, "mod", j), (2, 3, 6, 7))

        def par_count(l):
            return 16 * (11 if l == 0 else 10)

        def attn_order(l, kind, scores_last=False):
            U = attn_units(l)
            yield 0, "head"
            for i in range(len(U) + 3):
                if i + 1 < len(U) and U[i + 1][1] == 0:
                    yield U[i + 1][0], "head"
                if i < len(U) and not scores_last:
                    yield i, "s"
                if 2 <= i <= len(U) + 1:
                    yield i - 2, "pT"
                if i < len(U) and scores_last:
                    yield i, "s"
                if i >= 3:
                    yield i - 3, "pv"

        for l in range(DEPTH):
            plan_layer(l)

        def load_expert(sp, l, slot, kind, w):
            src = w.rearrange("o (k p) n -> p (o k) n", p=P)
            dst = slab[slot][:] if kind < 2 else slab[slot][:].rearrange("p (k j) n -> p k (j n)", k=4)
            sp.dma_start(dst, src).then_inc(m_in[l][slot], 16)

        def store_item(sp, l, m, u, item):
            sp.wait_ge(m["yA"], item + 2)
            sp.wait_ge(m["yD"], item + 2)
            sp.dma_start(y_d[l][bass.ds(item * P, P), :], yg[:, u, :]).then_inc(m_yo[l][u], 16)

        block = ctx.enter_context(nc.Block())

        @block.sync
        def _(sp):
            sp.dma_start(cst[:], consts[:, 0:C_ALL]).then_inc(s_cst, 16)
            sp.dma_start(crow[0:KC, :], a["c"].rearrange("o (k p) -> (o k) p", p=P)).then_inc(s_c, 16)
            sp.dma_start(crow[KC:2 * KC, :], a["c_ctx"].rearrange("(k p) -> k p", p=P)).then_inc(s_c, 16)
            w_v = a["w_mod"][0].rearrange("(k p) n -> p k n", p=P)
            with sp.Fori(0, MODG) as i:
                for u in range(4):
                    sp.wait_ge(mod_read, 4 * i + (u + 1))
                    sp.dma_start(slab[u][:], w_v[:, :, bass.ds((4 * i + u) * HALF, HALF)]).then_inc(mod_in[u], 16)
            def load_slab(l, n):
                mine = [q for q in slab_plan if q[0] == l]
                _, name, src, slot, loads, last = mine[n]
                if n >= 4:
                    bank.wait_full(sp, mine[n - 4][5])
                elif l == 0:
                    sp.wait_ge(mod_full, 1 + MODB - 4 + slot + 1)
                elif n == 1:
                    for t in range(NT):
                        sp.wait_ge(m_yk[t], 32 * l)
                if name == "up":
                    flat = slab[slot][:].rearrange("p k n -> p (k n)")
                    uq = a["mla_w_uq"][l].rearrange("(k p) n -> p k n", p=P)
                    sp.dma_start(flat[:, 0:2 * H * QK].rearrange("p (k n) -> p k n", k=2), uq).then_inc(slab_in[slot], 16)
                    sp.dma_start(flat[:, 2 * H * QK:2 * H * QK + H * (NOPE + VD)], a["mla_w_ukv"][l]).then_inc(slab_in[slot], 16)
                    return
                ap, w = src[0]
                if w is None:
                    dst = slab[slot][:].rearrange("p (k j) n -> p k (j n)", k=4)
                else:
                    dst = slab[slot][:, :, 0:w]
                sp.dma_start(dst, ap).then_inc(slab_in[slot], 16)

            for l in range(DEPTH):
                mine = [q for q in slab_plan if q[0] == l]
                for n in range(len(mine)):
                    if l == 0 or n:
                        load_slab(l, n)

                m = M[l]

                def load_item(u, e):
                    for kind, w in enumerate(("moe_w_gate", "moe_w_up", "moe_w_down")):
                        yield kind, MSLOT[3 * u + kind], a[w][l][e]

                slot_last = {q[3]: q[5] for q in mine}
                slot_last[4] = slot_last[5] = (l, "o", MERGE[-1], 1, T_LAST[l])
                for u in range(2):
                    for kind, slot, w in load_item(u, slice(u, u + 1)):
                        bank.wait_full(sp, slot_last[slot])
                        load_expert(sp, l, slot, kind, w)
                        if (u, kind) == (0, 1) and l + 1 < DEPTH:
                            w_v = a["w_mod"][l + 1].rearrange("(k p) n -> p k n", p=P)
                            for j in range(MODB):
                                at = MODSLOT[j % 4]
                                bank.wait_full(sp, slot_last[at])
                                sp.dma_start(slab[at][:], w_v[:, :, j * HALF:(j + 1) * HALF]).then_inc(mod_in[at], 16)
                                slot_last[at] = (l, "mod", j)
                sp.wait_ge(S[l]["ni"], 1)
                pairs = sp.value_load(ni[0:1, ITEMS:ITEMS + 1], min_val=NE // 2, max_val=ITEMS // 2)
                with sp.Fori(1, pairs) as q:
                    for u in range(2):
                        e = sp.value_load(ni[0:1, bass.ds(2 * q + u, 1)], min_val=0, max_val=NE - 1)
                        for kind, slot, w in load_item(u, bass.ds(e, 1)):
                            if kind < 2:
                                sp.wait_ge(m["gu"], 4 * q + (2 * u - 4 + kind + 1))
                            else:
                                sp.wait_ge(m["y"], 4 * q + (2 * u - 4 + 2))
                            load_expert(sp, l, slot, kind, w)
                        store_item(sp, l, m, u, 2 * q + (u - 2))
                store_item(sp, l, m, 0, 2 * pairs - 2)
                if l + 1 < DEPTH:
                    load_slab(l + 1, 0)
                store_item(sp, l, m, 1, 2 * pairs - 1)

        @block.tensor
        def _(pe):
            def pb(key):
                return ps[bank.at[key][0]]

            pe.wait_ge(s_cst, 16)
            pe.wait_ge(s_c, 32)
            pe.transpose(ps[7][:, 0:2 * KC], crow[0:2 * KC, :], ident[0:2 * KC, 0:2 * KC]).then_inc(mod_full, 1)
            pe.wait_ge(s_silu_c, 2)
            with pe.Fori(0, MODG) as i:
                for u in range(4):
                    pe.wait_ge(mod_in[u], 16 * i + 16)
                    pe.wait_ge(mod_read, 4 * i + (u + 1))
                    for k in range(KC):
                        mm = pe.matmul(ps[u][0:2, :], sT[:, k:2 * KC:KC], slab[u][:, k, :], start=k == 0, stop=k == KC - 1)
                    mm.then_inc(mod_full, 1)

            def transposes(key, parts):
                bank.wait_free(pe, key)
                for src, c in parts:
                    k, n = src.shape[0], src.shape[-1]
                    mm = pe.transpose(pb(key)[0:n, c:c + k], src, ident[0:k, 0:k])
                bank.filled(mm, key)

            def product(key, lhs, rhs, n, c=0, rows=P):
                bank.wait_free(pe, key)
                for k in range(len(lhs)):
                    mm = pe.matmul(pb(key)[0:rows, c:c + n], lhs[k], rhs[k], start=k == 0, stop=k == len(lhs) - 1)
                bank.filled(mm, key)

            for l in range(DEPTH):
                T, s = QT[l], S[l]

                def h_transposes(t):
                    pe.wait_ge(s["h"], t + 1)
                    for hf in range(2):
                        transposes((l, "h", t, hf), [(htile[:, t % 2, (4 * hf + c) * P:(4 * hf + c + 1) * P], c * P) for c in range(4)])

                def project(name, t, w, key=None):
                    sl = wait_slab(pe, l, name)
                    product(key or (l, name, t), [hT[:, k, t * P:(t + 1) * P] for k in range(KC)], [sl[:, k, 0:w] for k in range(KC)], w)

                for t in range(T):
                    h_transposes(t)
                    if l == 0:
                        pe.wait_ge(mod_read, 4 + MODB - 4 + t + 1)
                    bank.wait_read(pe, (l, "h", t, 0))
                    bank.wait_read(pe, (l, "h", t, 1))
                    project("b1", t, CC)
                for t in range(T):
                    project("b2", t, CC)
                for t in range(T, NT):
                    h_transposes(t)
                pe.wait_ge(s["par"], par_count(l))
                transposes((l, "conv_cols"), [(crows[0:CW + 3, c * P:(c + 1) * P], c * (CW + 3)) for c in range(4)])
                for t in range(NT):
                    bank.wait_read(pe, (l, "h", t, 0))
                    bank.wait_read(pe, (l, "h", t, 1))
                    project("b0", t, W_CQKV)
                    if t:
                        continue
                    for c in range(4):
                        for v in range(T):
                            bank.wait_read(pe, (l, "b1", v))
                        transposes((l, "yT", c), [(ybuf[:, v, c * P:(c + 1) * P], v * P) for v in range(T)])
                for t in range(NT):
                    project("b4", t, 2 * GKV * GD)
                for t in range(T):
                    project("b3", t, GH * GD)
                for t in range(T):
                    project("g10", t, HALF, key=(l, "g", 1, 0, t))
                pe.wait_ge(s["cn"], 1)
                for c in range(3):
                    tiles = range(T) if c < 2 else range(NT)
                    transposes((l, "cT", c), [(cqkv[:, t, c * P:(c + 1) * P], t * P) for t in tiles])
                pe.wait_ge(s["cvd"], 4)
                for t in range(T):
                    r = (t % LT) * P
                    transposes((l, "cvb", t), [(cv[:, c, t // LT, r:r + P], c * P) for c in range(4)])
                for t in range(T):
                    project("g11", t, HALF, key=(l, "g", 1, 1, t))
                for t in range(T):
                    bank.wait_read(pe, (l, "cvb", t))
                for c in range(4):
                    transposes((l, "zT", c), [(ybuf[:, t, c * P:(c + 1) * P], t * P) for t in range(T)])

                sl = wait_slab(pe, l, "up")[:].rearrange("p k n -> p (k n)")
                uq = sl[:, 0:2 * H * QK].rearrange("p (k n) -> p k n", k=2)
                ukv = sl[:, 2 * H * QK:2 * H * QK + H * (NOPE + VD)]
                for c in range(3):
                    bank.wait_read(pe, (l, "cT", c))
                for t in range(NT):
                    cols = slice(t * P, (t + 1) * P)
                    if t < T:
                        product((l, "uq", t, 0), [cT[:, k, cols] for k in range(2)], [uq[:, k, 0:HALF] for k in range(2)], HALF)
                        product((l, "uq", t, 1), [cT[:, k, cols] for k in range(2)], [uq[:, k, HALF:H * QK] for k in range(2)], H * QK - HALF)
                    for hf in range(2):
                        product((l, "ukv", t, hf), [cT[:, 2, t * P:(t + 1) * P]], [ukv[:, hf * HALF:(hf + 1) * HALF]], HALF)

                def branch(b, hf, t):
                    oT = (oT_mla, zT, oT_gqa)[b]
                    wo = wait_slab(pe, l, f"o{b}")[:].rearrange("p (k j) n -> p k (j n)", k=4)
                    product((l, "o", b, hf, t), [oT[:, c, t * P:(t + 1) * P] for c in range(4)],
                            [wo[:, c, hf * HALF:(hf + 1) * HALF] for c in range(4)], HALF)
                for c in range(4):
                    bank.wait_read(pe, (l, "zT", c))
                for hf in range(2):
                    for t in range(T):
                        branch(1, hf, t)

                U = attn_units(l)
                for kind in ("gqa", "mla"):
                    pe.wait_ge(s["nrm"], 1 if kind == "gqa" else 3)
                    d = QK if kind == "mla" else GD
                    kslot = (lambda h: h % 2) if kind == "mla" else (lambda h: h // 4)
                    for i, step in attn_order(l, kind):
                        if step == "head":
                            if kind == "mla":
                                q_of, k_of = (lambda t, h: q_tm[:, t, h, :]), (lambda t, h: kfull[:, t, h, :])
                            else:
                                q_of, k_of = (lambda t, h: gq[:, t, h * GD:(h + 1) * GD]), (lambda t, h: gkv[:, t, (h // 4) * GD:(h // 4 + 1) * GD])
                            transposes((l, kind, "qT", i), [(q_of(t, i), t * P) for t in range(T)])
                            if kind == "mla" or i % 4 == 0:
                                transposes((l, kind, "kT", i), [(k_of(t, i), t * P) for t in range(NT)])
                            continue
                        h, t = U[i]
                        k0, k1 = keys_of[t]
                        n = k1 - k0
                        if step == "s":
                            bank.wait_read(pe, (l, kind, "qT", h))
                            bank.wait_read(pe, (l, kind, "kT", h if kind == "mla" else h // 4 * 4))
                            product((l, kind, "s", i), [headT[0:d, h % 2, 0, t * P:(t + 1) * P]],
                                    [headT[0:d, kslot(h), 1, k0 * P:k1 * P]], n * P)
                        elif step == "pT":
                            bank.wait_read(pe, (l, kind, "s", i))
                            transposes((l, kind, "pT", i), [(prob[:, i % 2, j * P:(j + 1) * P], j * P) for j in range(n)])
                        else:
                            bank.wait_read(pe, (l, kind, "pT", i))
                            v = (lambda j: v_tm[:, j, h * VD:(h + 1) * VD]) if kind == "mla" else \
                                (lambda j: gkv[:, j, (GKV + h // 4) * GD:(GKV + h // 4 + 1) * GD])
                            product((l, kind, "pv", i), [probT[:, i % 2, j, :] for j in range(n)],
                                    [v(k0 + j) for j in range(n)], VD)
                    for i in range(len(U)):
                        if i >= len(U) - 2:
                            bank.wait_read(pe, (l, kind, "pv", i))
                    for c in range(4):
                        transposes((l, kind, "oT", c), [(o_tm[:, t, c * P:(c + 1) * P], t * P) for t in range(T)])

                for b in MERGE:
                    for c in range(4):
                        bank.wait_read(pe, (l, "mla" if b == 0 else "gqa", "oT", c))
                    for hf in range(2):
                        for t in range(T):
                            branch(b, hf, t)
                            project(f"g{b}{hf}", t, HALF, key=(l, "g", b, hf, t))
                for hf in range(2):
                    for t in range(T):
                        pe.wait_ge(s["mg"], hf * T + t + 1)
                        transposes((l, "mT", t, hf), [(merged[:, t, (4 * hf + c) * P:(4 * hf + c + 1) * P], c * P) for c in range(4)])
                def h2_transposes(t):
                    pe.wait_ge(s["h2"], t + 1)
                    for hf in range(2):
                        transposes((l, "h2", t, hf), [(htile[:, t % 2, (4 * hf + c) * P:(4 * hf + c + 1) * P], c * P) for c in range(4)])

                for hf in range(2):
                    for t in range(T):
                        bank.wait_read(pe, (l, "mT", t, 0))
                        bank.wait_read(pe, (l, "mT", t, 1))
                        project(f"w{hf}", t, HALF, key=(l, "w", hf, t))
                        if hf and t >= 2:
                            h2_transposes(t - 2)

                def modulation(js):
                    for j in js if l + 1 < DEPTH else ():
                        at = MODSLOT[j % 4]
                        pe.wait_ge(mod_in[at], 16 * (MODG + j // 4 + 1))
                        product((l, "mod", j), [sT[:, k:2 * KC:KC] for k in range(KC)], [slab[at][:, k, :] for k in range(KC)], HALF, rows=2)

                def scores(t):
                    for hf in range(2):
                        bank.wait_read(pe, (l, "h2", t, hf))
                    for k in range(KC):
                        mm = pe.matmul(pb(key)[:, t * NE:(t + 1) * NE], hT[:, k, t * P:(t + 1) * P], rw[:, k, :], start=k == 0, stop=k == KC - 1)
                    return mm
                modulation([0])
                key = (l, "router")
                bank.wait_free(pe, key)
                pe.wait_ge(s_zero, ZEROED)
                for t in range(T - 2):
                    scores(t)
                for t in range(T - 2, T):
                    h2_transposes(t)
                modulation([1])
                for t in range(T - 2, T):
                    mm = scores(t)
                bank.filled(mm, key)
                modulation([2, 3])
                key = (l, "place")
                bank.wait_free(pe, key)
                pe.wait_ge(s["rcst"], 16)
                pe.wait_ge(s["mask"], 1)
                mask = r1[:, R_MASK, 0:T * NE].rearrange("p (t e) -> p t e", e=NE)
                for t in range(T):
                    for b in range(t + 1):
                        lhs = rcst[:, R_TRI:R_TRI + P] if b == t else rcst[:, R_ONES:R_ONES + P]
                        pe.matmul(pb(key)[:, t * NE:(t + 1) * NE], lhs, mask[:, b, :], start=b == 0, stop=b == t)
                for t in range(T):
                    mm = pe.matmul(pb(key)[:, NT * NE:(NT + 1) * NE], rcst[:, R_ONES:R_ONES + P], mask[:, t, :], start=t == 0, stop=t == T - 1)
                bank.filled(mm, key)
                modulation(range(4, MODB))

                m = M[l]
                G, UP, X0, X1, HT_, Y0, Y1 = (ps[i] for i in (2, 3, 4, 5, 6, 7, 0))

                def gather_T(item, u):
                    pe.wait_ge(m_xg[l][u], item)
                    for hf, X in enumerate((X0, X1)):
                        for c in range(4):
                            mm = pe.transpose(X[:, c * P:(c + 1) * P], xg[:, u, (4 * hf + c) * P:(4 * hf + c + 1) * P], ident)
                        mm.then_inc(m["xt"], 1)

                for key in ((l, "router"), (l, "place"), (l, "h2", T - 1, 0), (l, "h2", T - 1, 1), (l, "h2", T - 2, 0), (l, "h2", T - 2, 1)):
                    bank.wait_read(pe, key)
                for t in range(T):
                    bank.wait_read(pe, (l, "w", 0, t))
                    bank.wait_read(pe, (l, "w", 1, t))
                for j in range(MODB - 4, MODB) if l + 1 < DEPTH else ():
                    bank.wait_read(pe, (l, "mod", j))
                pe.wait_ge(s["ni"], 1)
                rounds = pe.value_load(ni[0:1, ITEMS + 4:ITEMS + 5], min_val=NE // 2 - 1, max_val=ITEMS // 2 - 1)

                def gate_up(u, q, c, w):
                    pe.wait_ge(m["xtA"], 2 * q + (c + 1))
                    pe.wait_ge(m["xtD"], 2 * q + (c + 1))
                    for slot, B, free in ((MSLOT[3 * u], G, "sig"), (MSLOT[3 * u + 1], UP, "h")):
                        pe.wait_ge(m_in[l][slot], w)
                        pe.wait_ge(m[free], 2 * q + (c + 1))
                        for k in range(KC):
                            mm = pe.matmul(B[:], xgT[:, u, k, :], slab[slot][:, k, :], start=k == 0, stop=k == KC - 1)
                        mm.then_inc(m["gu"], 1)

                def hidden_T(u, q, c):
                    pe.wait_ge(m["h"], 2 * q + (c + 2))
                    pe.wait_ge(m["htA"], 2 * q + (c + 1))
                    for k in range(4):
                        mm = pe.transpose(HT_[:, k * P:(k + 1) * P], hh[:, u, k * P:(k + 1) * P], ident)
                    mm.then_inc(m["ht"], 1)

                def outputs(u, q, c, w):
                    pe.wait_ge(m["htA"], 2 * q + (c + 2))
                    pe.wait_ge(m_in[l][MSLOT[3 * u + 2]], w)
                    wd = slab[MSLOT[3 * u + 2]][:].rearrange("p (k j) n -> p k (j n)", k=4)
                    for hf, (Y, free) in enumerate(((Y0, "yA"), (Y1, "yD"))):
                        pe.wait_ge(m[free], 2 * q + (c + 1))
                        for k in range(4):
                            mm = pe.matmul(Y[:], hhT[:, u, k, :], wd[:, k, hf * HALF:(hf + 1) * HALF], start=k == 0, stop=k == 3)
                        mm.then_inc(m["y"], 1)

                gather_T(16, 0)
                gate_up(0, 0, 0, 16)
                gather_T(16, 1)
                hidden_T(0, 0, 0)
                with pe.Fori(0, rounds) as q:
                    gate_up(1, q, 1, 16 * q + 16)
                    outputs(0, q, 0, 16 * q + 16)
                    gather_T(16 * q + 32, 0)
                    hidden_T(1, q, 1)
                    gate_up(0, q, 2, 16 * q + 32)
                    outputs(1, q, 1, 16 * q + 16)
                    gather_T(16 * q + 32, 1)
                    hidden_T(0, q, 2)
                gate_up(1, rounds, 1, 16 * rounds + 16)
                outputs(0, rounds, 0, 16 * rounds + 16)
                hidden_T(1, rounds, 1)
                outputs(1, rounds, 1, 16 * rounds + 16)

        @block.scalar
        def _(act):
            steps = [0]

            def step(ins):
                ins.then_inc(act_step, 1)
                steps[0] += 1
                act.wait_ge(act_step, steps[0])

            def copy_of(key, dst, src):
                bank.wait_full(act, key)
                bank.read(act.activation(dst, src, ACT.Copy), key)

            def pb(key):
                return ps[bank.at[key][0]]

            act.wait_ge(mod_full, 1)
            act.activation(csig[:], ps[7][:, 0:2 * KC], ACT.Sigmoid).then_inc(s_silu_c, 1)
            act.wait_ge(mod_full, 4)
            act.dma_start(x_sb[:, 0:LT, :], a["x"].rearrange("o (t p) d -> p (o t) d", p=P)).then_inc(s_x, 16)
            act.dma_start(x_sb[:, LT:NT, :], a["ctx"].rearrange("o (t p) d -> p (o t) d", p=P)).then_inc(s_x, 16)

            def modulation_out(l, g):
                w = D_MOD // MODG
                act.dma_start(mod_d[:, l * D_MOD + g * w:l * D_MOD + (g + 1) * w], mods[0:2, g * w:(g + 1) * w]).then_inc(mod_out[g], 16)

            for l in range(DEPTH):
                T, s, m = QT[l], S[l], M[l]

                def square(n, t):
                    if n:
                        act.wait_ge(s["sq"], n)
                    act.activation(junk[:], x_sb[:, t, :], ACT.Square, accum_out=ssum[:, 0, t:t + 1]).then_inc(s["sq"], 1)

                def choose_roots():
                    act.activation(warm[:], cst[:, C_ID:C_ID + 1], ACT.Sqrt)

                def root(n, t):
                    act.wait_ge(s["sqm"], n + 1)
                    act.activation(ssum[:, 2, t:t + 1], ssum[:, 1, t:t + 1], ACT.Sqrt).then_inc(s["sqrt"], 1)

                def h_copies(name, t):
                    for hf in range(2):
                        key = (l, name, t, hf)
                        copy_of(key, hT[:, 4 * hf:4 * hf + 4, t * P:(t + 1) * P], pb(key)[:].rearrange("p (c n) -> p c n", c=4))

                def conv_input_gates():
                    for t in range(T):
                        key = (l, "b2", t)
                        bank.wait_full(act, key)
                        if t >= 2:
                            bank.wait_read(act, (l, "b1", t - 2))
                        bank.read(act.activation(sgt[:, t % 2, :], pb(key)[:], ACT.Sigmoid), key)

                if l == 0:
                    act.wait_ge(s_x, 32)
                    for t in range(NT):
                        square(t, t)
                    for g in range(MODG - 1):
                        act.wait_ge(mod_read, 4 * (g + 1) + 4)
                        modulation_out(l, g)
                    for t in range(NT):
                        root(t, t)
                    for t in range(T):
                        h_copies("h", t)
                        if t == 0:
                            act.wait_ge(mod_read, MODB + 4)
                            modulation_out(l, MODG - 1)
                    conv_input_gates()
                    for g in range(MODG):
                        act.wait_ge(mod_out[g], 16)
                else:
                    choose_roots()
                    for t in range(NT):
                        if 1 <= t <= T:
                            h_copies("h", t - 1)
                        act.wait_ge(S[l - 1]["xf"], t + 1)
                        square(t, t)
                        root(t, t)
                    conv_input_gates()
                    for t in range(T, NT):
                        h_copies("h", t)
                copy_of((l, "b0", 0), cqkv[:, 0, :], pb((l, "b0", 0))[:, 0:W_CQKV])
                act.wait_ge(s["pad"], 1)
                for c in range(4):
                    key = (l, "yT", c)
                    copy_of(key, ypad[:, c, 0:T // LT, CW // 2:CW // 2 + SEQ], pb(key)[:, 0:T * P].rearrange("p (s n) -> p s n", n=SEQ))
                def conv_terms(taps):
                    for w in taps:
                        if w > 8:
                            act.wait_ge(pool_step, l * (CW - 1) + w - 7)
                        act.activation(term(w)[:, 0:T // LT, :], ypad[:, 3, 0:T // LT, w:w + SEQ], ACT.Copy,
                                       scale=convc[:, 3, w:w + 1]).then_inc(s["term"], 1)
                bank.wait_read(act, (l, "conv_cols"))
                bank.wait_read(act, (l, "yT", 3))
                conv_terms(range(1, 9))
                for t in range(1, NT):
                    copy_of((l, "b0", t), cqkv[:, t, :], pb((l, "b0", t))[:, 0:W_CQKV])
                conv_terms(range(9, 17))
                act.wait_ge(s["csq"], 1)
                for t in range(NT):
                    bank.wait_read(act, (l, "b0", t))
                    if t < T:
                        act.activation(junk[:, 0:QR], cqkv[:, t, 0:QR], ACT.Square, accum_out=cstat[:, t, 0:1])
                    ins = act.activation(junk[:, QR:QR + KVR], cqkv[:, t, QR:QR + KVR], ACT.Square, accum_out=cstat[:, t, 1:2])
                    if t < NT - 1:
                        step(ins)
                ins.then_inc(s["csq"], 1)
                for t in range(NT):
                    copy_of((l, "b4", t), gkv[:, t, :], pb((l, "b4", t))[:, 0:2 * GKV * GD])
                conv_terms(range(17, 25))
                for t in range(T):
                    copy_of((l, "b3", t), gq[:, t, :], pb((l, "b3", t))[:])
                act.wait_ge(s["csq"], 3)
                act.activation(cstat[:], cstat[:], ACT.Sqrt).then_inc(s["csq"], 1)
                conv_terms(range(25, CW))
                act.wait_ge(s["st"], 1)
                act.activation(stat[:, :, 0:HEAD_A], stat[:, :, 0:HEAD_A], ACT.Sqrt).then_inc(s["st"], 1)

                def conv_gate(hf):
                    for t in range(T):
                        key = (l, "g", 1, hf, t)
                        bank.wait_full(act, key)
                        bank.read(act.activation(merged[:, t, hf * HALF:(hf + 1) * HALF], pb(key)[:], ACT.Sigmoid), key)
                conv_gate(0)
                for c in range(3):
                    n = (T if c < 2 else NT) * P
                    key = (l, "cT", c)
                    bank.wait_full(act, key)
                    bank.read(act.activation(cT[:, c, 0:n], pb(key)[:, 0:n], ACT.Identity, scale=colg[:, c:c + 1]), key)
                act.wait_ge(s["lnv"], 1)
                act.activation(mv[:, 0:T, 1:2], mv[:, 0:T, 1:2], ACT.Sqrt).then_inc(s["lns"], 1)
                conv_gate(1)
                for c in range(4):
                    key = (l, "zT", c)
                    bank.wait_full(act, key)
                    bank.read(act.activation(zT[:, c, 0:T * P], pb(key)[:, 0:T * P], ACT.Silu, scale=convc[:, c, CW + 1:CW + 2],
                                             bias=convc[:, c, CW + 2:CW + 3]), key)
                for t in range(NT):
                    if t < T:
                        q2 = q_tm[:, t].rearrange("p h d -> p (h d)")
                        copy_of((l, "uq", t, 0), q2[:, 0:HALF], pb((l, "uq", t, 0))[:])
                        copy_of((l, "uq", t, 1), q2[:, HALF:H * QK], pb((l, "uq", t, 1))[:, 0:H * QK - HALF])
                    for hf in range(2):
                        key = (l, "ukv", t, hf)
                        kv = pb(key)[:].rearrange("p (h d) -> p h d", h=4)
                        bank.wait_full(act, key)
                        act.activation(kfull[:, t, 4 * hf:4 * hf + 4, 0:NOPE], kv[:, :, 0:NOPE], ACT.Copy)
                        bank.read(act.activation(v_tm[:, t, 4 * hf * VD:4 * (hf + 1) * VD].rearrange("p (h d) -> p h d", h=4), kv[:, :, NOPE:NOPE + VD], ACT.Copy), key)
                act.wait_ge(s["st"], 3)
                act.activation(stat[:, :, HEAD_A:35], stat[:, :, HEAD_A:35], ACT.Sqrt).then_inc(s["st"], 1)
                act.wait_ge(s["nrm"], 1)
                for t in range(NT):
                    ins = act.activation(kfull[:, t, :, NOPE:QK], kpe[:, t, :].unsqueeze(1).to_broadcast([P, H, ROPE]), ACT.Copy)
                ins.then_inc(s["nrm"], 1)

                U = attn_units(l)
                for kind in ("gqa", "mla"):
                    d = QK if kind == "mla" else GD
                    kslot = (lambda h: h % 2) if kind == "mla" else (lambda h: h // 4)
                    scale = float(d) ** -0.5
                    for i, stage in attn_order(l, kind, scores_last=True):
                        key = (l, kind, stage, i)
                        if stage == "head":
                            if kind == "mla" or i % 4 == 0:
                                key = (l, kind, "kT", i)
                                copy_of(key, headT[0:d, kslot(i), 1, :], pb(key)[0:d, :])
                            continue
                        h, t = U[i]
                        n = keys_of[t][1] - keys_of[t][0]
                        if stage == "s":
                            act.wait_ge(s["nmax"], (len(U) if kind == "mla" else 0) + i + 1)
                            bank.wait_full(act, key)
                            if i >= 2:
                                bank.wait_full(act, (l, kind, "pT", i - 2))
                            bank.read(act.activation(prob[:, i % 2, 0:n * P], pb(key)[:, 0:n * P], ACT.Exp,
                                                     bias=nmax[:, i % 4:i % 4 + 1], scale=scale, accum_out=rsum[:, i % 8:i % 8 + 1]), key)
                        elif stage == "pT":
                            if i >= 2:
                                bank.wait_full(act, (l, kind, "pv", i - 2))
                            copy_of(key, probT[:, i % 2, 0:n, :], pb(key)[:, 0:n * P].rearrange("p (j q) -> p j q", q=P))
                    for c in range(4):
                        key = (l, kind, "oT", c)
                        dst = oT_mla if kind == "mla" else oT_gqa
                        copy_of(key, dst[:, c, 0:T * P], pb(key)[:, 0:T * P])

                i, used = 0, []
                for b in MERGE:
                    for hf in range(2):
                        for t in range(T):
                            key = (l, "g", b, hf, t)
                            bank.wait_full(act, key)
                            if i >= 2:
                                bank.wait_read(act, used[i - 2])
                            used.append((l, "o", b, hf, t))
                            bank.read(act.activation(sgt[:, i % 2, :], pb(key)[:], ACT.Sigmoid), key)
                            i += 1
                for hf in range(2):
                    for t in range(T):
                        key = (l, "mT", t, hf)
                        copy_of(key, hT[:, 4 * hf:4 * hf + 4, t * P:(t + 1) * P], pb(key)[:].rearrange("p (c n) -> p c n", c=4))

                stored = []

                def h2_store(t):
                    if t not in stored:
                        stored.append(t)
                        act.wait_ge(s["h2"], t + 1)
                        act.dma_start(h2_d[l][t * P:(t + 1) * P, :], htile[:, t % 2, :]).then_inc(s["h2o"], 16)
                choose_roots()
                for t in range(T):
                    act.wait_ge(s["xm"], T + t + 1)
                    square(NT + t, t)
                    if t >= 2:
                        h2_store(t - 2)
                        h2_store(1)
                        h_copies("h2", t - 2)
                    root(NT + t, t)
                for t in range(T - 2, T):
                    h2_store(t)
                    h_copies("h2", t)
                key = (l, "router")
                bank.wait_full(act, key)
                bank.read(act.activation(r1[:, R_S, 0:T * NE], pb(key)[:, 0:T * NE], ACT.Sigmoid), key)
                if l + 1 < DEPTH:
                    for g in range(MODG):
                        for j in range(4 * g, 4 * g + 4):
                            bank.wait_read(act, (l, "mod", j))
                        modulation_out(l + 1, g)
                    for g in range(MODG - 1):
                        act.wait_ge(mod_out[g], 32)

                X0, HT_, Y0 = ps[4], ps[6], ps[7]
                for name in ("sig", "htA", "yA"):
                    act.sem_inc(m[name], 1)
                for u in range(2):
                    act.sem_inc(m_yo[l][u], 16)
                act.wait_ge(s["ni"], 1)
                rounds = act.value_load(ni[0:1, ITEMS + 4:ITEMS + 5], min_val=NE // 2 - 1, max_val=ITEMS // 2 - 1)

                def tokens(u, q, c):
                    act.wait_ge(m["xt"], 4 * q + (2 * c + 1))
                    act.activation(xgT[:, u, 0:4, :], X0[:].rearrange("p (c n) -> p c n", c=4), ACT.Copy).then_inc(m["xtA"], 1)

                def gate(u, q, c):
                    act.wait_ge(m["gu"], 4 * q + (2 * c + 1))
                    act.wait_ge(m["h"], 2 * q + (c + 1))
                    act.activation(sg[:, u, :], ps[2][:], ACT.Silu).then_inc(m["sig"], 1)

                def hidden(u, q, c):
                    act.wait_ge(m["ht"], 2 * q + (c + 1))
                    act.activation(hhT[:, u], HT_[:].rearrange("p (c n) -> p c n", c=4), ACT.Copy).then_inc(m["htA"], 1)

                def output(u, q, c):
                    act.wait_ge(m["y"], 4 * q + (2 * c + 1))
                    act.wait_ge(m_yo[l][u], 16 * q + (8 * (c - u) + 16))
                    act.activation(yg[:, u, 0:HALF], Y0[:], ACT.Copy).then_inc(m["yA"], 1)

                tokens(0, 0, 0)
                if l + 1 < DEPTH:
                    act.wait_ge(mod_out[MODG - 1], 32)
                gate(0, 0, 0)
                tokens(1, 0, 1)
                hidden(0, 0, 0)
                with act.Fori(0, rounds) as q:
                    gate(1, q, 1)
                    output(0, q, 0)
                    tokens(0, q, 2)
                    hidden(1, q, 1)
                    gate(0, q, 2)
                    output(1, q, 1)
                    tokens(1, q, 3)
                    hidden(0, q, 2)
                gate(1, rounds, 1)
                output(0, rounds, 0)
                hidden(1, rounds, 1)
                output(1, rounds, 1)
            for t in range(LT):
                act.wait_ge(S[DEPTH - 1]["xf"], t + 1)
                act.dma_start(out[0, t * P:(t + 1) * P, :], x_sb[:, t, :]).then_inc(s_out, 16)
            act.wait_ge(s_out, 16 * LT)

        @block.vector
        def _(dve):
            steps = [0]

            def step(ins):
                ins.then_inc(dve_step, 1)
                steps[0] += 1
                dve.wait_ge(dve_step, steps[0])

            def pb(key):
                return ps[bank.at[key][0]]

            TT, TS, STT, RED = dve.tensor_tensor, dve.tensor_scalar, dve.scalar_tensor_tensor, dve.tensor_reduce

            dve.sem_inc(mod_read, 4)
            dve.memset(zero[:], 0).then_inc(s_zset, 1)
            dve.wait_ge(s_silu_c, 1)
            TT(sT[:], ps[7][:, 0:2 * KC], csig[:], ALU.mult).then_inc(s_silu_c, 1)

            def mean(l, n, t):
                dve.wait_ge(S[l]["sq"], n + 1)
                TS(ssum[:, 1, t:t + 1], ssum[:, 0, t:t + 1], 1.0 / D, EPS, ALU.mult, ALU.add).then_inc(S[l]["sqm"], 1)
            dve.wait_ge(s_bias, 16)
            with dve.Fori(0, MODG - 1) as i:
                for u in range(4):
                    dve.wait_ge(mod_full, 4 * i + (u + 2))
                    cols = mods[0:2, bass.ds((4 * i + u) * HALF, HALF)]
                    TT(cols, ps[u][0:2, :], cols, ALU.add).then_inc(mod_read, 1)

            for l in range(DEPTH):
                T, s, m = QT[l], S[l], M[l]

                def scales(k, rows, n_rows, n):
                    dve.wait_ge(S[k][rows], n_rows)
                    for r in range(n):
                        ins = STT(out=rowA[:, r, :], in0=rowA[:, r, :], scalar=1.0, in1=normg[:], op0=ALU.add, op1=ALU.mult)
                    step(ins)

                def normalise(k, n, t, free, done):
                    dve.wait_ge(S[k]["sqrt"], n + 1)
                    step(dve.reciprocal(ssum[:, 2, t:t + 1], ssum[:, 2, t:t + 1]))
                    free(k, t)
                    step(STT(out=htile[:, t % 2, :], in0=x_sb[:, t, :], scalar=ssum[:, 2, t:t + 1], in1=rowA[:, t // LT, :],
                             op0=ALU.mult, op1=ALU.mult))
                    TT(htile[:, t % 2, :], htile[:, t % 2, :], rowB[:, t // LT, :], ALU.add).then_inc(S[k][done], 1)

                def free1(k, t):
                    if t >= 2:
                        bank.wait_full(dve, (k, "h", t - 2, 1))
                if l == 0:
                    for t in range(NT):
                        mean(0, t, t)
                    scales(0, "rows1", 16 * 5, 2)
                    for t in range(NT):
                        if t == 1 or t == 2:
                            for u in range(2) if t == 1 else range(2, 4):
                                dve.wait_ge(mod_full, MODB - 4 + u + 2)
                                cols = mods[0:2, (MODB - 4 + u) * HALF:(MODB - 3 + u) * HALF]
                                TT(cols, ps[u][0:2, :], cols, ALU.add).then_inc(mod_read, 1)
                        normalise(0, t, t, free1, "h")
                    for g in range(MODG):
                        dve.wait_ge(mod_out[g], 16)

                for t in range(T):
                    key = (l, "b1", t)
                    bank.wait_read(dve, (l, "b2", t))
                    bank.wait_full(dve, key)
                    bank.read(TT(ybuf[:, t, :], pb(key)[:], sgt[:, t % 2, :], ALU.mult), key)
                dve.memset(cstat[:], 1.0).then_inc(s["csq"], 1)
                key = (l, "conv_cols")
                bank.wait_full(dve, key)
                bank.read(dve.tensor_copy(convc[:].rearrange("p c w -> p (c w)"), pb(key)[:, 0:4 * (CW + 3)]), key)
                bank.wait_read(dve, key)

                def cn():
                    dve.wait_ge(s["csq"], 2)
                    TS(cstat[:, :, 0:1], cstat[:, :, 0:1], 1.0 / QR, EPS, ALU.mult, ALU.add)
                    TS(cstat[:, :, 1:2], cstat[:, :, 1:2], 1.0 / KVR, EPS, ALU.mult, ALU.add).then_inc(s["csq"], 1)
                    dve.wait_ge(s["csq"], 4)
                    step(dve.reciprocal(cstat[:], cstat[:]))
                    for t in range(NT):
                        if t < T:
                            TS(cqkv[:, t, 0:QR], cqkv[:, t, 0:QR], cstat[:, t, 0:1], None, ALU.mult)
                        ins = TS(cqkv[:, t, QR:QR + KVR], cqkv[:, t, QR:QR + KVR], cstat[:, t, 1:2], None, ALU.mult)
                    ins.then_inc(s["cn"], 1)

                ns = T // LT
                summed = {}
                for w in range(CW):
                    for c in range(3):
                        src = ypad[:, c, 0:ns, w:w + SEQ]
                        acc = cv[:, c, 0:ns, :]
                        if w == 0:
                            bank.wait_read(dve, (l, "yT", c))
                            ins = TS(acc, src, convc[:, c, 0:1], convc[:, c, CW:CW + 1], ALU.mult, ALU.add)
                        else:
                            dve.wait_ge(dve_step, summed[c])
                            ins = STT(out=acc, in0=src, scalar=convc[:, c, w:w + 1], in1=acc, op0=ALU.mult, op1=ALU.add)
                        if w < CW - 1:
                            ins.then_inc(dve_step, 1)
                            steps[0] += 1
                            summed[c] = steps[0]
                        else:
                            ins.then_inc(s["cvd"], 1)
                cn()
                def heads(x, d):
                    return x.rearrange("p (h d) -> p h d", d=d)

                def parts_a(t):
                    parts = [(heads(gkv[:, t, 0:GKV * GD], GD), 8, 10, 2 * QK + GD, GD, heads(gkv[:, t, 0:GKV * GD], GD), 16, 32),
                             (heads(cqkv[:, t, QR + KVR:W_CQKV], ROPE), 10, 11, QK + NOPE, ROPE, heads(kpe[:, t, :], ROPE), 8, 0)]
                    if t < T:
                        parts += [(heads(gq[:, t, :], GD), 0, 8, 2 * QK, GD, heads(gq[:, t, :], GD), 16, 32)]
                    return parts

                def parts_b(t):
                    parts = [(kfull[:, t, :, 0:NOPE], 19, 27, QK, NOPE, kfull[:, t, :, 0:NOPE], 0, 0)]
                    if t < T:
                        parts += [(q_tm[:, t, :, 0:NOPE], 11, 19, 0, NOPE, q_tm[:, t, :, 0:NOPE], 0, 0),
                                  (q_tm[:, t, :, NOPE:QK], 27, 35, NOPE, ROPE, q_tm[:, t, :, NOPE:QK], 8, 0)]
                    return parts
                squares = [0]

                def statistics(parts):
                    for t in range(NT):
                        if parts is parts_b:
                            for hf in range(2):
                                bank.wait_read(dve, (l, "ukv", t, hf))
                                if t < T:
                                    bank.wait_read(dve, (l, "uq", t, hf))
                        else:
                            bank.wait_read(dve, (l, "b4", t))
                            if t < T:
                                bank.wait_read(dve, (l, "b3", t))
                        for x, c0, c1, g, d, dst, f, r in parts(t):
                            at = squares[0] % 2 * HALF
                            squares[0] += 1
                            sq = heads(tmp3[:, at:at + (c1 - c0) * d], d)
                            step(TT(sq, x, x, ALU.mult))
                            ins = RED(stat[:, t, c0:c1], sq, AX, ALU.add)
                    step(ins)

                def gains(parts, t):
                    for k in range(2):
                        for x, c0, c1, g, d, dst, f, r in parts(t):
                            hs = c1 - c0
                            if k == 0:
                                ins = TT(dst, x, stat[:, t, c0:c1].unsqueeze(2).to_broadcast([P, hs, d]), ALU.mult)
                            else:
                                ins = TT(dst, dst, qkg[:, g:g + d].unsqueeze(1).to_broadcast([P, hs, d]), ALU.mult)
                        step(ins)
                    if t >= LT:
                        return ins
                    for x, c0, c1, g, d, dst, f, r in parts(t):
                        if not f:
                            continue
                        hs = c1 - c0
                        v = dst.rearrange("p h (a b f) -> p h a b f", a=2, b=2)
                        x1, x2 = v[:, :, :, 0, :], v[:, :, :, 1, :]
                        r0 = C_ROPE + t * ROPEW + r
                        cs, sn = (cst[:, r0 + k * 2 * f:r0 + (k + 1) * 2 * f].rearrange("p (a f) -> p a f", f=f).unsqueeze(1)
                                  .to_broadcast([P, hs, 2, f]) for k in range(2))
                        tt = [ropt[:, k, 0:hs * 2 * f].rearrange("p (h a f) -> p h a f", a=2, f=f) for k in range(4)]
                        TT(tt[0], x1, cs, ALU.mult)
                        TT(tt[1], x2, sn, ALU.mult)
                        TT(tt[2], x2, cs, ALU.mult)
                        step(TT(tt[3], x1, sn, ALU.mult))
                        TT(x1, tt[0], tt[1], ALU.subtract)
                        ins = TT(x2, tt[2], tt[3], ALU.add)
                        step(ins)

                def conv_branch(hf, tiles):
                    for t in tiles:
                        key = (l, "o", 1, hf, t)
                        bank.wait_read(dve, (l, "g", 1, hf, t))
                        bank.wait_full(dve, key)
                        dst = merged[:, t, hf * HALF:(hf + 1) * HALF]
                        bank.read(TT(dst, pb(key)[:], dst, ALU.mult), key)

                step(dve.memset(stat[:], 1.0))
                statistics(parts_a)
                TS(stat[:, :, 0:10], stat[:, :, 0:10], 1.0 / GD, EPS, ALU.mult, ALU.add)
                TS(stat[:, :, 10:HEAD_A], stat[:, :, 10:HEAD_A], 1.0 / ROPE, EPS, ALU.mult, ALU.add).then_inc(s["st"], 1)
                dve.wait_ge(s["st"], 2)
                step(dve.reciprocal(stat[:, :, 0:HEAD_A], stat[:, :, 0:HEAD_A]))
                for t in range(NT):
                    gains(parts_a, t)
                dve.sem_inc(s["nrm"], 1)

                for t in range(T):
                    bank.wait_full(dve, (l, "cvb", t))
                    ins = dve.bn_stats(bnst[:, t, 0:6], pb((l, "cvb", t))[:])
                step(ins)
                for t in range(T):
                    ins = dve.bn_aggr(mv[:, t, :], bnst[:, t, 0:6])
                step(ins)
                TS(mv[:, 0:T, 1:2], mv[:, 0:T, 1:2], EPS, None, ALU.add).then_inc(s["lnv"], 1)
                dve.wait_ge(s["lns"], 1)
                step(dve.reciprocal(mv[:, 0:T, 1:2], mv[:, 0:T, 1:2]))
                for t in range(T):
                    key = (l, "cvb", t)
                    bank.read(TS(ybuf[:, t, :], pb(key)[:], mv[:, t, 0:1], mv[:, t, 1:2], ALU.subtract, ALU.mult), key)

                statistics(parts_b)
                TS(stat[:, :, HEAD_A:27], stat[:, :, HEAD_A:27], 1.0 / NOPE, EPS, ALU.mult, ALU.add)
                TS(stat[:, :, 27:35], stat[:, :, 27:35], 1.0 / ROPE, EPS, ALU.mult, ALU.add).then_inc(s["st"], 1)
                dve.wait_ge(s["st"], 4)
                step(dve.reciprocal(stat[:, :, HEAD_A:35], stat[:, :, HEAD_A:35]))
                for t in range(NT):
                    gains(parts_b, t)
                    if t < T:
                        conv_branch(0, [t])
                dve.sem_inc(s["nrm"], 1)
                conv_branch(1, range(T))

                U = attn_units(l)
                for kind in ("gqa", "mla"):
                    d = QK if kind == "mla" else GD
                    for i, stage in attn_order(l, kind):
                        key = (l, kind, stage, i)
                        if stage == "head":
                            key = (l, kind, "qT", i)
                            bank.wait_full(dve, key)
                            bank.read(dve.tensor_copy(headT[0:d, i % 2, 0, 0:T * P], pb(key)[0:d, 0:T * P]), key)
                            continue
                        h, t = U[i]
                        n = keys_of[t][1] - keys_of[t][0]
                        if stage == "s":
                            bank.wait_full(dve, key)
                            step(dve.reduce_max(mxs[:, i % 4:i % 4 + 1], pb(key)[:, 0:n * P], AX))
                            TS(nmax[:, i % 4:i % 4 + 1], mxs[:, i % 4:i % 4 + 1], -float(d) ** -0.5, None, ALU.mult).then_inc(s["nmax"], 1)
                        elif stage == "pv":
                            bank.wait_read(dve, (l, kind, "s", i))
                            step(dve.reciprocal(rinv[:, i % 4:i % 4 + 1], rsum[:, i % 8:i % 8 + 1]))
                            bank.wait_full(dve, key)
                            if kind == "mla" and i == 0:
                                bank.wait_full(dve, (l, "gqa", "oT", 3))
                            bank.read(TS(o_tm[:, t, h * VD:(h + 1) * VD], pb(key)[:, 0:VD], rinv[:, i % 4:i % 4 + 1], None, ALU.mult), key)

                i = 0
                for b in MERGE:
                    for hf in range(2):
                        for t in range(T):
                            key = (l, "o", b, hf, t)
                            bank.wait_full(dve, key)
                            bank.wait_read(dve, (l, "g", b, hf, t))
                            dst = merged[:, t, hf * HALF:(hf + 1) * HALF]
                            bank.read(TT(tmp[:], pb(key)[:], sgt[:, i % 2, :], ALU.mult), key)
                            bank.wait_read(dve, key)
                            ins = TT(dst, dst, tmp[:], ALU.add)
                            if b == MERGE[-1]:
                                ins.then_inc(s["mg"], 1)
                                dve.wait_ge(s["mg"], hf * T + t + 1)
                            else:
                                step(ins)
                            i += 1
                def free2(k, t):
                    if t >= 2:
                        bank.wait_full(dve, (k, "h2", t - 2, 1))
                        dve.wait_ge(s["h2o"], 32)
                dve.wait_ge(s["rows2"], 16 * (T // LT))
                for hf in range(2):
                    if hf:
                        scales(l, "rows3", 16 * (3 if T <= LT else 5), T // LT)
                    for t in range(T):
                        key = (l, "w", hf, t)
                        bank.wait_full(dve, key)
                        cols = slice(hf * HALF, (hf + 1) * HALF)
                        bank.read(TT(tmp[:], pb(key)[:], rowG[:, t // LT, cols], ALU.mult), key)
                        bank.wait_read(dve, key)
                        ins = TT(x_sb[:, t, cols], x_sb[:, t, cols], tmp[:], ALU.add)
                        ins.then_inc(s["xm"], 1)
                        dve.wait_ge(s["xm"], hf * T + t + 1)
                        if hf and t:
                            mean(l, NT + t - 1, t - 1)
                            normalise(l, NT + t - 1, t - 1, free2, "h2")
                mean(l, NT + T - 1, T - 1)
                normalise(l, NT + T - 1, T - 1, free2, "h2")

                def modulation(js):
                    if l + 1 < DEPTH:
                        for j in js:
                            key = (l, "mod", j)
                            bank.wait_full(dve, key)
                            cols = mods[0:2, j * HALF:(j + 1) * HALF]
                            bank.read(TT(cols, pb(key)[0:2, :], cols, ALU.add), key)
                dve.wait_ge(s_bias, 32 if l + 1 < DEPTH else 16)
                modulation([0, 1])

                dve.wait_ge(s["rcst"], 16)
                key = (l, "router")
                bank.wait_read(dve, key)
                slots = [2]
                W = T * NE

                def r(n_=1):
                    k = slots[0]
                    slots[0] += n_
                    return r1[:, k:k + n_, :].rearrange("p k n -> p (k n)")

                def te(x, k=T):
                    return x[:, 0:k * NE].rearrange("p (t e) -> p t e", e=NE)

                def bc(x, n_, w_):
                    return x[:, 0:n_].unsqueeze(2).to_broadcast([P, n_, w_])

                sc = r1[:, R_S, :]
                sel = r()
                dve.tensor_copy(toku[:, 0:NT], rcst[:, R_TOK:R_TOK + NT])
                step(TT(te(sel), te(sc), qkg[:, 2 * QK + 2 * GD:2 * QK + 2 * GD + NE].unsqueeze(1).to_broadcast([P, T, NE]), ALU.add))
                G4 = T * NG
                sp_ = sel[:, 0:W].rearrange("p (g q) -> p g q", q=2)
                mx, mn, a1, a2, a3, a4, gs, gm, k1, k2 = (r() for _ in range(10))
                pr = lambda x: x[:, 0:2 * G4].rearrange("p (g q) -> p g q", q=2)
                TT(mx[:, 0:2 * G4].unsqueeze(2), sp_[:, :, 0:1], sp_[:, :, 1:2], ALU.max)
                step(TT(mn[:, 0:2 * G4].unsqueeze(2), sp_[:, :, 0:1], sp_[:, :, 1:2], ALU.min))
                TT(a1[:, 0:G4].unsqueeze(2), pr(mx)[:, :, 0:1], pr(mx)[:, :, 1:2], ALU.max)
                TT(a2[:, 0:G4].unsqueeze(2), pr(mx)[:, :, 0:1], pr(mx)[:, :, 1:2], ALU.min)
                step(TT(a3[:, 0:G4].unsqueeze(2), pr(mn)[:, :, 0:1], pr(mn)[:, :, 1:2], ALU.max))
                step(TT(a4[:, 0:G4], a2[:, 0:G4], a3[:, 0:G4], ALU.max))
                step(TT(gs[:, 0:G4], a1[:, 0:G4], a4[:, 0:G4], ALU.add))

                def first_largest(out_, x, n_, w_, rev):
                    v = lambda y: y[:, 0:n_ * w_].rearrange("p (n w) -> p n w", w=w_)
                    step(RED(k1[:, 0:n_], v(x), AX, ALU.max))
                    step(TT(v(k2), v(x), bc(k1, n_, w_), ALU.is_equal))
                    step(TT(v(k2), v(k2), rcst[:, rev:rev + w_].unsqueeze(1).to_broadcast([P, n_, w_]), ALU.mult))
                    step(RED(k1[:, 0:n_], v(k2), AX, ALU.max))
                    step(TT(v(out_), v(k2), bc(k1, n_, w_), ALU.is_equal))

                first_largest(gm, gs, T, NG, R_GREV)
                pen = a1
                BIG = 1e30
                grp = lambda x: x[:, 0:W].rearrange("p (g q) -> p g q", q=EG)
                TS(pen[:, 0:G4], gm[:, 0:G4], BIG, -BIG, ALU.mult, ALU.add)
                inside = r()
                step(TT(grp(inside), grp(sel), bc(gm, G4, EG), ALU.mult))
                step(TT(grp(inside), grp(inside), bc(pen, G4, EG), ALU.add))
                oh = r1[:, slots[0]:slots[0] + 2, 0:W]
                o1, o2 = r(), r()
                first_largest(o1, inside, T, NE, R_REV)
                second = r()
                step(STT(out=second[:, 0:W], in0=o1[:, 0:W], scalar=-2 * BIG, in1=inside[:, 0:W], op0=ALU.mult, op1=ALU.add))
                first_largest(o2, second, T, NE, R_REV)
                mask = r1[:, R_MASK, :]
                TT(mask[:, 0:W], o1[:, 0:W], o2[:, 0:W], ALU.add).then_inc(s["mask"], 1)
                modulation([2, 3])
                oh4 = oh.rearrange("p k (t e) -> p k t e", e=NE)
                prod = r(2)
                p4 = prod[:, 0:2 * NT * NE].rearrange("p (k n) -> p k n", k=2)[:, :, 0:W].rearrange("p k (t e) -> p k t e", e=NE)
                res = r()

                def picked(row, table):
                    for k in range(2):
                        ins = TT(p4[:, k], oh4[:, k], table, ALU.mult)
                    step(ins)
                    for k in range(2):
                        ins = RED(res[:, row * 8 + k * T:row * 8 + (k + 1) * T], p4[:, k], AX, ALU.add)
                    step(ins)
                    return res[:, row * 8:row * 8 + 2 * T]

                w_ = picked(0, te(sc))
                den = res[:, 8:8 + T]
                step(TT(den, w_[:, 0:T], w_[:, T:2 * T], ALU.add))
                step(dve.reciprocal(den, den))
                for k in range(2):
                    TT(wk[:, k, 0:T], w_[:, k * T:(k + 1) * T], den, ALU.mult)
                key = (l, "place")
                pos, cnt = r(), r()
                bank.wait_full(dve, key)
                dve.tensor_copy(pos[:, 0:W], pb(key)[:, 0:W])
                bank.read(dve.tensor_copy(cnt[:, 0:NE], pb(key)[:, NT * NE:(NT + 1) * NE]), key)
                bank.wait_read(dve, key)
                over = cnt[:, NE:2 * NE]
                step(TS(over, cnt[:, 0:NE], float(P), None, ALU.is_gt))
                step(STT(out=over, in0=cnt[:, 0:NE], scalar=float(2 * P), in1=over, op0=ALU.is_gt, op1=ALU.add))
                step(STT(out=over, in0=cnt[:, 0:NE], scalar=float(3 * P), in1=over, op0=ALU.is_gt, op1=ALU.add))
                big = r(4)
                b3 = big[:, 0:NE * NE].rearrange("p (e f) -> p e f", f=NE)
                ob, incl = cnt[:, 2 * NE:3 * NE], cnt[:, 3 * NE:4 * NE]
                step(TT(b3, rcst[:, R_LT:R_LT + NE * NE].rearrange("p (e f) -> p e f", f=NE), over.unsqueeze(1).to_broadcast([P, NE, NE]), ALU.mult))
                step(RED(ob, b3, AX, ALU.add))
                step(TT(incl, ob, over, ALU.add))
                p_ = picked(1, te(pos))
                e_ = picked(2, rcst[:, R_EID:R_EID + NE].unsqueeze(1).to_broadcast([P, T, NE]))
                b_ = picked(3, ob.unsqueeze(1).to_broadcast([P, T, NE]))
                gt, j_, it, sl = (res[:, 8 * k:8 * k + 2 * T] for k in (4, 5, 6, 7))
                step(TS(gt, p_, float(P), None, ALU.is_ge))
                step(STT(out=j_, in0=p_, scalar=float(2 * P), in1=gt, op0=ALU.is_ge, op1=ALU.add))
                step(STT(out=j_, in0=p_, scalar=float(3 * P), in1=j_, op0=ALU.is_ge, op1=ALU.add))
                step(STT(out=it, in0=j_, scalar=float(NE - 1), in1=b_, op0=ALU.add, op1=ALU.add))
                step(TT(it, it, e_, ALU.subtract))
                step(TT(it, it, gt, ALU.mult))
                step(TT(it, it, e_, ALU.add))
                step(STT(out=sl, in0=j_, scalar=-float(P), in1=p_, op0=ALU.mult, op1=ALU.add))
                for k in range(2):
                    cols = slice(k * T, (k + 1) * T)
                    STT(out=rowY[:, k, 0:T], in0=it[:, cols], scalar=float(P), in1=sl[:, cols], op0=ALU.mult, op1=ALU.add)
                    ins = STT(out=rowL[:, k, 0:T], in0=sl[:, cols], scalar=float(LISTW), in1=it[:, cols], op0=ALU.mult, op1=ALU.add)
                ins.then_inc(s["mask"], 1)
                V = incl[:, NE - 1:NE]
                fl = r()
                npair = fl[:, 0:1]
                step(TS(npair, V, 1.0, float(NE // 2), ALU.is_ge, ALU.add))
                for x in (3.0, 5.0, 7.0):
                    step(STT(out=npair, in0=V, scalar=x, in1=npair, op0=ALU.is_ge, op1=ALU.add))
                i3 = big[:, 0:8 * NE].rearrange("p (e f) -> p e f", f=NE)
                step(TT(i3, incl.unsqueeze(1).to_broadcast([P, 8, NE]), rcst[:, R_IT:R_IT + 8].unsqueeze(2).to_broadcast([P, 8, NE]), ALU.is_le))
                step(RED(fl[:, 8:16], i3, AX, ALU.add))
                TS(ni[:, NE:ITEMS], fl[:, 8:16], float(NE - 1), None, ALU.min)
                dve.tensor_copy(ni[:, 0:NE], rcst[:, R_EID:R_EID + NE])
                TS(ni[:, ITEMS + 2:ITEMS + 3], npair, 4.0, -2.0, ALU.mult, ALU.add)
                TS(ni[:, ITEMS + 4:ITEMS + 5], npair, -1.0, None, ALU.add)
                TS(ni[:, ITEMS + 3:ITEMS + 4], npair, 4.0, None, ALU.mult)
                TS(ni[:, ITEMS + 1:ITEMS + 2], npair, 16.0, 16.0, ALU.mult, ALU.add)
                dve.tensor_copy(ni[:, ITEMS:ITEMS + 1], npair).then_inc(s["ni"], 1)
                modulation(range(4, MODB))
                if l + 1 < DEPTH:
                    for g in range(MODG - 1):
                        dve.wait_ge(mod_out[g], 32)

                UP, X1, Y1 = ps[3], ps[5], ps[0]
                for name in ("h", "yD"):
                    dve.sem_inc(m[name], 1)
                dve.wait_ge(s["ni"], 1)
                rounds = dve.value_load(ni[0:1, ITEMS + 4:ITEMS + 5], min_val=NE // 2 - 1, max_val=ITEMS // 2 - 1)

                def tokens(u, q, c):
                    dve.wait_ge(m["xt"], 4 * q + (2 * c + 2))
                    dve.tensor_copy(xgT[:, u, 4:8, :], X1[:].rearrange("p (c n) -> p c n", c=4)).then_inc(m["xtD"], 1)

                def hidden(u, q, c):
                    dve.wait_ge(m["gu"], 4 * q + (2 * c + 2))
                    dve.wait_ge(m["sig"], 2 * q + (c + 2))
                    TT(hh[:, u, :], UP[:], sg[:, u, :], ALU.mult).then_inc(m["h"], 1)

                def output(u, q, c):
                    dve.wait_ge(m["y"], 4 * q + (2 * c + 2))
                    dve.wait_ge(m_yo[l][u], 16 * q + (8 * (c - u) + 16))
                    dve.tensor_copy(yg[:, u, HALF:D], Y1[:]).then_inc(m["yD"], 1)

                tokens(0, 0, 0)
                if l + 1 < DEPTH:
                    dve.wait_ge(mod_out[MODG - 1], 32)
                hidden(0, 0, 0)
                tokens(1, 0, 1)
                with dve.Fori(0, rounds) as q:
                    hidden(1, q, 1)
                    output(0, q, 0)
                    tokens(0, q, 2)
                    hidden(0, q, 2)
                    output(1, q, 1)
                    tokens(1, q, 3)
                hidden(1, rounds, 1)
                output(0, rounds, 0)
                output(1, rounds, 1)

                if l + 1 < DEPTH:
                    scales(l + 1, "rows1", 16 * 5, 2)
                dve.wait_ge(s["rows4"], 16 * (T // LT))
                for t in range(T):
                    y1, y2 = chosen[t]
                    dve.wait_ge(m_yk[t], 32 * (l + 1))
                    step(TS(y2, y2, wk[:, 1, t:t + 1], None, ALU.mult))
                    step(STT(out=y2, in0=y1, scalar=wk[:, 0, t:t + 1], in1=y2, op0=ALU.mult, op1=ALU.add))
                    step(TT(y2, y2, rowC[:, t // LT, :], ALU.mult))
                    TT(x_sb[:, t, :], x_sb[:, t, :], y2, ALU.add).then_inc(s["xf"], 1)
                    if l + 1 < DEPTH:
                        mean(l + 1, t, t)
                        normalise(l + 1, t, t, free1, "h")

        @block.gpsimd
        def _(pool):
            def spread(dst, row, done):
                pool.dma_start(dst, row.to_broadcast([dst.shape[0], row.shape[-1]])).then_inc(done, 16)

            def mod_row(l, which, r):
                return mod_d[r:r + 1, l * D_MOD + which * D:l * D_MOD + (which + 1) * D]

            def parameters(l):
                par = S[l]["par"]
                pool.dma_start(crows[0:CW, :], a["conv_w"][l]).then_inc(par, 16)
                for k, name in enumerate(("conv_b", "conv_ln_g", "conv_ln_b")):
                    pool.dma_start(crows[CW + k:CW + k + 1, :], a[name][l:l + 1, :]).then_inc(par, 16)
                spread(qkg[:, 0:QK], a["mla_q_gain"][l:l + 1, :], par)
                spread(qkg[:, QK:2 * QK], a["mla_k_gain"][l:l + 1, :], par)
                spread(qkg[:, 2 * QK:2 * QK + GD], a["gqa_q_gain"][l:l + 1, :], par)
                spread(qkg[:, 2 * QK + GD:2 * QK + 2 * GD], a["gqa_k_gain"][l:l + 1, :], par)
                if l == 0:
                    spread(qkg[:, 2 * QK + 2 * GD:], a["router_bias"].rearrange("(o e) -> o e", o=1), par)
                pool.dma_start(colg[:, 0:2].rearrange("p (k o) -> p k o", o=1), a["mla_q_norm"][l].rearrange("(k p o) -> p k o", p=P, o=1),
                               allow_slow_non_contiguous=True).then_inc(par, 16)
                pool.dma_start(colg[:, 2:3], a["mla_kv_norm"][l].rearrange("(p o) -> p o", o=1)).then_inc(par, 16)

            def rows1(l):
                spread(normg[:], a["norm1_g"][l:l + 1, :], S[l]["rows1"])
                pool.wait_ge(mod_out[0], 16 * (l + 1))
                for r in range(2):
                    spread(rowA[:, r, :], mod_row(l, 1, r), S[l]["rows1"])
                    spread(rowB[:, r, :], mod_row(l, 0, r), S[l]["rows1"])

            spread(mods[0:2, :], a["b_mod"][0:1, :], s_bias)
            parameters(0)
            pool.dma_start(rw[:], a["router_w"].rearrange("(k p) e -> p k e", p=P)).then_inc(s_zero, 16)
            pool.memset(ypad[:], 0.0).then_inc(S[0]["pad"], 1)
            rows1(0)
            pool.wait_ge(s_zset, 1)
            for l in range(DEPTH):
                pool.dma_start(list_d[l].rearrange("(p w) o -> p (w o)", p=P), zero[:]).then_inc(s_zero, 16)

            for l in range(DEPTH):
                T, s, m = QT[l], S[l], M[l]
                n = T // LT
                bank.wait_read(pool, (l, "conv_cols"))
                bank.wait_read(pool, (l, "yT", 3))
                acc = cv[:, 3, 0:n, :]
                pool.tensor_scalar(acc, ypad[:, 3, 0:n, 0:SEQ], convc[:, 3, 0:1], convc[:, 3, CW:CW + 1], ALU.mult, ALU.add).then_inc(pool_step, 1)
                for w in range(1, CW):
                    pool.wait_ge(s["term"], w)
                    pool.wait_ge(pool_step, l * (CW - 1) + w)
                    ins = pool.tensor_tensor(acc, acc, term(w)[:, 0:n, :], ALU.add)
                    ins.then_inc(pool_step if w < CW - 1 else s["cvd"], 1)
                if l == 0:
                    pool.wait_ge(s["nrm"], 3)
                    pool.memset(normg[:], 0.0).then_inc(s_zset, 1)
                    pool.wait_ge(s_zset, 2)
                    for k in range(DEPTH):
                        rows = y_d[k][NE * P:ITEMS * P, :].rearrange("(i p) d -> p i d", p=P)
                        pool.dma_start(rows, normg[:].unsqueeze(1).to_broadcast([P, ITEMS - NE, D])).then_inc(s_zero, 16)
                bank.wait_full(pool, (l, "mla", "oT", 3))
                for g in range(1, MODG):
                    pool.wait_ge(mod_out[g], 16 * (l + 1))
                for r in range(n):
                    spread(rowG[:, r, :], mod_row(l, 2, r), s["rows2"])
                pool.wait_ge(s_zero, ZEROED)
                spread(normg[:], a["norm2_g"][l:l + 1, :], s["rows3"])
                pool.dma_start(rcst[:], consts[:, C_ALL:C_ALL + R_ALL]).then_inc(s["rcst"], 16)
                bank.wait_full(pool, (l, "mT", T - 1, 1))
                for r in range(n):
                    spread(rowB[:, r, :], mod_row(l, 3, r), s["rows3"])
                    spread(rowA[:, r, :], mod_row(l, 4, r), s["rows3"])
                pool.wait_ge(s["xm"], 2 * T)
                if l + 1 < DEPTH:
                    spread(mods[0:2, :], a["b_mod"][l + 1:l + 2, :], s_bias)
                    parameters(l + 1)
                pool.wait_ge(s["mask"], 2)
                pool.wait_ge(s_zero, ZEROED)
                for t in range(T):
                    for k in range(2):
                        pool.indirect_dma_start(list_d[l], bass.IndirectOffsetOnAxis(ap=rowL[:, k, t:t + 1], axis=0), toku[:, t:t + 1], None).then_inc(s["scat"], 16)
                pool.wait_ge(s["scat"], 32 * T)
                pool.wait_ge(s["h2o"], 16 * T)
                pool.dma_start(lst[:], list_d[l].rearrange("(p w) o -> p (w o)", p=P)).then_inc(s["scat"], 16)
                pool.wait_ge(s["scat"], 32 * T + 16)
                pool.wait_ge(s["ni"], 1)
                pairs = pool.value_load(ni[0:1, ITEMS:ITEMS + 1], min_val=NE // 2, max_val=ITEMS // 2)
                stored = pool.value_load(ni[0:1, ITEMS + 1:ITEMS + 2], min_val=16, max_val=16 * ITEMS)

                def gather(u):
                    pool.indirect_dma_start(xg[:, u, :], None, h2_d[l], bass.IndirectOffsetOnAxis(ap=cur[:, u, 0:1], axis=0)).then_inc(m_xg[l][u], 16)

                def take(u, col):
                    return pool.tensor_copy(cur[:, u, 0:1], lst[:, col])
                for u in range(2):
                    take(u, slice(u, u + 1)).then_inc(m["cur"], 1)
                pool.wait_ge(m["cur"], 2)
                gather(0)
                if l + 1 < DEPTH:
                    for g in range(MODG):
                        pool.wait_ge(mod_out[g], 32)
                gather(1)
                if l + 1 < DEPTH:
                    pool.wait_ge(s["h2"], T)
                    rows1(l + 1)
                with pool.Fori(4, 2 * pairs + 2, 2) as i:
                    pool.wait_ge(m["xt"], 2 * i - 4)
                    for u in range(2):
                        take(u, bass.ds(i - 2 + u, 1)).then_inc(m["cur"], 1)
                    for u in range(2):
                        pool.wait_ge(s["ni"], 1)
                        pool.wait_ge(m["cur"], i)
                        gather(u)
                before_last = pool.value_load(ni[0:1, ITEMS + 2:ITEMS + 3], min_val=1, max_val=4 * ITEMS)
                pool.wait_ge(s["ni"], 1)
                pool.wait_ge(m["gu"], before_last)
                for r in range(n):
                    spread(rowC[:, r, :], mod_row(l, 5, r), s["rows4"])
                if l + 1 < DEPTH:
                    pool.memset(ypad[:], 0.0).then_inc(S[l + 1]["pad"], 1)
                all_xt = pool.value_load(ni[0:1, ITEMS + 3:ITEMS + 4], min_val=1, max_val=4 * ITEMS)
                for v in range(2):
                    pool.wait_ge(s["ni"], 1)
                    pool.wait_ge(m_yo[l][v], stored)
                pool.wait_ge(s["ni"], 1)
                pool.wait_ge(m["xt"], all_xt)
                for t in range(T):
                    for k in range(2):
                        pool.indirect_dma_start(chosen[t][k], None, y_d[l], bass.IndirectOffsetOnAxis(ap=rowY[:, k, t:t + 1], axis=0)).then_inc(m_yk[t], 16)


_INS = ["x", "c", "ctx", "c_ctx", "w_mod", "b_mod", "norm1_g", "norm2_g", "w_in", "mla_q_norm", "mla_kv_norm", "mla_w_uq",
        "mla_w_ukv", "mla_q_gain", "mla_k_gain", "mla_w_o", "conv_w", "conv_b", "conv_ln_g", "conv_ln_b", "conv_w_o",
        "gqa_q_gain", "gqa_k_gain", "gqa_w_o", "w_out", "router_w", "router_bias", "moe_w_gate", "moe_w_up", "moe_w_down"]


def constants():
    import numpy as np

    f = np.float32
    t = np.zeros((P, C_ALL + R_ALL), f)
    t[:, C_ID:C_ID + P] = np.eye(P, dtype=f)
    n = np.arange(SEQ)
    for tile in range(LT):
        rows = slice(tile * P, (tile + 1) * P)
        at = C_ROPE + tile * ROPEW
        for dim in (ROPE // 2, GD // 2):
            inv = (f(10000.0) ** (-np.arange(0, dim, 2, dtype=f) / f(dim))).astype(f)
            ang = np.concatenate([pos[:, None].astype(f) * inv[None, :] for pos in (n // GRID_W, n % GRID_W)], axis=1)
            for fn in (np.cos, np.sin):
                t[:, at:at + dim] = fn(ang[rows]).astype(f)
                at += dim
    r = t[:, C_ALL:]
    r[:, R_TRI:R_TRI + P] = np.triu(np.ones((P, P), f), 1)
    r[:, R_ONES:R_ONES + P] = 1
    r[:, R_TOK:R_TOK + NT] = np.arange(P)[:, None] + P * np.arange(NT)[None, :]
    r[:, R_EID:R_EID + NE] = np.arange(NE)
    r[:, R_REV:R_REV + NE] = NE - np.arange(NE)
    r[:, R_GREV:R_GREV + NG] = NG - np.arange(NG)
    r[:, R_IT:R_IT + 8] = np.arange(8)
    r[:, R_LT:R_LT + NE * NE] = np.tril(np.ones((NE, NE), f), -1).reshape(-1)
    return t


def kernel(**inputs):
    import numpy as _np
    import concourse.bacc as _bacc
    from concourse.bass_utils import run_bass_kernel_spmd as _run

    nc = _bacc.Bacc("TRN2", target_bir_lowering=False, num_devices=1)
    arrays, aps = {}, {}
    for name in _INS:
        v = _np.ascontiguousarray(inputs[name])
        arrays[f"in_{name}"] = v
        aps[name] = nc.dram_tensor(f"in_{name}", v.shape, mybir.dt.from_np(v.dtype), kind="ExternalInput").ap()
    v = constants()
    arrays["constants"] = v
    consts = nc.dram_tensor("constants", v.shape, F32, kind="ExternalInput").ap()
    out = nc.dram_tensor("out", (1, SEQ, D), F32, kind="ExternalOutput").ap()
    backbone(nc, aps, consts, out)
    return _run(nc, [arrays], core_ids=[0]).results[0]["out"]
```
